# Optimizing a Trainium2 kernel written in Bass

```python
import math
import jax
import jax.numpy as jnp
from jax import lax
import numpy as np

D_MODEL = 1024
BATCH = 1
SEQ = 256
DEPTH = 1

SSM_EXPAND = 2
D_INNER = SSM_EXPAND * D_MODEL
SSM_HEAD_DIM = 64
SSM_HEADS = D_INNER // SSM_HEAD_DIM
SSM_GROUPS = 4
SSM_STATE = 128
SSM_CONV = 4
SSM_CHUNK = 128
D_CONV = D_INNER + 2 * SSM_GROUPS * SSM_STATE

ATT_HEADS = 16
ATT_HEAD_DIM = 64
ATT_KV_GROUPS = 4
ATT_HPG = ATT_HEADS // ATT_KV_GROUPS
ATT_WIDTH = ATT_HEADS * ATT_HEAD_DIM
KV_WIDTH = ATT_KV_GROUPS * ATT_HEAD_DIM
CMP_BLOCK = 32
CMP_STRIDE = 16
CMP_HIDDEN = 256
SLC_BLOCK = 64
SLC_TOPK = 16
WINDOW = 512
ATT_Q_BLOCK = 64
FORCE_BONUS = 1000.0

N_BRANCH = 2
EPS = 1e-6
NEG_INF = -1e30

IN_SIZES = (D_INNER, D_CONV, SSM_HEADS, ATT_WIDTH, 6 * KV_WIDTH, 3 * ATT_HEADS, ATT_WIDTH, N_BRANCH * D_MODEL)
IN_SPLITS = tuple(int(v) for v in np.cumsum(IN_SIZES)[:-1])
IN_TOTAL = int(sum(IN_SIZES))

kernel_name = 'hybrid_ssd_nsa_griffin_block'

def _rmsnorm(x, g):
    xf = x.astype(jnp.float32)
    y = xf * lax.rsqrt(jnp.mean(xf * xf, axis=-1, keepdims=True) + EPS)
    return (y * g.astype(jnp.float32)).astype(x.dtype)

def _alibi_slopes():
    m = 2.0 ** (-8.0 * np.arange(1, ATT_HEADS + 1) / ATT_HEADS)
    return jnp.asarray(m.reshape(ATT_KV_GROUPS, ATT_HPG), dtype=jnp.float32)

def _causal_dwconv(u, w, b):
    k = w.shape[0]
    y = lax.conv_general_dilated(u, w[:, None, :].astype(u.dtype), window_strides=(1,),
                                 padding=[(k - 1, 0)], dimension_numbers=('NWC', 'WIO', 'NWC'),
                                 feature_group_count=u.shape[-1])
    return y + b

def _ssd_chunked(xh, dt, a, bm, cm):
    bsz, s, h, p = xh.shape
    nc = s // SSM_CHUNK
    cl = SSM_CHUNK
    hg = SSM_HEADS // SSM_GROUPS
    xdt = (xh * dt[..., None]).reshape(bsz, nc, cl, SSM_GROUPS, hg, p)
    adt = (dt * a).reshape(bsz, nc, cl, SSM_GROUPS, hg)
    b_ = bm.reshape(bsz, nc, cl, SSM_GROUPS, SSM_STATE)
    c_ = cm.reshape(bsz, nc, cl, SSM_GROUPS, SSM_STATE)
    a_cs = jnp.cumsum(adt, axis=2)
    causal = jnp.tril(jnp.ones((cl, cl), dtype=bool))[None, None, :, :, None, None]
    seg = a_cs[:, :, :, None] - a_cs[:, :, None, :]
    decay = jnp.exp(jnp.where(causal, seg, -jnp.inf))
    cb = jnp.einsum('bclgn,bcsgn->bclsg', c_, b_)
    y_diag = jnp.einsum('bclsg,bclsgh,bcsghp->bclghp', cb, decay, xdt)
    decay_states = jnp.exp(a_cs[:, :, -1:] - a_cs)
    states = jnp.einsum('bclgn,bclgh,bclghp->bcghpn', b_, decay_states, xdt)
    chunk_decay = jnp.exp(a_cs[:, :, -1])

    def step(carry, inp):
        st, dec = inp
        return carry * dec[..., None, None] + st, carry

    h0 = jnp.zeros(states.shape[:1] + states.shape[2:], states.dtype)
    _, prev = lax.scan(step, h0, (jnp.moveaxis(states, 1, 0), jnp.moveaxis(chunk_decay, 1, 0)))
    prev = jnp.moveaxis(prev, 0, 1)
    y_off = jnp.einsum('bclgn,bcghpn,bclgh->bclghp', c_, prev, jnp.exp(a_cs))
    return (y_diag + y_off).reshape(bsz, s, h, p)

def _mamba2_branch(z, xbc, dt_raw, conv_w, conv_b, dt_bias, a_log, d_skip, g_norm):
    bsz, s, _ = z.shape
    xbc = jax.nn.silu(_causal_dwconv(xbc, conv_w, conv_b))
    xs, bm, cm = jnp.split(xbc, [D_INNER, D_INNER + SSM_GROUPS * SSM_STATE], axis=-1)
    xh = xs.reshape(bsz, s, SSM_HEADS, SSM_HEAD_DIM)
    bm = bm.reshape(bsz, s, SSM_GROUPS, SSM_STATE)
    cm = cm.reshape(bsz, s, SSM_GROUPS, SSM_STATE)
    dt = jax.nn.softplus((dt_raw + dt_bias).astype(jnp.float32))
    a = -jnp.exp(a_log.astype(jnp.float32))
    y = _ssd_chunked(xh, dt, a, bm, cm) + xh * d_skip[:, None]
    y = y.reshape(bsz, s, D_INNER) * jax.nn.silu(z)
    gsz = D_INNER // SSM_GROUPS
    y = _rmsnorm(y.reshape(bsz, s, SSM_GROUPS, gsz), g_norm.reshape(SSM_GROUPS, gsz))
    return y.reshape(bsz, s, D_INNER)

def _compress(kv, pos, w1, w2):
    bsz, s, g, d = kv.shape
    n_cmp = (s - CMP_BLOCK) // CMP_STRIDE + 1
    idx = np.arange(n_cmp)[:, None] * CMP_STRIDE + np.arange(CMP_BLOCK)[None, :]
    blk = kv[:, idx] + pos[None, None, :, None, :]
    blk = jnp.transpose(blk, (0, 1, 3, 2, 4)).reshape(bsz, n_cmp, g, CMP_BLOCK * d)
    return jax.nn.silu(blk @ w1) @ w2

def _cmp_to_slc(n_cmp, n_slc):
    cs = np.arange(n_cmp) * CMP_STRIDE
    ss = np.arange(n_slc) * SLC_BLOCK
    lo = np.maximum(cs[:, None], ss[None, :])
    hi = np.minimum(cs[:, None] + CMP_BLOCK, ss[None, :] + SLC_BLOCK)
    return jnp.asarray(np.clip(hi - lo, 0, None) / CMP_BLOCK, dtype=jnp.float32)

def _nsa_branch(q, kv, gate_raw, z_att, cmp_pos_k, cmp_w1_k, cmp_w2_k, cmp_pos_v, cmp_w1_v, cmp_w2_v):
    bsz, s, _ = q.shape
    ng, hg, d = ATT_KV_GROUPS, ATT_HPG, ATT_HEAD_DIM
    scale = ATT_HEAD_DIM ** -0.5
    slopes = _alibi_slopes()
    q = q.reshape(bsz, s, ng, hg, d)
    kc, vc, ks, vs, kw, vw = [t.reshape(bsz, s, ng, d) for t in jnp.split(kv, 6, axis=-1)]
    t_pos = jnp.arange(s)

    kc = _compress(kc, cmp_pos_k, cmp_w1_k, cmp_w2_k)
    vc = _compress(vc, cmp_pos_v, cmp_w1_v, cmp_w2_v)
    n_cmp = kc.shape[1]
    cmp_end = jnp.arange(n_cmp) * CMP_STRIDE + (CMP_BLOCK - 1)
    dist_c = (t_pos[:, None] - cmp_end[None, :]).astype(jnp.float32)
    valid_c = dist_c >= 0
    sc = jnp.einsum('btghd,bjgd->bghtj', q, kc).astype(jnp.float32) * scale - slopes[None, :, :, None, None] * dist_c
    sc = jnp.where(valid_c, sc, NEG_INF)
    p_c = jnp.where(valid_c, jax.nn.softmax(sc, axis=-1), 0.0)
    o_cmp = jnp.einsum('bghtj,bjgd->btghd', p_c, vc)

    n_slc = s // SLC_BLOCK
    n_sel = min(SLC_TOPK, n_slc)
    imp = jnp.einsum('bghtj,jk->bgtk', p_c, _cmp_to_slc(n_cmp, n_slc))
    blk_t = (t_pos // SLC_BLOCK)[:, None]
    kk = jnp.arange(n_slc)[None, :]
    forced = (kk == 0) | (kk == blk_t) | (kk == blk_t - 1)
    score = jnp.where(forced, imp + FORCE_BONUS, jnp.where(kk <= blk_t, imp, -1.0))
    _, sel = lax.top_k(score, n_sel)

    ks_b = ks.reshape(bsz, n_slc, SLC_BLOCK, ng, d).transpose(0, 3, 1, 2, 4)
    vs_b = vs.reshape(bsz, n_slc, SLC_BLOCK, ng, d).transpose(0, 3, 1, 2, 4)
    kw_p = jnp.pad(kw, ((0, 0), (WINDOW, 0), (0, 0), (0, 0)))
    vw_p = jnp.pad(vw, ((0, 0), (WINDOW, 0), (0, 0), (0, 0)))
    b_ix = jnp.arange(bsz)[:, None, None, None]
    g_ix = jnp.arange(ng)[None, :, None, None]
    span = ATT_Q_BLOCK + WINDOW

    def q_block(i):
        t0 = i * ATT_Q_BLOCK
        tq = t0 + jnp.arange(ATT_Q_BLOCK)
        qb = lax.dynamic_slice_in_dim(q, t0, ATT_Q_BLOCK, axis=1)
        ib = lax.dynamic_slice_in_dim(sel, t0, ATT_Q_BLOCK, axis=2)
        kg = ks_b[b_ix, g_ix, ib]
        vg = vs_b[b_ix, g_ix, ib]
        spos = ib[..., None] * SLC_BLOCK + jnp.arange(SLC_BLOCK)
        ds = (tq[None, None, :, None, None] - spos).astype(jnp.float32)[:, :, None]
        ss = jnp.einsum('btghd,bgtnld->bghtnl', qb, kg).astype(jnp.float32) * scale - slopes[None, :, :, None, None, None] * ds
        ss = jnp.where(ds >= 0, ss, NEG_INF)
        ps = jax.nn.softmax(ss.reshape(ss.shape[:4] + (-1,)), axis=-1).reshape(ss.shape)
        o_s = jnp.einsum('bghtnl,bgtnld->btghd', ps, vg)
        kwb = lax.dynamic_slice_in_dim(kw_p, t0, span, axis=1)
        vwb = lax.dynamic_slice_in_dim(vw_p, t0, span, axis=1)
        kpos = t0 - WINDOW + jnp.arange(span)
        dw = (tq[:, None] - kpos[None, :]).astype(jnp.float32)
        ok = (dw >= 0) & (dw < WINDOW) & (kpos[None, :] >= 0)
        sw = jnp.einsum('btghd,bsgd->bghts', qb, kwb).astype(jnp.float32) * scale - slopes[None, :, :, None, None] * dw
        sw = jnp.where(ok, sw, NEG_INF)
        o_w = jnp.einsum('bghts,bsgd->btghd', jax.nn.softmax(sw, axis=-1), vwb)
        return o_s, o_w

    o_slc, o_win = lax.map(q_block, jnp.arange(s // ATT_Q_BLOCK))
    o_slc = jnp.moveaxis(o_slc, 0, 1).reshape(bsz, s, ng, hg, d)
    o_win = jnp.moveaxis(o_win, 0, 1).reshape(bsz, s, ng, hg, d)
    g = jax.nn.sigmoid(gate_raw.astype(jnp.float32)).reshape(bsz, s, ng, hg, 3, 1)
    o = g[..., 0, :] * o_cmp + g[..., 1, :] * o_slc + g[..., 2, :] * o_win
    return o.reshape(bsz, s, ATT_WIDTH) * jax.nn.silu(z_att)

def _layer(x, c, w_ada, b_ada, g_pre, g_post, w_in, conv_w, conv_b, dt_bias, a_log, d_skip,
           g_ssm_norm, w_ssm_out, cmp_pos_k, cmp_w1_k, cmp_w2_k, cmp_pos_v, cmp_w1_v, cmp_w2_v,
           w_nsa_out, w_out):
    bsz, s, dm = x.shape
    shift, scale, gate = jnp.split(c @ w_ada + b_ada, 3, axis=-1)
    h = _rmsnorm(x, g_pre) * (1.0 + scale[:, None, :]) + shift[:, None, :]
    z_ssm, xbc, dt_raw, q, kv, nsa_gate, z_att, merge_gate = jnp.split(h @ w_in, IN_SPLITS, axis=-1)
    y_ssm = _mamba2_branch(z_ssm, xbc, dt_raw, conv_w, conv_b, dt_bias, a_log, d_skip, g_ssm_norm) @ w_ssm_out
    y_nsa = _nsa_branch(q, kv, nsa_gate, z_att, cmp_pos_k, cmp_w1_k, cmp_w2_k,
                        cmp_pos_v, cmp_w1_v, cmp_w2_v) @ w_nsa_out
    mg = jax.nn.sigmoid(merge_gate.reshape(bsz, s, N_BRANCH, dm))
    merged = mg[:, :, 0] * y_ssm + mg[:, :, 1] * y_nsa
    out = merged @ w_out
    return x + gate[:, None, :] * _rmsnorm(out, g_post)

def setup_inputs(seed: int = 0) -> dict:
    key = jax.random.key(seed)
    ks = jax.random.split(key, 24)
    nl = DEPTH

    def nrm(k, shape, sd):
        return jax.random.normal(k, shape, jnp.float32) * sd

    dt0 = jnp.exp(jax.random.uniform(ks[9], (nl, SSM_HEADS), jnp.float32, math.log(1e-3), math.log(1e-1)))
    fan_cmp = CMP_BLOCK * ATT_HEAD_DIM
    return {
        'x': nrm(ks[0], (BATCH, SEQ, D_MODEL), 1.0),
        'c': nrm(ks[1], (BATCH, D_MODEL), 1.0),
        'w_ada': nrm(ks[2], (nl, D_MODEL, 3 * D_MODEL), 0.5 * D_MODEL ** -0.5),
        'b_ada': nrm(ks[3], (nl, 3 * D_MODEL), 0.01),
        'g_pre': 1.0 + nrm(ks[4], (nl, D_MODEL), 0.05),
        'g_post': 1.0 + nrm(ks[5], (nl, D_MODEL), 0.05),
        'w_in': nrm(ks[6], (nl, D_MODEL, IN_TOTAL), D_MODEL ** -0.5),
        'conv_w': nrm(ks[7], (nl, SSM_CONV, D_CONV), SSM_CONV ** -0.5),
        'conv_b': nrm(ks[8], (nl, D_CONV), 0.01),
        'dt_bias': dt0 + jnp.log(-jnp.expm1(-dt0)),
        'a_log': jnp.log(jax.random.uniform(ks[10], (nl, SSM_HEADS), jnp.float32, 1.0, 16.0)),
        'd_skip': 1.0 + nrm(ks[11], (nl, SSM_HEADS), 0.1),
        'g_ssm_norm': 1.0 + nrm(ks[12], (nl, D_INNER), 0.05),
        'w_ssm_out': nrm(ks[13], (nl, D_INNER, D_MODEL), D_INNER ** -0.5),
        'cmp_pos_k': nrm(ks[14], (nl, CMP_BLOCK, ATT_HEAD_DIM), 0.1),
        'cmp_w1_k': nrm(ks[15], (nl, fan_cmp, CMP_HIDDEN), fan_cmp ** -0.5),
        'cmp_w2_k': nrm(ks[16], (nl, CMP_HIDDEN, ATT_HEAD_DIM), CMP_HIDDEN ** -0.5),
        'cmp_pos_v': nrm(ks[17], (nl, CMP_BLOCK, ATT_HEAD_DIM), 0.1),
        'cmp_w1_v': nrm(ks[18], (nl, fan_cmp, CMP_HIDDEN), fan_cmp ** -0.5),
        'cmp_w2_v': nrm(ks[19], (nl, CMP_HIDDEN, ATT_HEAD_DIM), CMP_HIDDEN ** -0.5),
        'w_nsa_out': nrm(ks[20], (nl, ATT_WIDTH, D_MODEL), ATT_WIDTH ** -0.5),
        'w_out': nrm(ks[21], (nl, D_MODEL, D_MODEL), D_MODEL ** -0.5),
    }

def reference(x, c, w_ada, b_ada, g_pre, g_post, w_in, conv_w, conv_b, dt_bias, a_log, d_skip,
              g_ssm_norm, w_ssm_out, cmp_pos_k, cmp_w1_k, cmp_w2_k, cmp_pos_v, cmp_w1_v, cmp_w2_v,
              w_nsa_out, w_out):
    for layer in range(DEPTH):
        x = _layer(x, c, w_ada[layer], b_ada[layer], g_pre[layer], g_post[layer], w_in[layer],
                   conv_w[layer], conv_b[layer], dt_bias[layer], a_log[layer], d_skip[layer],
                   g_ssm_norm[layer], w_ssm_out[layer], cmp_pos_k[layer], cmp_w1_k[layer],
                   cmp_w2_k[layer], cmp_pos_v[layer], cmp_w1_v[layer], cmp_w2_v[layer],
                   w_nsa_out[layer], w_out[layer])
    return x


_drawn_inputs = setup_inputs


def setup_inputs(seed=0):
    import zlib

    import numpy as np

    out = dict(_drawn_inputs(seed))
    spreads = {}
    factors = {'b_ada': 4.38,
     'conv_b': 8.0,
     'd_skip': 2.923,
     'g_ssm_norm': 2.891,
     'cmp_pos_k': 64.0,
     'cmp_pos_v': 6.157,
     'cmp_w1_k': 5.192,
     'cmp_w2_k': 5.071}
    for name, (base, spread) in spreads.items():
        noise = np.random.default_rng([zlib.crc32(name.encode()), seed]).standard_normal(out[name].shape)
        drawn = base * np.exp(spread * noise) if base else spread * noise
        out[name] = jnp.asarray(drawn.astype(out[name].dtype))
    for name, factor in factors.items():
        out[name] = (out[name] * factor).astype(out[name].dtype)
    return out
```

```python
import math

import numpy as np

import concourse.bass as bass
from concourse import mybir

P = 128
SEQ, D_MODEL = 256, 1024
D_INNER, SSM_HEADS, HEAD_DIM, SSM_GROUPS, STATE, CHUNK = 2048, 32, 64, 4, 128, 128
ATT_HEADS, KV_GROUPS, HPG = 16, 4, 4
CMP_BLOCK, CMP_STRIDE, CMP_HIDDEN = 32, 16, 256
N_CMP = (SEQ - CMP_BLOCK) // CMP_STRIDE + 1
EPS = 1e-6
NEG = -1e30
KT = D_MODEL // P
NCHUNK = SEQ // CHUNK
HPC = SSM_HEADS // SSM_GROUPS
QUADS = SSM_HEADS // 4
TPG = 4

D_CONV = D_INNER + 2 * SSM_GROUPS * STATE
OFF_Z = 0
OFF_X = D_INNER
OFF_B = OFF_X + D_INNER
OFF_C = OFF_B + SSM_GROUPS * STATE
OFF_DT = OFF_X + D_CONV
OFF_Q = OFF_DT + SSM_HEADS
OFF_KV = OFF_Q + ATT_HEADS * HEAD_DIM
OFF_GATE = OFF_KV + 6 * KV_GROUPS * HEAD_DIM
OFF_ZA = OFF_GATE + 3 * ATT_HEADS
OFF_MG = OFF_ZA + ATT_HEADS * HEAD_DIM
GATE_ROW = 64


def weight_units():
    units = [("dtg", 0, 0)]
    units += [("b", j, 0) for j in range(4)] + [("c", j, 0) for j in range(4)]
    for g in range(SSM_GROUPS):
        units += [("x", TPG * g + j, 0) for j in range(TPG)] + [("z", TPG * g + j, 0) for j in range(TPG)]
    units += [("kc", j, 0) for j in range(2)] + [("vc", j, 0) for j in range(2)]
    units += [("w1k", 0, part) for part in range(4)] + [("w1v", 0, part) for part in range(4)]
    for kind in ("ks", "vs", "kw", "vw"):
        units += [(kind, j, 0) for j in range(2)]
    units += [("q", j, 0) for j in range(8)] + [("za", j, 0) for j in range(8)]
    units += [("mg", j, 0) for j in range(16)]
    units += [("ssm", j, part) for j in range(8) for part in range(2)]
    units += [("nsa", j, 0) for j in range(8)] + [("out", j, 0) for j in range(8)]
    return units


UNITS = weight_units()
NATIVE = ("w1k", "w1v")
CONV = ("b", "c", "x")
LAST_PART = {"w1k": 3, "w1v": 3, "ssm": 1}


def schedule():
    after = {}

    def put(u, *steps):
        after.setdefault(u, []).extend(steps)

    put(2, ("dtT", 0))
    put(6, ("acs", 0))
    put(8, ("bt", 0))
    put(11, ("cb", 0))
    put(12, ("cb", 1))
    for g in range(SSM_GROUPS):
        b = 17 + 8 * g
        put(b, ("xt", (g, 0)))
        put(b + 1, ("xt", (g, 1)), ("seg", 2 * g))
        put(b + 2, ("ea", 2 * g))
        put(b + 3, ("st", g))
        put(b + 4, ("y", 4 * g), ("y", 4 * g + 1), ("seg", 2 * g + 1))
        put(b + 5, ("ea", 2 * g + 1))
        put(b + 7, ("y", 4 * g + 2), ("y", 4 * g + 3))
        put(b + 8, ("ysq", g))
        put(b + 9, ("ssq", g))
        for j in range(TPG):
            put(b + 11 + j, ("yn", TPG * g + j))
            put(b + 12 + j, ("ynlo", TPG * g + j))
    put(43, ("blk", 0))
    put(45, ("blk", 1))
    put(51, ("hidT", 0))
    put(54, ("hidT", 1))
    put(55, ("kcp", 0))
    put(56, ("vcp", 0))
    put(58, ("vt", 0))
    put(62, ("vt", 1))
    put(70, ("cs", 0))
    put(72, ("cs2", 0))
    put(75, ("ct", 0))
    put(76, ("ct", 1))
    for h in range(ATT_HEADS):
        put(73 + 2 * h, ("sc", h))
        put(74 + 2 * h, ("ps", h))
        put(76 + 2 * h, ("pt", h))
    for p in range(ATT_HEADS // 2):
        put(79 + 4 * p, ("pv", p))
        put(max(95, 80 + 4 * p) + (0 if p < 7 else 0), ("osp", p))
    put(112, ("adag", 0))
    put(113, ("adagT", 0))
    for m in range(8):
        put(118 + m if m < 7 else 124, ("osq", m) if m < 7 else ("none", 0))
    steps = []
    for u in range(len(UNITS)):
        steps.append(("gemm", u))
        steps += after.get(u, [])
    steps.append(("flush", 0))
    steps.append(("osq", 7))
    return [s for s in steps if s[0] != "none"]


STEPS = schedule()
SPLIT_IDX, NATIVE_IDX, TILE_IDX = {}, {}, {}
for _u, (_kind, _j, _part) in enumerate(UNITS):
    if _kind in NATIVE:
        NATIVE_IDX[_u] = len(NATIVE_IDX)
    else:
        SPLIT_IDX[_u] = len(SPLIT_IDX)
    if _part == 0:
        TILE_IDX[(_kind, _j)] = len(TILE_IDX)
SPLIT_UNITS = sorted(SPLIT_IDX)
T_STEPS = ("dtT", "acs", "bt", "cb", "xt", "ea", "st", "ssq", "hidT", "kcp", "vcp", "vt", "cs", "ct", "pt", "adag", "adagT")
T_IDX, S_IDX, Y_IDX, HAPPENS = {}, {}, {}, {}
_seen = {}
for _s in STEPS:
    HAPPENS[_s] = _seen.get(_s[0], 0)
    _seen[_s[0]] = HAPPENS[_s] + 1
    if _s[0] in T_STEPS:
        for _n in range(2 if _s[0] == "pt" else 1):
            T_IDX[_s + (_n,)] = len(T_IDX)
    if _s[0] in ("seg", "sc"):
        S_IDX[_s] = len(S_IDX)
    if _s[0] in ("y", "pv"):
        Y_IDX[_s] = len(Y_IDX)

TH_IDX, _pending = {}, None
for _kind, _j, _part in UNITS:
    if _part != LAST_PART.get(_kind, 0):
        continue
    if _kind in CONV or _pending:
        if _pending:
            TH_IDX[_pending] = len(TH_IDX)
            _pending = None
    if _kind in CONV:
        _pending = (_kind, _j)
    elif _kind in ("z", "za", "w1k", "w1v"):
        TH_IDX[(_kind, _j)] = len(TH_IDX)

PAR = {}


def _par(name, n):
    PAR[name] = (PAR["end"][1] if "end" in PAR else 0, (PAR["end"][1] if "end" in PAR else 0) + n)
    PAR["end"] = (0, PAR[name][1])


for _name, _n in (("c", KT), ("conv_w", 96), ("conv_b", 24), ("dt_bias", 1), ("g_pre", 8), ("g_post", 8), ("b_ada", 24),
                  ("g_ssm", 16), ("d_skip", 16), ("a_log", SSM_HEADS), ("pos_k", 32), ("pos_v", 32),
                  ("w2k", 256), ("w2v", 128)):
    _par(_name, _n)
CST = {}


def _cst(name, n):
    CST[name] = (CST["end"][1] if "end" in CST else 0, (CST["end"][1] if "end" in CST else 0) + n)
    CST["end"] = (0, CST[name][1])


for _name, _n in (("ident", P), ("tri", P), ("tri_strict", P), ("ones", P), ("mask_sl", P), ("mask_qk", P),
                  ("onehot", SSM_HEADS), ("bias_c", 2 * 16 * 16), ("valid_c", 2 * 16)):
    _cst(_name, _n)

RAW_SLOTS, HI_SLOTS, LO_SLOTS = 6, 3, 3


def build(nc, xT, par_in, cst_in, alibi_q, alibi_k, w_ada1, w_ada2, wpack, out):
    f32, f32r, bf16 = mybir.dt.float32, mybir.dt.float32r, mybir.dt.bfloat16
    ALU, ACT, AX = mybir.AluOpType, mybir.ActivationFunctionType, mybir.AxisListType

    cursor = [(nc.sbuf_base + 63) // 64 * 64]

    def place(name, shape, dt, at=None):
        size = (int(np.prod(shape[1:])) * (2 if dt == bf16 else 4) + 63) // 64 * 64
        off = cursor[0] if at is None else at
        if at is None:
            cursor[0] += size
        return nc.alloc_sbuf_tensor_at(name, shape, dt, offset=off)

    h_at = cursor[0]
    HH = place("h_hi", [P, KT, SEQ], f32r)
    HL = place("h_lo", [P, KT, SEQ], f32r)
    RAW = place("w_raw", [P, RAW_SLOTS, 1024], f32)
    WH = place("w_hi", [P, HI_SLOTS, 1024], f32r)
    WL = place("w_lo", [P, LO_SLOTS, 1024], f32r)
    PR = place("params", [P, PAR["end"][1]], f32)
    CS = place("consts", [P, CST["end"][1]], f32)
    IDB = place("ident_bf16", [P, P], bf16)
    MSL = place("mask_sl_bf16", [P, P], bf16)
    MQK = place("mask_qk_bf16", [P, P], bf16)
    CW = place("conv_half", [P, 120], f32)
    MOD = place("mod", [P, 16], f32)
    AB = place("ada_scale", [P, 16], f32)
    GATE = place("att_gate", [P, 2, ATT_HEADS, 3], f32)
    SM = place("softmax_small", [P, 2, 4, 4], f32)
    ys_at = cursor[0]
    F0 = place("dt_gate_T", [P, SEQ], f32)
    DTT = place("dt_gate_tok", [P, 2, P], f32)
    DT = place("dt", [P, 2, SSM_HEADS], f32)
    DTW = place("dt_work", [P, 6, 2, SSM_HEADS], f32)
    ADT4 = place("adt4", [P, 2, 4, SSM_HEADS], f32)
    HI4 = place("acs_hi", [P, 2, P], f32r)
    TP = place("acs_rows", [P, 2, P], f32)
    ST = place("acs_cols", [P, 2, P], f32r)
    ONZ = place("ones_then_zeros", [P, P], f32r)
    DS = place("decay_to_end", [P, SSM_HEADS], f32)
    AEX = place("exp_a_log", [P, SSM_HEADS], f32)
    HI4X = place("released", [1, 1], f32)
    assert cursor[0] - ys_at >= 8192, cursor[0] - ys_at
    YS = place("y_ssm_out", [P, 8, SEQ], f32, at=ys_at)
    z_at = cursor[0]
    Z = place("z_gate_then_y", [P, 16, SEQ], f32)
    YNH = place("ynorm_hi", [P, 16, SEQ], f32r, at=z_at)
    YNL = place("ynorm_lo", [P, 16, SEQ], f32r)
    ZA = place("z_att_then_o", [P, 8, SEQ], f32)
    q_at = cursor[0]
    QS = place("q_hi_lo", [P, ATT_HEADS, SEQ], f32r)
    KH = place("k_hi", [P, KV_GROUPS, 2, SEQ], f32r)
    KL = place("k_lo", [P, KV_GROUPS, 2, SEQ], f32r)
    V = place("v", [P, 2, 2, KV_GROUPS, HEAD_DIM], f32)
    over_at = cursor[0]
    kb = 1024
    assert over_at + 48 * kb <= 229344, over_at
    ADA = place("w_ada_shift_scale", [P, KT, 2048], f32, at=z_at)
    XT = place("x_T", [P, KT, SEQ], f32, at=over_at)
    SQX = place("x_sq", [P, KT, SEQ], f32, at=over_at + 8 * kb)
    RX = place("rstd_x", [P, 2, SEQ], f32, at=over_at + 16 * kb)
    ROWS = place("ada_rows", [P, 512], f32, at=over_at + 18 * kb)
    XG = place("x_conv_T", [P, 2, TPG, SEQ], f32, at=q_at)
    BTT = place("b_T", [P, 4, SEQ], f32, at=q_at + 8 * kb)
    CTT = place("c_T", [P, 4, SEQ], f32, at=q_at + 12 * kb)
    BTOK = place("b_tok", [P, 4, STATE], f32, at=q_at + 16 * kb)
    XDT = place("x_dt", [P, 2, HPC, HEAD_DIM], f32, at=q_at + 18 * kb)
    XDS = place("x_dt_decay", [P, HPC, HEAD_DIM], f32, at=q_at + 22 * kb)
    STA = place("state", [P, HPC * HEAD_DIM], f32, at=q_at + 24 * kb)
    CB = place("cb_T", [P, 4, 2, P], f32, at=q_at + 26 * kb)
    MV = place("seg_moving", [P, 2, 4, P], f32r, at=over_at)
    EX = place("decay", [P, 2, 4, P], f32, at=over_at + 4 * kb)
    MM = place("cb_decay", [P, 2, 4, P], f32, at=over_at + 8 * kb)
    EA = place("exp_acs", [P, 4, P], f32, at=over_at + 12 * kb)
    CE = place("c_exp_acs", [P, 4, P], f32, at=over_at + 14 * kb)
    SQ = place("y_sq", [P, 4, SEQ], f32, at=over_at + 16 * kb)
    YT = place("y_tmp", [P, 2, SEQ], f32, at=over_at + 20 * kb)
    RN = place("rstd_y", [P, 2, SEQ], f32, at=over_at + 22 * kb)
    BLK = place("cmp_blocks", [P, 2, 16, KV_GROUPS * N_CMP], f32, at=over_at + 24 * kb)
    KVC = place("kv_cmp_T", [P, 4, SEQ], f32, at=over_at + 32 * kb)
    HID = place("cmp_hidden", [P, 2, CMP_HIDDEN], f32, at=over_at + 36 * kb)
    HVR = place("hid_v_T", [P, 2, KV_GROUPS, 4, 32], f32, at=over_at + 38 * kb)
    ACC = place("conv_acc", [P, 2, SEQ], f32, at=over_at + 42 * kb)
    TH = place("tanh_tmp", [P, 2, SEQ], f32, at=over_at + 44 * kb)
    HIDK = place("hid_k_T", [P, 2, 60], f32, at=over_at + 46 * kb)
    KCH = place("k_cmp_hi", [P, KV_GROUPS, 16], f32r, at=over_at + 46 * kb + 512)
    KCL = place("k_cmp_lo", [P, KV_GROUPS, 16], f32r, at=over_at + 46 * kb + 768)
    MT = place("merge_tanh", [P, 16, SEQ], f32, at=over_at)
    CSW = place("cmp_scores", [P, 2, ATT_HEADS, 16], f32, at=over_at)
    CSM = place("cmp_small", [P, 3, 2, ATT_HEADS], f32, at=over_at + 2 * kb)
    E = place("probs", [P, 2, 2, 384], f32, at=over_at + 16 * kb)
    PT = place("probs_T", [P, 2, 2, 384], f32, at=over_at + 22 * kb)
    PC = place("cmp_probs", [P, 2, ATT_HEADS, 32], f32, at=over_at + 22 * kb)
    PCT = place("cmp_probs_T", [P, KV_GROUPS, SEQ], f32, at=over_at + 28 * kb)
    VC = place("v_cmp", [P, KV_GROUPS, 2, P], f32, at=over_at + 32 * kb)
    ALQ = place("alibi_q", [P, ATT_HEADS * SEQ], bf16, at=over_at + 36 * kb)
    ALK = place("alibi_k", [P, 2, SEQ], bf16, at=over_at + 47 * kb)
    VT = place("v_T", [P, 2, SEQ], f32, at=over_at + 26 * kb)
    OH = place("o_hi", [P, 8, SEQ], f32r, at=h_at)
    OL = place("o_lo", [P, 8, SEQ], f32r, at=h_at + 8 * kb)
    MH = place("merged_hi", [P, 8, SEQ], f32r, at=z_at)
    ML = place("merged_lo", [P, 8, SEQ], f32r, at=z_at + 8 * kb)
    MTMP = place("merge_tmp", [P, 2, 2, SEQ], f32, at=over_at + 16 * kb)
    SQO = place("out_sq", [P, 2, SEQ], f32, at=over_at + 20 * kb)
    ROWS2 = place("ada_gate_rows", [P, 256], f32, at=over_at + 22 * kb)
    GG = place("gate_times_g", [P, 2, 8], f32, at=over_at + 23 * kb)
    RF = place("rstd_out", [P, 2, SEQ], f32, at=over_at + 24 * kb)
    XR = place("x_residual", [P, 8, SEQ], f32, at=over_at + 28 * kb)
    ADA2 = place("w_ada_gate", [P, KT, 1024], f32, at=q_at)
    OUT = place("out_T", [P, 8, SEQ], f32, at=q_at - 8 * kb)

    def par(name, lo=0, hi=None):
        a, b = PAR[name]
        return PR[:, a + lo:(b if hi is None else a + hi)]

    def cst(name, lo=0, hi=None):
        a, b = CST[name]
        return CS[:, a + lo:(b if hi is None else a + hi)]

    GB = [nc.alloc_psum_tensor(f"gemm{i}", [P, 512], f32) for i in range(2)]
    SB = [nc.alloc_psum_tensor(f"score{i}", [P, 512], f32) for i in range(2)]
    TB = [nc.alloc_psum_tensor(f"small{i}", [P, 512], f32) for i in range(2)]
    YB = [nc.alloc_psum_tensor(f"y{i}", [P, 512], f32) for i in range(2)]
    sems = {}

    def sem(name):
        if name not in sems:
            sems[name] = nc.alloc_semaphore(name)
        return sems[name]

    ada_in = [sem(f"ada_in{k}") for k in range(KT)]
    w_in = [sem(f"w_in{r}") for r in range(RAW_SLOTS)]
    par_in_s, cst_in_s, x_in, al_in, al2_in, ada2_in, xr_in, out_done = map(
        sem, ("params_in", "consts_in", "x_in", "alibi_in", "alibi2_in", "ada2_in", "xr_in", "out_done"))
    hi_ready, lo_ready, unit_mm, native_mm = map(sem, ("hi_ready", "lo_ready", "unit_mm", "native_mm"))
    g_free, t_full, t_free, s_full, s_free, y_full, y_free = (
        [sem(f"{n}{b}") for b in range(2)]
        for n in ("g_free", "t_full", "t_free", "s_full", "s_free", "y_full", "y_free"))
    consts_made, zeros = sem("consts_made"), sem("zeros")
    cw_ready, sqx_done, ssx_full, varx_done, rx_done, ada_full, rows_done, modT_full, h_f32, h_hi, h_ready = map(
        sem, ("cw_ready", "sqx", "ssx_full", "varx", "rx", "ada_full", "rows", "modT_full", "h_f32", "h_hi_done", "h_ready"))
    abs_done, dt_exp, dt_u, dt_ln, a_exp, gate_tanh, adt_done, hi4_done, cols_ready = map(
        sem, ("abs", "dt_exp", "dt_u", "dt_ln", "a_exp", "gate_tanh", "adt", "hi4", "cols_ready"))
    conv_acc, th_full, gated = map(sem, ("conv_acc_s", "th_full", "gated"))
    xds_done, mv_done, ce_done, ypre_done, ysq_done, rn_done, ynf_done, ynh_done, yn_done = map(
        sem, ("xds", "mv", "ce", "ypre", "ysq", "rn", "ynf", "ynh", "yn"))
    mm_done = [sem("mm0"), sem("mm1")]
    blk_done = [sem("blk0"), sem("blk1")]
    kch_done, kh_done, qh_done, cs_sub, cs_exp, pc_done, max_done, p_done, oh_done, o_split = map(
        sem, ("kch", "kh", "qh", "cs_sub", "cs_exp", "pc", "max", "p", "oh", "o_split"))
    mf_done, mh_done, ml_done, osq_full, varf_done, rf_done, fin_done = map(
        sem, ("mf", "mh", "ml", "osq_full", "varf", "rf", "fin"))
    dve_seq, act_seq, pool_seq = sem("dve_seq"), sem("act_seq"), sem("pool_seq")

    def conv_index(kind, j):
        return {"b": j, "c": 4 + j, "x": 8 + j}[kind]

    def conv_src(kind, j):
        return {"x": j, "b": 16 + j, "c": 20 + j}[kind]

    def conv_dst(kind, j):
        return {"b": BTT, "c": CTT}[kind][:, j, :] if kind != "x" else XG[:, (j // TPG) % 2, j % TPG, :]

    def wait_small_full(eng, key):
        eng.wait_ge(t_full[T_IDX[key] % 2], T_IDX[key] // 2 + 1)

    def wait_small_out(eng, key):
        eng.wait_ge(t_free[T_IDX[key] % 2], T_IDX[key] // 2 + 1)

    def wait_tile_full(eng, tile):
        u = UNITS.index(tile + (LAST_PART.get(tile[0], 0),))
        if u in SPLIT_IDX:
            eng.wait_ge(unit_mm, SPLIT_IDX[u] + 1)
        else:
            eng.wait_ge(native_mm, NATIVE_IDX[u] + 1)

    out_count = {}
    for tile in TILE_IDX:
        if tile[0] not in ("z", "za", "w1k", "w1v"):
            b = TILE_IDX[tile] % 2
            out_count[tile] = sum(1 for other in out_count if TILE_IDX[other] % 2 == b) + 1

    def wait_tile_out(eng, tile):
        if tile in out_count:
            eng.wait_ge(g_free[TILE_IDX[tile] % 2], out_count[tile])
        else:
            eng.wait_ge(gated, TH_IDX[tile] + 1)

    def wait_y_full(eng, key):
        eng.wait_ge(y_full[Y_IDX[key] % 2], Y_IDX[key] // 2 + 1)

    def wait_y_out(eng, key):
        eng.wait_ge(y_free[Y_IDX[key] % 2], Y_IDX[key] // 2 + 1)

    def finished_tile(u):
        kind, j, part = UNITS[u]
        return (kind, j) if part == LAST_PART.get(kind, 0) else None

    def compress_blocks(eng, e, b):
        wait_tile_out(eng, ("vc" if b else "kc", 0))
        wait_tile_out(eng, ("vc" if b else "kc", 1))
        pos = PAR["pos_v" if b else "pos_k"][0]
        for g in range(KV_GROUPS):
            rows = slice(64 * (g % 2), 64 * (g % 2) + 64)
            kv = KVC[rows, 2 * b + g // 2, :].rearrange("p (j r n) -> p n r j", r=8, n=2)
            for n in range(2):
                for half in range(2):
                    r = PR[rows, pos + 16 * half + n:pos + 16 * half + 16:2].unsqueeze(2).to_broadcast([64, 8, N_CMP])
                    e.tensor_tensor(BLK[64 * n:64 * n + 64, b, 8 * half:8 * half + 8, N_CMP * g:N_CMP * (g + 1)],
                                    kv[:, n, :, half:half + N_CMP], r, ALU.add).then_inc(blk_done[b], 1)
                    if b:
                        eng.wait_ge(blk_done[b], 4 * g + 2 * n + half + 1)

    with nc.Block() as block:

        @block.sync
        def _(sp):
            sp.dma_start(PR[:], par_in).then_inc(par_in_s, 16)
            sp.dma_start(XT[:], xT).then_inc(x_in, 16)
            for k in range(KT):
                sp.dma_start(ADA[:, k, :], w_ada1[:, k, :]).then_inc(ada_in[k], 16)
                if k == 1:
                    sp.dma_start(CS[:], cst_in).then_inc(cst_in_s, 16)
            for u in range(len(UNITS)):
                if u >= RAW_SLOTS:
                    v = u - RAW_SLOTS
                    if v in SPLIT_IDX:
                        sp.wait_ge(lo_ready, SPLIT_IDX[v] + 1)
                    else:
                        sp.wait_ge(native_mm, NATIVE_IDX[v] + 1)
                sp.dma_start(RAW[:, u % RAW_SLOTS, :], wpack[u]).then_inc(w_in[u % RAW_SLOTS], 16)
                if u == 66:
                    wait_small_full(sp, ("vcp", 0, 0))
                    sp.wait_ge(gated, TH_IDX[("x", 15)] + 1)
                    sp.dma_start(ALQ[:].bitcast(mybir.dt.uint16), alibi_q).then_inc(al_in, 16)
                    sp.dma_start(ALK[:].bitcast(mybir.dt.uint16), alibi_k).then_inc(al2_in, 16)
                if u == 110:
                    sp.wait_ge(s_full[1], len(S_IDX))
                    wait_y_out(sp, ("pv", 7))
                    sp.dma_start(ADA2[:], w_ada2).then_inc(ada2_in, 16)
                    sp.dma_start(XR[:], xT).then_inc(xr_in, 16)
            for m in range(8):
                sp.wait_ge(fin_done, m + 1)
                sp.dma_start(out[:, m, :], OUT[:, m, :]).then_inc(out_done, 16)
            sp.wait_ge(out_done, 8 * 16)

        @block.tensor
        def _(pe):
            ident = cst("ident")
            pe.wait_ge(cst_in_s, 16)
            pe.wait_ge(sqx_done, 1)
            for k in range(KT):
                last = nc.tensor.matmul(YB[0][:, 0:SEQ], cst("ones"), SQX[:, k, :], start=(k == 0), stop=(k == KT - 1))
            last.then_inc(ssx_full, 1)
            pe.wait_ge(par_in_s, 16)
            for k in range(KT):
                pe.wait_ge(ada_in[k], 16)
                for j in range(4):
                    last = nc.tensor.matmul(SB[0][32 * j:32 * j + 1, :], par("c", k, k + 1), ADA[:, k, 512 * j:512 * j + 512],
                                            start=(k == 0), stop=(k == KT - 1))
            last.then_inc(ada_full, 1)
            pe.wait_ge(rows_done, 4)
            pe.wait_ge(zeros, 1)
            for m in range(4):
                last = nc.tensor.transpose(SB[1][:, P * m:P * m + P], ROWS[:, P * m:P * m + P], ident)
            last.then_inc(modT_full, 1)
            pe.wait_ge(h_ready, KT)

            def begin_small(key):
                n = T_IDX[key]
                if n >= 2:
                    pe.wait_ge(t_free[n % 2], n // 2)
                return TB[n % 2]

            def end_small(ins, key):
                ins.then_inc(t_full[T_IDX[key] % 2], 1)

            tiles = list(TILE_IDX)

            def weight_unit(u):
                kind, j, part = UNITS[u]
                tile = TILE_IDX[(kind, j)]
                bank = GB[tile % 2]
                if part == 0 and tile >= 2:
                    wait_tile_out(pe, tiles[tile - 2])
                raw = RAW[:, u % RAW_SLOTS, :]
                if kind in NATIVE:
                    b = 0 if kind == "w1k" else 1
                    pe.wait_ge(w_in[u % RAW_SLOTS], 16 * (u // RAW_SLOTS + 1))
                    if part == 0:
                        pe.wait_ge(blk_done[b], 16)
                    for r in range(4):
                        last = nc.tensor.matmul(bank[0:60, 0:CMP_HIDDEN], BLK[:, b, 4 * part + r, :],
                                                raw[:, CMP_HIDDEN * r:CMP_HIDDEN * (r + 1)],
                                                start=(part == 0 and r == 0), stop=(part == 3 and r == 3))
                    last.then_inc(native_mm, 1)
                    return
                n = SPLIT_IDX[u]
                if kind == "ssm":
                    hi, lo, k0, parts = YNH, YNL, 8 * part, 2
                    if j == 0:
                        pe.wait_ge(yn_done, 8 * (part + 1))
                elif kind == "nsa":
                    hi, lo, k0, parts = OH, OL, 0, 1
                    if j == 0:
                        pe.wait_ge(o_split, 8)
                elif kind == "out":
                    hi, lo, k0, parts = MH, ML, 0, 1
                else:
                    hi, lo, k0, parts = HH, HL, 0, 1
                pe.wait_ge(hi_ready, n + 1)
                pe.wait_ge(lo_ready, n + 1)
                for k in range(KT):
                    if kind == "out" and j == 0:
                        pe.wait_ge(ml_done, k + 1)
                    w_hi = WH[:, n % HI_SLOTS, P * k:P * k + P]
                    w_lo = WL[:, n % LO_SLOTS, P * k:P * k + P]
                    first, end = (k == 0 and part == 0), (k == KT - 1 and part == parts - 1)
                    nc.tensor.matmul(bank[:, 0:SEQ], w_hi, hi[:, k0 + k, :], start=first, stop=False)
                    nc.tensor.matmul(bank[:, 0:SEQ], w_hi, lo[:, k0 + k, :], start=False, stop=False)
                    last = nc.tensor.matmul(bank[:, 0:SEQ], w_lo, hi[:, k0 + k, :], start=False, stop=end)
                last.then_inc(unit_mm, 1)

            for step in STEPS:
                what, i = step
                if what == "gemm":
                    weight_unit(i)
                elif what == "dtT":
                    key = step + (0,)
                    bank = begin_small(key)
                    wait_tile_out(pe, ("dtg", 0))
                    for c in range(2):
                        last = nc.tensor.transpose(bank[:, P * c:P * c + P], F0[:, P * c:P * c + P], ident)
                    end_small(last, key)
                elif what == "acs":
                    key = step + (0,)
                    bank = begin_small(key)
                    pe.wait_ge(adt_done, 1)
                    for c in range(2):
                        nc.tensor.matmul(bank[:, P * c:P * c + P], ADT4[:, c, :, :].rearrange("p r h -> p (r h)"),
                                         cst("tri"), start=True, stop=True)
                    last = nc.tensor.matmul(bank[:, 256:256 + SSM_HEADS], cst("tri_strict"), ADT4[:, 0, 0, :],
                                            start=True, stop=True)
                    end_small(last, key)
                elif what == "bt":
                    key = step + (0,)
                    bank = begin_small(key)
                    pe.wait_ge(gated, TH_IDX[("b", 3)] + 1)
                    for g in range(4):
                        last = nc.tensor.transpose(bank[:, P * g:P * g + P], BTT[:, g, 0:CHUNK], ident)
                    end_small(last, key)
                elif what == "cb":
                    key = step + (0,)
                    bank = begin_small(key)
                    pe.wait_ge(gated, TH_IDX[("c", 3)] + 1)
                    for gg in range(2):
                        for c in range(2):
                            o = P * (2 * gg + c)
                            last = nc.tensor.matmul(bank[:, o:o + P], BTT[:, 2 * i + gg, CHUNK * c:CHUNK * (c + 1)],
                                                    CTT[:, 2 * i + gg, CHUNK * c:CHUNK * (c + 1)], start=True, stop=True)
                    end_small(last, key)
                elif what == "xt":
                    g, c = i
                    key = step + (0,)
                    bank = begin_small(key)
                    pe.wait_ge(gated, TH_IDX[("x", TPG * g + 3)] + 1)
                    for t in range(TPG):
                        last = nc.tensor.transpose(bank[:, P * t:P * t + P], XG[:, g % 2, t, CHUNK * c:CHUNK * (c + 1)], ident)
                    end_small(last, key)
                elif what == "st":
                    key = step + (0,)
                    bank = begin_small(key)
                    pe.wait_ge(xds_done, i + 1)
                    wait_small_out(pe, ("bt", 0, 0))
                    last = nc.tensor.matmul(bank[:, :], BTOK[:, i, :], XDS[:, :, :].rearrange("p h d -> p (h d)"),
                                            start=True, stop=True)
                    end_small(last, key)
                elif what == "seg":
                    n = S_IDX[step]
                    for c in range(2):
                        if n >= 1:
                            pe.wait_ge(s_free[c], n)
                        if i == 0 and c == 0:
                            pe.wait_ge(cols_ready, 4)
                            pe.wait_ge(consts_made, 7)
                        pe.wait_ge(mv_done, 2 * i + c + 1)
                        mv = MV[:, c, :, :].rearrange("p j l -> p (j l)")
                        nc.tensor.matmul(SB[c][:, :], ST[:, c, :], mv, start=True, stop=False)
                        last = nc.tensor.matmul(SB[c][:, :], IDB[:], MSL[:].unsqueeze(1).to_broadcast([P, 4, P]),
                                                start=False, stop=True)
                        last.then_inc(s_full[c], 1)
                elif what == "ea":
                    key = step + (0,)
                    bank = begin_small(key)
                    last = nc.tensor.matmul(bank[:, :], ONZ[:], MV[:, 1, :, :].rearrange("p j l -> p (j l)"),
                                            start=True, stop=True)
                    end_small(last, key)
                elif what == "y":
                    n = Y_IDX[step]
                    bank = YB[n % 2]
                    if n >= 2:
                        pe.wait_ge(y_free[n % 2], n // 2)
                    g, quad = i // TPG, i // 2
                    pe.wait_ge(mm_done[0], quad + 1)
                    pe.wait_ge(mm_done[1], quad + 1)
                    pe.wait_ge(ce_done, quad + 1)
                    wait_small_out(pe, ("st", g, 0))
                    wait_small_out(pe, ("xt", (g, 1), 0))
                    for c in range(2):
                        for k in range(2):
                            h = 2 * (i % TPG) + k
                            q4 = 2 * (i % 2) + k
                            o = bank[64 * k:64 * k + 64, CHUNK * c:CHUNK * (c + 1)]
                            last = nc.tensor.matmul(o, XDT[:, c, h, :], MM[:, c, q4, :], start=True, stop=(c == 0))
                    for k in range(2):
                        h, q4 = 2 * (i % TPG) + k, 2 * (i % 2) + k
                        last = nc.tensor.matmul(bank[64 * k:64 * k + 64, CHUNK:SEQ], STA[:, HEAD_DIM * h:HEAD_DIM * (h + 1)],
                                                CE[:, q4, :], start=False, stop=True)
                    last.then_inc(y_full[n % 2], 1)
                elif what == "ssq":
                    key = step + (0,)
                    bank = begin_small(key)
                    pe.wait_ge(ysq_done, i + 1)
                    for t in range(TPG):
                        last = nc.tensor.matmul(bank[:, 0:SEQ], cst("ones"), SQ[:, t, :], start=(t == 0), stop=(t == TPG - 1))
                    end_small(last, key)
                elif what == "hidT":
                    key = step + (0,)
                    bank = begin_small(key)
                    pe.wait_ge(gated, TH_IDX[("w1v" if i else "w1k", 0)] + 1)
                    for k in range(2):
                        last = nc.tensor.transpose(bank[:, 60 * k:60 * k + 60], HID[0:60, i, P * k:P * k + P],
                                                   CS[0:60, CST["ident"][0]:CST["ident"][0] + 60])
                    end_small(last, key)
                elif what == "kcp":
                    key = step + (0,)
                    bank = begin_small(key)
                    wait_small_out(pe, ("hidT", 0, 0))
                    for k in range(2):
                        last = nc.tensor.matmul(bank[:, 0:60], par("w2k", P * k, P * k + P), HIDK[:, k, :],
                                                start=(k == 0), stop=(k == 1))
                    end_small(last, key)
                elif what == "vcp":
                    key = step + (0,)
                    bank = begin_small(key)
                    wait_small_out(pe, ("hidT", 1, 0))
                    for g in range(KV_GROUPS):
                        for k in range(2):
                            last = nc.tensor.matmul(bank[:, 64 * g:64 * g + 64], HVR[:, k, g, :, :].rearrange("p a b -> p (a b)"),
                                                    par("w2v", 64 * k, 64 * k + 64), start=(k == 0), stop=(k == 1))
                    end_small(last, key)
                elif what == "vt":
                    key = step + (0,)
                    bank = begin_small(key)
                    wait_tile_out(pe, ("vw" if i else "vs", 0))
                    wait_tile_out(pe, ("vw" if i else "vs", 1))
                    for kt in range(2):
                        for j in range(2):
                            o = P * (2 * kt + j)
                            last = nc.tensor.transpose(bank[:, o:o + P], VT[:, j, P * kt:P * kt + P], ident)
                    end_small(last, key)
                elif what == "cs":
                    key = step + (0,)
                    bank = begin_small(key)
                    for j in (6, 7):
                        wait_tile_out(pe, ("q", j))
                    wait_small_out(pe, ("kcp", 0, 0))
                    for qt in range(2):
                        for h in range(ATT_HEADS):
                            o = 256 * qt + 16 * h
                            q = QS[:, h, P * qt:P * qt + P]
                            nc.tensor.matmul(bank[:, o:o + 16], q, KCH[:, h // HPG, :], start=True, stop=False)
                            last = nc.tensor.matmul(bank[:, o:o + 16], q, KCL[:, h // HPG, :], start=False, stop=True)
                    end_small(last, key)
                elif what == "ct":
                    key = step + (0,)
                    bank = begin_small(key)
                    pe.wait_ge(pc_done, 1)
                    for gg in range(2):
                        for qt in range(2):
                            src = PC[:, qt, 4 * (2 * i + gg):4 * (2 * i + gg) + 4, :].rearrange("p h j -> p (h j)")
                            o = 256 * gg + P * qt
                            last = nc.tensor.transpose(bank[:, o:o + P], src, ident)
                    end_small(last, key)
                elif what == "sc":
                    n = S_IDX[step]
                    if i == 0:
                        pe.wait_ge(al_in, 16)
                        pe.wait_ge(al2_in, 16)
                    for qt in range(2):
                        pe.wait_ge(s_free[qt], n)
                        nk = P * (qt + 1)
                        o = SB[qt][:, 0:2 * nk].rearrange("p (b k) -> p b k", b=2)
                        q = QS[:, i, P * qt:P * qt + P]
                        nc.tensor.matmul(o, q, KH[:, i // HPG, :, 0:nk], start=True, stop=False)
                        nc.tensor.matmul(o, q, KL[:, i // HPG, :, 0:nk], start=False, stop=False)
                        nc.tensor.matmul(o, ALQ[:, SEQ * i + P * qt:SEQ * i + P * qt + P], ALK[:, :, 0:nk], start=False, stop=False)
                        last = nc.tensor.matmul(o[:, :, P * qt:nk], IDB[:], MQK[:].unsqueeze(1).to_broadcast([P, 2, P]),
                                                start=False, stop=True)
                        last.then_inc(s_full[qt], 1)
                elif what == "pt":
                    pe.wait_ge(p_done, 4 * (i + 1))
                    e = E[:, i % 2, :, :]
                    key = step + (0,)
                    bank = begin_small(key)
                    for b in range(2):
                        nc.tensor.transpose(bank[:, 256 * b:256 * b + P], e[:, b, 0:P], ident)
                        last = nc.tensor.transpose(bank[:, 256 * b + P:256 * b + 256], e[:, b, P:2 * P], ident)
                    end_small(last, key)
                    key = step + (1,)
                    bank = begin_small(key)
                    for b in range(2):
                        last = nc.tensor.transpose(bank[:, P * b:P * b + P], e[:, b, 2 * P:3 * P], ident)
                    end_small(last, key)
                elif what == "pv":
                    n = Y_IDX[step]
                    bank = YB[n % 2]
                    if n >= 2:
                        pe.wait_ge(y_free[n % 2], n // 2)
                    g = (2 * i) // HPG
                    if i == 0:
                        wait_small_out(pe, ("ct", 0, 0))
                        wait_small_out(pe, ("ct", 1, 0))
                    for h in (2 * i, 2 * i + 1):
                        wait_small_out(pe, ("pt", h, 0))
                        wait_small_out(pe, ("pt", h, 1))
                    nc.tensor.matmul(bank[:, 0:SEQ], VC[:, g, i % 2, :], PCT[:, g, :], start=True, stop=False,
                                     skip_group_check=True)
                    for b in range(2):
                        for kt in range(2):
                            for k in range(2):
                                src = PT[:, k, b, 0:SEQ] if kt == 0 else PT[:, k, b, SEQ:SEQ + P]
                                last = nc.tensor.matmul(bank[64 * k:64 * k + 64, P * kt:SEQ], V[:, b, kt, g, :], src,
                                                        start=False, stop=(b == 1 and kt == 1), skip_group_check=True)
                    last.then_inc(y_full[n % 2], 1)
                elif what == "adag":
                    key = step + (0,)
                    bank = begin_small(key)
                    pe.wait_ge(ada2_in, 16)
                    for k in range(KT):
                        for j in range(4):
                            last = nc.tensor.matmul(bank[32 * j:32 * j + 1, 0:256], par("c", k, k + 1),
                                                    ADA2[:, k, 256 * j:256 * j + 256], start=(k == 0), stop=(k == KT - 1))
                    end_small(last, key)
                elif what == "adagT":
                    key = step + (0,)
                    bank = begin_small(key)
                    wait_small_out(pe, ("adag", 0, 0))
                    pe.wait_ge(zeros, 7)
                    for m in range(2):
                        last = nc.tensor.transpose(bank[:, P * m:P * m + P], ROWS2[:, P * m:P * m + P], ident)
                    end_small(last, key)
                elif what == "osq":
                    if i == 0:
                        wait_y_out(pe, ("pv", 6))
                        wait_y_out(pe, ("pv", 7))
                    wait_tile_out(pe, ("out", i))
                    last = nc.tensor.matmul(YB[0][:, 0:SEQ], cst("ones"), SQO[:, i % 2, :], start=(i == 0), stop=(i == 7))
                    last.then_inc(osq_full, 1)

        @block.scalar
        def _(act):
            def split_hi(n):
                u = SPLIT_UNITS[n]
                act.wait_ge(w_in[u % RAW_SLOTS], 16 * (u // RAW_SLOTS + 1))
                if n >= HI_SLOTS:
                    act.wait_ge(unit_mm, n - HI_SLOTS + 1)
                nc.scalar.copy(WH[:, n % HI_SLOTS, :], RAW[:, u % RAW_SLOTS, :]).then_inc(hi_ready, 1)

            def tanh_half(tile, src, rows=P):
                k = TH_IDX[tile]
                if k >= 2:
                    act.wait_ge(gated, k - 1)
                nc.scalar.activation(TH[0:rows, k % 2, :], src, ACT.Tanh, scale=0.5).then_inc(th_full, 1)

            pending = []

            def read_out(tile):
                if tile is None:
                    return
                kind, j = tile
                t = TILE_IDX[tile]
                bank = GB[t % 2][:, 0:SEQ]
                if kind != "out" or True:
                    wait_tile_full(act, tile)
                if kind in CONV:
                    ci, col = conv_index(kind, j), conv_src(kind, j)
                    if ci >= 2:
                        act.wait_ge(gated, max(v for k, v in TH_IDX.items() if k[0] in CONV and conv_index(*k) == ci - 2) + 1)
                    nc.scalar.activation(ACC[:, ci % 2, :], bank, ACT.Identity, bias=CW[:, 96 + col:97 + col],
                                         scale=CW[:, 4 * col + 3:4 * col + 4]).then_inc(conv_acc, 1)
                if pending:
                    prev = pending.pop()
                    ci = conv_index(*prev)
                    wait_tile_out(act, prev)
                    k = TH_IDX[prev]
                    if k >= 2:
                        act.wait_ge(gated, k - 1)
                    nc.scalar.activation(TH[:, k % 2, :], ACC[:, ci % 2, :], ACT.Tanh).then_inc(th_full, 1)
                if kind in CONV:
                    pending.append(tile)
                elif kind == "dtg":
                    nc.scalar.activation(F0[:], bank, ACT.Identity, bias=par("dt_bias")).then_inc(g_free[t % 2], 1)
                elif kind in ("z", "za"):
                    tanh_half(tile, bank)
                elif kind in NATIVE:
                    tanh_half(tile, GB[t % 2][0:60, 0:CMP_HIDDEN], 60)
                elif kind in ("kc", "vc"):
                    nc.scalar.copy(KVC[:, j + 2 * (kind == "vc"), :], bank).then_inc(g_free[t % 2], 1)
                elif kind in ("vs", "vw"):
                    if kind == "vw":
                        wait_small_full(act, ("vt", 0, 0))
                    nc.scalar.copy(VT[:, j, :], bank).then_inc(g_free[t % 2], 1)
                elif kind in ("ks", "kw"):
                    for half in range(2):
                        for dup in range(2):
                            nc.scalar.copy(KH[64 * dup:64 * dup + 64, 2 * j + half, int(kind == "kw"), :],
                                           GB[t % 2][64 * half:64 * half + 64, 0:SEQ]).then_inc(kh_done, 1)
                elif kind == "q":
                    for half in range(2):
                        nc.scalar.mul(QS[0:64, 2 * j + half, :], GB[t % 2][64 * half:64 * half + 64, 0:SEQ],
                                      HEAD_DIM ** -0.5).then_inc(qh_done, 1)
                elif kind == "mg":
                    nc.scalar.activation(MT[:, j, :], bank, ACT.Tanh, scale=0.5).then_inc(g_free[t % 2], 1)
                elif kind == "nsa":
                    act.wait_ge(mf_done, j + 1)
                    nc.scalar.copy(MH[:, j, :], MTMP[:, j % 2, 1, :]).then_inc(mh_done, 1)
                elif kind == "out":
                    nc.scalar.copy(OUT[:, j, :], bank)
                    if j >= 2:
                        act.wait_ge(osq_full, j - 1)
                    nc.scalar.activation(SQO[:, j % 2, :], bank, ACT.Square).then_inc(g_free[t % 2], 1)

            act.wait_ge(x_in, 16)
            nc.scalar.activation(SQX[:], XT[:], ACT.Square).then_inc(sqx_done, 1)
            act.wait_ge(par_in_s, 16)
            nc.scalar.activation(AEX[:], par("a_log"), ACT.Exp).then_inc(a_exp, 1)
            act.wait_ge(varx_done, 1)
            nc.scalar.activation(RX[:, 0, :], RX[:, 0, :], ACT.Sqrt).then_inc(rx_done, 1)
            act.wait_ge(zeros, 1)
            act.wait_ge(ada_full, 1)
            for j in range(4):
                nc.scalar.copy(ROWS[32 * j:32 * j + 1, :], SB[0][32 * j:32 * j + 1, :]).then_inc(rows_done, 1)
            for k in range(KT):
                act.wait_ge(h_f32, k + 1)
                nc.scalar.copy(HH[:, k, :], XT[:, k, :]).then_inc(h_hi, 1)
            for n in range(2):
                split_hi(n)
            act.wait_ge(cw_ready, 1)

            done = None
            for step in STEPS:
                what, i = step
                key = step + (0,)
                bank = TB[T_IDX[key] % 2] if key in T_IDX else None
                release = t_free[T_IDX[key] % 2] if key in T_IDX else None
                if what == "gemm":
                    if i + 2 in SPLIT_IDX:
                        split_hi(SPLIT_IDX[i + 2])
                    read_out(done)
                    done = finished_tile(i)
                elif what == "flush":
                    read_out(done)
                elif what == "dtT":
                    wait_small_full(act, key)
                    nc.scalar.copy(DTT[:], bank[:, 0:2 * P].rearrange("p (c f) -> p c f", c=2)).then_inc(release, 1)
                    wait_small_out(act, key)
                    nc.scalar.activation(GATE[:], DTT[:, :, GATE_ROW:GATE_ROW + 48].rearrange("p c (h n) -> p c h n", n=3),
                                         ACT.Tanh, scale=0.5).then_inc(gate_tanh, 1)
                    act.wait_ge(abs_done, 1)
                    nc.scalar.activation(DTW[:, 2], DTW[:, 0], ACT.Exp, scale=-1.0).then_inc(dt_exp, 1)
                    act.wait_ge(dt_u, 1)
                    nc.scalar.activation(DTW[:, 4], DTW[:, 3], ACT.Ln).then_inc(dt_ln, 1)
                elif what == "acs":
                    wait_small_full(act, key)
                    nc.scalar.activation(DS[:], bank[:, 256:256 + SSM_HEADS], ACT.Exp)
                    nc.scalar.copy(HI4[:], bank[:, 0:2 * P].rearrange("p (c l) -> p c l", c=2)).then_inc(hi4_done, 1)
                elif what == "bt":
                    wait_small_full(act, key)
                    nc.scalar.copy(BTOK[:].rearrange("p g n -> p (g n)"), bank[:, :]).then_inc(release, 1)
                elif what == "cb":
                    wait_small_full(act, key)
                    nc.scalar.copy(CB[:, 2 * i:2 * i + 2, :, :].rearrange("p g c l -> p (g c l)"), bank[:, :]).then_inc(release, 1)
                elif what == "st":
                    wait_small_full(act, key)
                    if i >= 1:
                        wait_y_full(act, ("y", TPG * i - 1))
                    nc.scalar.copy(STA[:], bank[:, :]).then_inc(release, 1)
                elif what == "seg":
                    n = S_IDX[step]
                    for c in range(2):
                        act.wait_ge(s_full[c], n + 1)
                        if i >= 1:
                            act.wait_ge(mm_done[c], i)
                        nc.scalar.activation(EX[:, c, :, :].rearrange("p j l -> p (j l)"), SB[c][:, :],
                                             ACT.Exp).then_inc(s_free[c], 1)
                elif what == "ea":
                    wait_small_full(act, key)
                    if i >= 1:
                        act.wait_ge(ce_done, i)
                    nc.scalar.activation(EA[:].rearrange("p j l -> p (j l)"), bank[:, :], ACT.Exp).then_inc(release, 1)
                elif what == "ysq":
                    act.wait_ge(ypre_done, TPG * (i + 1))
                    if i >= 1:
                        wait_small_full(act, ("ssq", i - 1, 0))
                    nc.scalar.activation(SQ[:], Z[:, TPG * i:TPG * (i + 1), :], ACT.Square).then_inc(ysq_done, 1)
                elif what == "ssq":
                    wait_small_out(act, key)
                    nc.scalar.activation(RN[:, 0, :], RN[:, 0, :], ACT.Sqrt).then_inc(rn_done, 1)
                elif what == "yn":
                    act.wait_ge(ynf_done, i + 1)
                    nc.scalar.copy(YNH[:, i, :], YT[:, i % 2, :]).then_inc(ynh_done, 1)
                elif what == "hidT":
                    wait_small_full(act, key)
                    if i == 0:
                        nc.scalar.mul(HIDK[:].rearrange("p k n -> p (k n)"), bank[:, 0:120], 0.5).then_inc(release, 1)
                    else:
                        act.wait_ge(zeros, 2)
                        for k in range(2):
                            src = bank[:, 60 * k:60 * k + 60].rearrange("p (g j) -> p g j", g=KV_GROUPS).unsqueeze(2)
                            last = nc.scalar.mul(HVR[:, k, :, :, 0:N_CMP], src.to_broadcast([P, KV_GROUPS, 4, N_CMP]), 0.5)
                        last.then_inc(release, 1)
                elif what == "kcp":
                    wait_small_full(act, key)
                    act.wait_ge(zeros, 5)
                    nc.scalar.copy(KCH[:, :, 0:N_CMP], bank[:, 0:60].rearrange("p (g j) -> p g j", g=KV_GROUPS)).then_inc(kch_done, 1)
                elif what == "vcp":
                    wait_small_full(act, key)
                    act.wait_ge(zeros, 3)
                    for hh in range(4):
                        rows = slice(32 * hh, 32 * hh + 32)
                        last = nc.scalar.copy(VC[rows, :, hh // 2, 64 * (hh % 2):64 * (hh % 2) + 64],
                                              bank[rows, 0:256].rearrange("p (g d) -> p g d", g=KV_GROUPS))
                    last.then_inc(release, 1)
                elif what == "vt":
                    wait_small_full(act, key)
                    nc.scalar.copy(V[:, i, :, :, :].rearrange("p k g d -> p (k g d)"), bank[:, :]).then_inc(release, 1)
                elif what == "cs":
                    act.wait_ge(cs_sub, 1)
                    nc.scalar.activation(CSW[:], CSW[:], ACT.Exp).then_inc(cs_exp, 1)
                elif what == "ct":
                    wait_small_full(act, key)
                    nc.scalar.copy(PCT[:, 2 * i:2 * i + 2, :].rearrange("p g q -> p (g q)"), bank[:, :]).then_inc(release, 1)
                elif what == "sc":
                    n, k = S_IDX[step], i % 2
                    if i >= 2:
                        wait_small_full(act, ("pt", i - 2, 1))
                    for qt in range(2):
                        act.wait_ge(max_done, 2 * i + qt + 1)
                        nk = P * (qt + 1)
                        for b in range(2):
                            c = 2 * qt + b
                            last = nc.scalar.activation(E[:, k, b, P * qt:P * qt + nk], SB[qt][:, nk * b:nk * b + nk], ACT.Exp,
                                                        bias=SM[:, k, 0, c:c + 1], accum_out=SM[:, k, 1, c:c + 1])
                        last.then_inc(s_free[qt], 1)
                elif what == "pt":
                    wait_small_full(act, key)
                    if i >= 2:
                        wait_y_full(act, ("pv", i // 2 - 1))
                    nc.scalar.copy(PT[:, i % 2, :, 0:SEQ], bank[:, :].rearrange("p (b q) -> p b q", b=2)).then_inc(release, 1)
                elif what == "osp":
                    wait_y_out(act, ("pv", i))
                    nc.scalar.copy(OH[:, i, :], ZA[:, i, :]).then_inc(oh_done, 1)
                elif what == "adag":
                    wait_small_full(act, key)
                    act.wait_ge(zeros, 7)
                    for j in range(4):
                        last = nc.scalar.copy(ROWS2[32 * j:32 * j + 1, :], bank[32 * j:32 * j + 1, 0:256])
                    last.then_inc(release, 1)
            act.wait_ge(varf_done, 1)
            nc.scalar.activation(RF[:, 0, :], RF[:, 0, :], ACT.Sqrt).then_inc(rf_done, 1)

        @block.vector
        def _(dve):
            count = [0]

            def link(ins):
                count[0] += 1
                ins.then_inc(dve_seq, 1)
                dve.wait_ge(dve_seq, count[0])

            def split_lo(n):
                u = SPLIT_UNITS[n]
                dve.wait_ge(hi_ready, n + 1)
                if n >= LO_SLOTS:
                    dve.wait_ge(unit_mm, n - LO_SLOTS + 1)
                nc.vector.tensor_tensor(WL[:, n % LO_SLOTS, :], RAW[:, u % RAW_SLOTS, :], WH[:, n % HI_SLOTS, :],
                                        ALU.subtract).then_inc(lo_ready, 1)

            def gate(tile, out_ap, src, rows=P):
                k = TH_IDX[tile]
                dve.wait_ge(th_full, k + 1)
                if tile[0] in CONV:
                    wait_tile_out(dve, tile)
                nc.vector.scalar_tensor_tensor(out_ap, TH[0:rows, k % 2, :], 1.0, src, ALU.add, ALU.mult).then_inc(gated, 1)

            pending = []

            def read_out(tile):
                if tile is None:
                    return
                kind, j = tile
                t = TILE_IDX[tile]
                bank = GB[t % 2][:, 0:SEQ]
                if kind in CONV:
                    ci, col = conv_index(kind, j), conv_src(kind, j)
                    dve.wait_ge(conv_acc, ci + 1)
                    for tap in (2, 1, 0):
                        s = 3 - tap
                        ins = nc.vector.scalar_tensor_tensor(ACC[:, ci % 2, s:SEQ], GB[t % 2][:, 0:SEQ - s],
                                                             CW[:, 4 * col + tap:4 * col + tap + 1], ACC[:, ci % 2, s:SEQ],
                                                             ALU.mult, ALU.add)
                        if tap:
                            link(ins)
                        else:
                            ins.then_inc(g_free[t % 2], 1)
                if pending:
                    prev = pending.pop()
                    ci = conv_index(*prev)
                    if prev[0] == "x" and prev[1] >= 2 * TPG:
                        wait_small_full(dve, ("xt", (prev[1] // TPG - 2, 1), 0))
                        wait_y_out(dve, ("y", TPG * (prev[1] // TPG - 2) + 3))
                    gate(prev, conv_dst(*prev), ACC[:, ci % 2, :])
                if kind in CONV:
                    pending.append(tile)
                elif kind in ("z", "za"):
                    gate(tile, (Z if kind == "z" else ZA)[:, j, :], bank)
                elif kind in NATIVE:
                    gate(tile, HID[0:60, int(kind == "w1v"), :], GB[t % 2][0:60, 0:CMP_HIDDEN], 60)
                elif kind in ("ks", "kw"):
                    br = int(kind == "kw")
                    for half in range(2):
                        for dup in range(2):
                            dve.wait_ge(kh_done, 8 * br + 4 * j + 4)
                            rows = slice(64 * dup, 64 * dup + 64)
                            last = nc.vector.tensor_tensor(KL[rows, 2 * j + half, br, :], GB[t % 2][64 * half:64 * half + 64, 0:SEQ],
                                                           KH[rows, 2 * j + half, br, :], ALU.subtract)
                    last.then_inc(g_free[t % 2], 1)
                elif kind == "q":
                    for half in range(2):
                        dve.wait_ge(qh_done, 2 * j + 2)
                        last = nc.vector.scalar_tensor_tensor(QS[64:128, 2 * j + half, :], GB[t % 2][64 * half:64 * half + 64, 0:SEQ],
                                                              HEAD_DIM ** -0.5, QS[0:64, 2 * j + half, :], ALU.mult, ALU.subtract)
                    last.then_inc(g_free[t % 2], 1)
                elif kind == "ssm":
                    wait_tile_full(dve, tile)
                    nc.vector.scalar_tensor_tensor(YS[:, j, :], MT[:, j, :], 1.0, bank, ALU.add, ALU.mult).then_inc(g_free[t % 2], 1)
                elif kind == "nsa":
                    wait_tile_full(dve, tile)
                    if j >= 2:
                        dve.wait_ge(ml_done, j - 1)
                    nc.vector.scalar_tensor_tensor(MTMP[:, j % 2, 0, :], MT[:, 8 + j, :], 1.0, bank, ALU.add,
                                                   ALU.mult).then_inc(g_free[t % 2], 1)
                    wait_tile_out(dve, tile)
                    nc.vector.tensor_tensor(MTMP[:, j % 2, 1, :], MTMP[:, j % 2, 0, :], YS[:, j, :], ALU.add).then_inc(mf_done, 1)
                    for m in ([j - 1] if j else []) + ([7] if j == 7 else []):
                        dve.wait_ge(mh_done, m + 1)
                        nc.vector.tensor_tensor(ML[:, m, :], MTMP[:, m % 2, 1, :], MH[:, m, :], ALU.subtract).then_inc(ml_done, 1)

            dve.wait_ge(par_in_s, 16)
            nc.vector.tensor_scalar(CW[:], PR[:, PAR["conv_w"][0]:PAR["conv_b"][1]], 0.5, None, ALU.mult).then_inc(cw_ready, 1)
            dve.wait_ge(ssx_full, 1)
            nc.vector.tensor_scalar(RX[:, 0, :], YB[0][:, 0:SEQ], 1.0 / D_MODEL, EPS, ALU.mult, ALU.add).then_inc(varx_done, 1)
            dve.wait_ge(rx_done, 1)
            link(nc.vector.reciprocal(RX[:, 1, :], RX[:, 0, :]))
            link(nc.vector.tensor_tensor(XT[:], XT[:], RX[:, 1, :].unsqueeze(1).to_broadcast([P, KT, SEQ]), ALU.mult))
            dve.wait_ge(modT_full, 1)
            rows = SB[1][:, :].rearrange("p (m j r) -> p j m r", m=4, j=4)[:, :, :, 0]
            link(nc.vector.tensor_tensor(MOD[:].rearrange("p (j m) -> p j m", j=4), rows,
                                         par("b_ada", 0, 16).rearrange("p (j m) -> p j m", j=4), ALU.add))
            link(nc.vector.scalar_tensor_tensor(AB[:, 0:8], MOD[:, 8:16], 1.0, par("g_pre"), ALU.add, ALU.mult))
            for k in range(KT):
                nc.vector.tensor_scalar(XT[:, k, :], XT[:, k, :], AB[:, k:k + 1], MOD[:, k:k + 1], ALU.mult,
                                        ALU.add).then_inc(h_f32, 1)
                if k >= 1:
                    dve.wait_ge(h_hi, k)
                    nc.vector.tensor_tensor(HL[:, k - 1, :], XT[:, k - 1, :], HH[:, k - 1, :], ALU.subtract).then_inc(h_ready, 1)
            dve.wait_ge(h_hi, KT)
            nc.vector.tensor_tensor(HL[:, KT - 1, :], XT[:, KT - 1, :], HH[:, KT - 1, :], ALU.subtract).then_inc(h_ready, 1)
            for n in range(2):
                split_lo(n)

            done = None
            for step in STEPS:
                what, i = step
                key = step + (0,)
                bank = TB[T_IDX[key] % 2] if key in T_IDX else None
                release = t_free[T_IDX[key] % 2] if key in T_IDX else None
                if what == "gemm":
                    if i + 2 in SPLIT_IDX:
                        split_lo(SPLIT_IDX[i + 2])
                    read_out(done)
                    done = finished_tile(i)
                elif what == "flush":
                    read_out(done)
                elif what == "dtT":
                    wait_small_out(dve, key)
                    x = DTT[:, :, 0:SSM_HEADS]
                    nc.vector.scalar_tensor_tensor(DTW[:, 0], x, -1.0, x, ALU.mult, ALU.max).then_inc(abs_done, 1)
                    nc.vector.tensor_scalar(DTW[:, 1], x, 0.0, None, ALU.max)
                    dve.wait_ge(dt_exp, 1)
                    nc.vector.tensor_scalar(DTW[:, 3], DTW[:, 2], 1.0, None, ALU.add).then_inc(dt_u, 1)
                    dve.wait_ge(dt_u, 1)
                    nc.vector.tensor_scalar(DT[:], DTW[:, 3], 1.0, None, ALU.subtract)
                    link(nc.vector.reciprocal(DTW[:, 5], DTW[:, 3]))
                    link(nc.vector.tensor_tensor(DT[:], DTW[:, 2], DT[:], ALU.subtract))
                    link(nc.vector.tensor_tensor(DT[:], DT[:], DTW[:, 5], ALU.mult))
                    link(nc.vector.tensor_tensor(DT[:], DT[:], DTW[:, 1], ALU.add))
                    dve.wait_ge(dt_ln, 1)
                    link(nc.vector.tensor_tensor(DT[:], DT[:], DTW[:, 4], ALU.add))
                    dve.wait_ge(a_exp, 1)
                    link(nc.vector.tensor_tensor(DTW[:, 0], DT[:], AEX[:].unsqueeze(1).to_broadcast([P, 2, SSM_HEADS]), ALU.mult))
                    nc.vector.tensor_scalar(ADT4[:], DTW[:, 0].unsqueeze(2).to_broadcast([P, 2, 4, SSM_HEADS]), -1.0, None,
                                            ALU.mult).then_inc(adt_done, 1)
                    dve.wait_ge(gate_tanh, 1)
                    nc.vector.tensor_scalar(GATE[:], GATE[:], 0.25, 0.25, ALU.mult, ALU.add)
                elif what == "acs":
                    dve.wait_ge(hi4_done, 1)
                    dve.wait_ge(consts_made, 7)
                    acs = bank[:, 0:2 * P].rearrange("p (c l) -> p c l", c=2)
                    nc.vector.tensor_copy(TP[0:32], HI4[0:32]).then_inc(cols_ready, 1)
                    nc.vector.tensor_tensor(TP[32:64], acs[32:64], HI4[32:64], ALU.subtract).then_inc(cols_ready, 1)
                    nc.vector.tensor_copy(ST[64:96], HI4[64:96]).then_inc(cols_ready, 1)
                    nc.vector.tensor_tensor(ST[96:128], acs[96:128], HI4[96:128], ALU.subtract).then_inc(cols_ready, 1)
                    nc.vector.tensor_copy(HI4X[:], bank[0:1, 0:1]).then_inc(release, 1)
                elif what == "xt":
                    g, c = i
                    wait_small_full(dve, key)
                    if g >= 1:
                        wait_y_full(dve, ("y", TPG * g - 1))
                    if c == 0 and g >= 1:
                        dve.wait_ge(xds_done, g)
                    dt = DT[:, c, HPC * g:HPC * (g + 1)].unsqueeze(2).to_broadcast([P, HPC, HEAD_DIM])
                    nc.vector.tensor_tensor(XDT[:, c, :, :], bank[:, :].rearrange("p (h d) -> p h d", h=HPC), dt,
                                            ALU.mult).then_inc(release, 1)
                elif what == "seg":
                    dve.wait_ge(s_free[0], S_IDX[step] + 1)
                    if i >= 1:
                        wait_y_full(dve, ("y", 2 * i - 1))
                        wait_y_full(dve, ("y", 2 * i - 2))
                    wait_small_out(dve, ("cb", i // 4, 0))
                    nc.vector.tensor_tensor(MM[:, 0, :, :], EX[:, 0, :, :], CB[:, i // 2, 0, :].unsqueeze(1).to_broadcast([P, 4, P]),
                                            ALU.mult).then_inc(mm_done[0], 1)
                elif what == "y":
                    n = Y_IDX[step]
                    wait_y_full(dve, step)
                    x = XG[:, (i // TPG) % 2, i % TPG, :]
                    nc.vector.scalar_tensor_tensor(x, x, par("d_skip", i, i + 1), YB[n % 2][:, 0:SEQ], ALU.mult,
                                                   ALU.add).then_inc(y_free[n % 2], 1)
                    wait_y_out(dve, step)
                    nc.vector.tensor_tensor(Z[:, i, :], x, Z[:, i, :], ALU.mult).then_inc(ypre_done, 1)
                elif what == "ssq":
                    wait_small_full(dve, key)
                    gsz = D_INNER // SSM_GROUPS
                    nc.vector.tensor_scalar(RN[:, 0, :], bank[:, 0:SEQ], 1.0 / gsz, 4.0 * EPS, ALU.mult, ALU.add).then_inc(release, 1)
                elif what == "yn":
                    if i % TPG == 0:
                        dve.wait_ge(rn_done, i // TPG + 1)
                        link(nc.vector.reciprocal(RN[:, 1, :], RN[:, 0, :]))
                        dve.wait_ge(ysq_done, i // TPG + 1)
                    if i >= 2:
                        dve.wait_ge(yn_done, i - 1)
                    nc.vector.scalar_tensor_tensor(YT[:, i % 2, :], Z[:, i, :], par("g_ssm", i, i + 1), RN[:, 1, :], ALU.mult,
                                                   ALU.mult).then_inc(ynf_done, 1)
                elif what == "ynlo":
                    dve.wait_ge(ynh_done, i + 1)
                    nc.vector.tensor_tensor(YNL[:, i, :], YT[:, i % 2, :], YNH[:, i, :], ALU.subtract).then_inc(yn_done, 1)
                elif what == "blk" and i == 0:
                    compress_blocks(dve, nc.vector, 0)
                elif what == "kcp":
                    dve.wait_ge(kch_done, 1)
                    nc.vector.tensor_tensor(KCL[:, :, 0:N_CMP], bank[:, 0:60].rearrange("p (g j) -> p g j", g=KV_GROUPS),
                                            KCH[:, :, 0:N_CMP], ALU.subtract).then_inc(release, 1)
                elif what == "cs":
                    wait_small_full(dve, key)
                    sc = bank[:, :].rearrange("p (t h j) -> p t h j", t=2, h=ATT_HEADS)
                    nc.vector.tensor_tensor(CSW[:], sc, cst("bias_c").rearrange("p (t h j) -> p t h j", t=2, h=ATT_HEADS),
                                            ALU.add).then_inc(release, 1)
                    wait_small_out(dve, key)
                    link(nc.vector.tensor_reduce(CSM[:, 0], CSW[:], AX.X, ALU.max))
                    nc.vector.tensor_tensor(CSW[:], CSW[:], CSM[:, 0].unsqueeze(3).to_broadcast([P, 2, ATT_HEADS, 16]),
                                            ALU.subtract).then_inc(cs_sub, 1)
                elif what == "cs2":
                    dve.wait_ge(cs_exp, 1)
                    dve.wait_ge(zeros, 6)
                    link(nc.vector.tensor_reduce(CSM[:, 1], CSW[:], AX.X, ALU.add))
                    link(nc.vector.reciprocal(CSM[:, 2], CSM[:, 1]))
                    nc.vector.tensor_tensor(CSM[:, 0], CSM[:, 2], GATE[:, :, :, 0], ALU.mult)
                    valid = cst("valid_c").rearrange("p (t j) -> p t j", t=2).unsqueeze(2).to_broadcast([P, 2, ATT_HEADS, 16])
                    link(nc.vector.tensor_tensor(CSW[:], CSW[:], valid, ALU.mult))
                    nc.vector.tensor_tensor(PC[:, :, :, 0:16], CSW[:], CSM[:, 0].unsqueeze(3).to_broadcast([P, 2, ATT_HEADS, 16]),
                                            ALU.mult).then_inc(pc_done, 1)
                elif what == "sc":
                    n, k = S_IDX[step], i % 2
                    for qt in range(2):
                        dve.wait_ge(s_full[qt], n + 1)
                        nk = P * (qt + 1)
                        nc.vector.tensor_reduce(SM[:, k, 0, 2 * qt:2 * qt + 2], SB[qt][:, 0:2 * nk].rearrange("p (b n) -> p b n", b=2),
                                                AX.X, ALU.max, negate=True).then_inc(max_done, 1)
                elif what == "ps":
                    n, k = S_IDX[("sc", i)], i % 2
                    dve.wait_ge(s_free[0], n + 1)
                    dve.wait_ge(s_free[1], n + 1)
                    link(nc.vector.reciprocal(SM[:, k, 2, :], SM[:, k, 1, :]))
                    link(nc.vector.tensor_tensor(SM[:, k, 3, :].rearrange("p (t b) -> p t b", t=2),
                                                 SM[:, k, 2, :].rearrange("p (t b) -> p t b", t=2), GATE[:, :, i, 1:3], ALU.mult))
                    for qt in range(2):
                        for b in range(2):
                            e = E[:, k, b, P * qt:P * qt + P * (qt + 1)]
                            nc.vector.tensor_scalar(e, e, SM[:, k, 3, 2 * qt + b:2 * qt + b + 1], None, ALU.mult).then_inc(p_done, 1)
                elif what == "pt":
                    key1 = step + (1,)
                    wait_small_full(dve, key1)
                    if i >= 2:
                        wait_y_full(dve, ("pv", i // 2 - 1))
                    if i < 2:
                        wait_small_full(dve, ("ct", 1, 0))
                    nc.vector.tensor_copy(PT[:, i % 2, :, SEQ:SEQ + P],
                                          TB[T_IDX[key1] % 2][:, 0:SEQ].rearrange("p (b q) -> p b q", b=2)
                                          ).then_inc(t_free[T_IDX[key1] % 2], 1)
                elif what == "pv":
                    n = Y_IDX[step]
                    wait_y_full(dve, step)
                    dve.wait_ge(gated, TH_IDX[("za", i)] + 1)
                    nc.vector.tensor_tensor(ZA[:, i, :], ZA[:, i, :], YB[n % 2][:, 0:SEQ], ALU.mult).then_inc(y_free[n % 2], 1)
                elif what == "osp":
                    dve.wait_ge(oh_done, i + 1)
                    nc.vector.tensor_tensor(OL[:, i, :], ZA[:, i, :], OH[:, i, :], ALU.subtract).then_inc(o_split, 1)
                elif what == "adagT":
                    wait_small_full(dve, key)
                    rows = bank[:, 0:2 * P].rearrange("p (m j r) -> p j m r", m=2, j=4)[:, :, :, 0]
                    link(nc.vector.tensor_tensor(GG[:, 0, :].rearrange("p (j m) -> p j m", j=4), rows,
                                                 par("b_ada", 16, 24).rearrange("p (j m) -> p j m", j=4), ALU.add))
                    link(nc.vector.tensor_tensor(GG[:, 1, :], GG[:, 0, :], par("g_post"), ALU.mult))
            dve.wait_ge(osq_full, 8)
            nc.vector.tensor_scalar(RF[:, 0, :], YB[0][:, 0:SEQ], 1.0 / D_MODEL, 4.0 * EPS, ALU.mult, ALU.add).then_inc(varf_done, 1)
            dve.wait_ge(rf_done, 1)
            link(nc.vector.reciprocal(RF[:, 1, :], RF[:, 0, :]))
            dve.wait_ge(xr_in, 16)
            wait_tile_out(dve, ("out", 6))
            wait_tile_out(dve, ("out", 7))
            for m in range(9):
                if m < 8:
                    nc.vector.scalar_tensor_tensor(OUT[:, m, :], OUT[:, m, :], GG[:, 1, m:m + 1], RF[:, 1, :], ALU.mult,
                                                   ALU.mult).then_inc(dve_seq, 1)
                    count[0] += 1
                if m >= 1:
                    dve.wait_ge(dve_seq, count[0] - (1 if m < 8 else 0))
                    nc.vector.tensor_tensor(OUT[:, m - 1, :], OUT[:, m - 1, :], XR[:, m - 1, :], ALU.add).then_inc(fin_done, 1)

        @block.gpsimd
        def _(pool):
            made = [0]

            def link(ins):
                made[0] += 1
                ins.then_inc(pool_seq, 1)
                pool.wait_ge(pool_seq, made[0])

            nc.gpsimd.memset(ROWS[:], 0.0).then_inc(zeros, 1)
            pool.wait_ge(zeros, 1)
            for n, (ap, value) in enumerate(((ST[0:64].bitcast(f32), 1.0), (TP[64:128], -1.0), (ONZ[0:64].bitcast(f32), 1.0),
                                             (ONZ[64:128].bitcast(f32), 0.0))):
                nc.gpsimd.memset(ap, value).then_inc(consts_made, 1)
                pool.wait_ge(consts_made, n + 1)
            pool.wait_ge(cst_in_s, 16)
            nc.gpsimd.tensor_copy(IDB[:], cst("ident")).then_inc(consts_made, 1)
            nc.gpsimd.tensor_copy(MSL[:], cst("mask_sl")).then_inc(consts_made, 1)
            nc.gpsimd.tensor_copy(MQK[:], cst("mask_qk")).then_inc(consts_made, 1)

            def moving_rows(quad):
                for c in range(2):
                    oh = cst("onehot", 4 * quad, 4 * quad + 4).unsqueeze(2).to_broadcast([P, 4, P])
                    nc.gpsimd.tensor_tensor(MV[:, c, :, :], TP[:, c, :].unsqueeze(1).to_broadcast([P, 4, P]), oh,
                                            ALU.mult).then_inc(mv_done, 1)

            for step in STEPS:
                what, i = step
                key = step + (0,)
                if what == "acs":
                    pool.wait_ge(cols_ready, 4)
                    moving_rows(0)
                elif what == "xt" and i[1] == 0:
                    g = i[0]
                    wait_small_out(pool, key)
                    if g >= 1:
                        wait_small_full(pool, ("st", g - 1, 0))
                    pool.wait_ge(hi4_done, 1)
                    nc.gpsimd.tensor_tensor(XDS[:], XDT[:, 0, :, :],
                                            DS[:, HPC * g:HPC * (g + 1)].unsqueeze(2).to_broadcast([P, HPC, HEAD_DIM]),
                                            ALU.mult).then_inc(xds_done, 1)
                elif what == "seg":
                    pool.wait_ge(s_free[1], S_IDX[step] + 1)
                    if i >= 1:
                        wait_y_full(pool, ("y", 2 * i - 1))
                        wait_y_full(pool, ("y", 2 * i - 2))
                    wait_small_out(pool, ("cb", i // 4, 0))
                    nc.gpsimd.tensor_tensor(MM[:, 1, :, :], EX[:, 1, :, :], CB[:, i // 2, 1, :].unsqueeze(1).to_broadcast([P, 4, P]),
                                            ALU.mult).then_inc(mm_done[1], 1)
                elif what == "ea":
                    wait_small_out(pool, key)
                    g = i // 2
                    nc.gpsimd.tensor_tensor(CE[:], EA[:], CTT[:, g, CHUNK:SEQ].unsqueeze(1).to_broadcast([P, 4, P]),
                                            ALU.mult).then_inc(ce_done, 1)
                    if i + 1 < QUADS:
                        moving_rows(i + 1)
                elif what == "blk" and i == 0:
                    nc.gpsimd.memset(HVR[:], 0.0).then_inc(zeros, 1)
                elif what == "blk":
                    compress_blocks(pool, nc.gpsimd, 1)
                    nc.gpsimd.memset(VC[:], 0.0).then_inc(zeros, 1)
                    nc.gpsimd.memset(KCH[:].bitcast(f32), 0.0).then_inc(zeros, 1)
                    nc.gpsimd.memset(KCL[:].bitcast(f32), 0.0).then_inc(zeros, 1)
                elif what == "cs":
                    pool.wait_ge(ynf_done, 16)
                    nc.gpsimd.memset(PC[:], 0.0).then_inc(zeros, 1)
                elif what == "osp" and i == 7:
                    wait_y_full(pool, ("pv", 7))
                    nc.gpsimd.memset(ROWS2[:], 0.0).then_inc(zeros, 1)


def host_constants():
    f = np.float32
    i = np.arange(P)
    onehot = (i[:, None] % SSM_HEADS == np.arange(SSM_HEADS)[None, :]).astype(f)
    slopes = (2.0 ** (-8.0 * np.arange(1, ATT_HEADS + 1) / ATT_HEADS)).astype(f)
    t = np.arange(SEQ).reshape(2, P).T
    end = np.arange(16) * CMP_STRIDE + CMP_BLOCK - 1
    dist = (t[:, :, None] - end[None, None, :]).astype(f)
    valid = (dist >= 0) & (np.arange(16) < N_CMP)[None, None, :]
    bias = np.where(valid[:, :, None, :], -slopes[None, None, :, None] * dist[:, :, None, :], f(NEG)).astype(f)
    parts = {"ident": np.eye(P), "tri": i[:, None] <= i[None, :], "tri_strict": i[:, None] > i[None, :],
             "ones": np.ones((P, P)), "mask_sl": np.where(i[None, :] < i[:, None], NEG, 0.0),
             "mask_qk": np.where(i[None, :] > i[:, None], NEG, 0.0), "onehot": onehot,
             "bias_c": bias.reshape(P, -1), "valid_c": valid.reshape(P, -1)}
    consts = np.concatenate([np.asarray(parts[n], f).reshape(P, -1) for n in CST if n != "end"], axis=1)

    def bf16_bits(v):
        out, rest = [], v.astype(f)
        for _ in range(3):
            bits = rest.view(np.uint32) & np.uint32(0xFFFF0000)
            out.append((bits >> 16).astype(np.uint16))
            rest = (rest - bits.view(f)).astype(f)
        return out

    alibi_q = np.zeros((P, ATT_HEADS, SEQ), np.uint16)
    alibi_k = np.zeros((P, 2, SEQ), np.uint16)
    pos = np.arange(SEQ, dtype=f)
    for n, bits in enumerate(bf16_bits(np.repeat(slopes[:, None], SEQ, 1).copy())):
        alibi_q[n] = bits
        alibi_k[n] = (pos.view(np.uint32) >> 16).astype(np.uint16)[None, :]
    for n, bits in enumerate(bf16_bits((-slopes[:, None] * pos[None, :]).astype(f))):
        alibi_q[3 + n] = bits
        alibi_k[3 + n] = np.uint16(0x3F80)
    return consts, alibi_q.reshape(P, -1), alibi_k


def lay_out(inputs):
    w = {k: np.asarray(v) for k, v in inputs.items()}
    f = np.float32

    def cols(v, n):
        return v.reshape(n, P).T

    def tile_of(m):
        k, n = m.shape
        return m.reshape(k // P, P, n // P, P).transpose(2, 1, 0, 3)

    w_in = w["w_in"][0]
    lens = {"z": (OFF_Z, D_INNER), "x": (OFF_X, D_INNER), "b": (OFF_B, 512), "c": (OFF_C, 512), "q": (OFF_Q, 1024),
            "kc": (OFF_KV, 256), "vc": (OFF_KV + 256, 256), "ks": (OFF_KV + 512, 256), "vs": (OFF_KV + 768, 256),
            "kw": (OFF_KV + 1024, 256), "vw": (OFF_KV + 1280, 256), "za": (OFF_ZA, 1024), "mg": (OFF_MG, 2048)}
    tiles = {k: tile_of(w_in[:, a:a + n]) for k, (a, n) in lens.items()}
    dtg = np.zeros((D_MODEL, P), f)
    dtg[:, 0:SSM_HEADS] = w_in[:, OFF_DT:OFF_DT + SSM_HEADS]
    dtg[:, GATE_ROW:GATE_ROW + 48] = w_in[:, OFF_GATE:OFF_GATE + 48]
    tiles["dtg"] = tile_of(dtg)
    ssm = tile_of(w["w_ssm_out"][0])
    tiles["nsa"], tiles["out"] = tile_of(w["w_nsa_out"][0]), tile_of(w["w_out"][0])
    w1 = {k: w[n][0].reshape(16, 2, 64, CMP_HIDDEN).transpose(1, 2, 0, 3).reshape(P, 4, 1024)
          for k, n in (("w1k", "cmp_w1_k"), ("w1v", "cmp_w1_v"))}
    wpack = np.empty((len(UNITS), P, 1024), f)
    for u, (kind, j, part) in enumerate(UNITS):
        if kind in w1:
            wpack[u] = w1[kind][:, part]
        elif kind == "ssm":
            wpack[u] = ssm[j][:, 8 * part:8 * part + 8].reshape(P, 1024)
        else:
            wpack[u] = tiles[kind][j].reshape(P, 1024)
    dt_bias = np.zeros((P, 1), f)
    dt_bias[0:SSM_HEADS, 0] = w["dt_bias"][0]
    pos = {k: np.concatenate([w[k][0].T, w[k][0].T], 0) for k in ("cmp_pos_k", "cmp_pos_v")}
    w2 = {k: w[k][0].reshape(2, P, 64).transpose(1, 0, 2) for k in ("cmp_w2_k", "cmp_w2_v")}
    parts = {"c": cols(w["c"][0], KT), "conv_w": w["conv_w"][0].reshape(4, 24, P).transpose(2, 1, 0).reshape(P, 96),
             "conv_b": cols(w["conv_b"][0], 24), "dt_bias": dt_bias, "g_pre": cols(w["g_pre"][0], 8),
             "g_post": cols(w["g_post"][0], 8), "b_ada": cols(w["b_ada"][0], 24), "g_ssm": cols(w["g_ssm_norm"][0], 16),
             "d_skip": cols(np.repeat(w["d_skip"][0], HEAD_DIM), 16), "a_log": np.repeat(w["a_log"], P, 0),
             "pos_k": pos["cmp_pos_k"], "pos_v": pos["cmp_pos_v"],
             "w2k": np.concatenate([w2["cmp_w2_k"]] * 2, 2).reshape(P, 256), "w2v": w2["cmp_w2_v"].reshape(P, 128)}
    params = np.concatenate([parts[n] for n in PAR if n != "end"], axis=1)
    xT = w["x"][0].T.reshape(KT, P, SEQ).transpose(1, 0, 2)
    ada = w["w_ada"][0].reshape(KT, P, 3 * D_MODEL).transpose(1, 0, 2)
    consts, alibi_q, alibi_k = host_constants()
    return {"xT": xT, "params": params, "consts": consts, "alibi_q": alibi_q, "alibi_k": alibi_k,
            "w_ada1": ada[:, :, 0:2048], "w_ada2": ada[:, :, 2048:3072], "wpack": wpack}


def kernel(**inputs):
    import concourse.bacc as bacc
    from concourse.bass_utils import run_bass_kernel_spmd

    nc = bacc.Bacc("TRN2", target_bir_lowering=False, num_devices=1)
    arrays, args = {}, []
    for name, a in lay_out(inputs).items():
        a = np.ascontiguousarray(a)
        arrays[f"in_{name}"] = a
        args.append(nc.dram_tensor(f"in_{name}", a.shape, mybir.dt.from_np(a.dtype), kind="ExternalInput").ap())
    out = nc.dram_tensor("out_T_dram", (P, KT, SEQ), mybir.dt.float32, kind="ExternalOutput").ap()
    build(nc, *args, out)
    r = run_bass_kernel_spmd(nc, [arrays], core_ids=[0])
    got = r.results[0]["out_T_dram"]
    return got.transpose(2, 1, 0).reshape(1, SEQ, D_MODEL)
```

```python
import math

import numpy as np

import concourse.bass as bass
from concourse import mybir

P = 128
SEQ, D_MODEL = 256, 1024
D_INNER, SSM_HEADS, HEAD_DIM, SSM_GROUPS, STATE, CHUNK = 2048, 32, 64, 4, 128, 128
ATT_HEADS, KV_GROUPS, HPG = 16, 4, 4
CMP_BLOCK, CMP_STRIDE, CMP_HIDDEN = 32, 16, 256
N_CMP = (SEQ - CMP_BLOCK) // CMP_STRIDE + 1
EPS = 1e-6
NEG = -1e30
KT = D_MODEL // P
NCHUNK = SEQ // CHUNK
HPC = SSM_HEADS // SSM_GROUPS
QUADS = SSM_HEADS // 4
TPG = 4

D_CONV = D_INNER + 2 * SSM_GROUPS * STATE
OFF_Z = 0
OFF_X = D_INNER
OFF_B = OFF_X + D_INNER
OFF_C = OFF_B + SSM_GROUPS * STATE
OFF_DT = OFF_X + D_CONV
OFF_Q = OFF_DT + SSM_HEADS
OFF_KV = OFF_Q + ATT_HEADS * HEAD_DIM
OFF_GATE = OFF_KV + 6 * KV_GROUPS * HEAD_DIM
OFF_ZA = OFF_GATE + 3 * ATT_HEADS
OFF_MG = OFF_ZA + ATT_HEADS * HEAD_DIM
GATE_ROW = 64


def weight_units():
    units = [("dtg", 0, 0)]
    units += [("b", j, 0) for j in range(4)] + [("c", j, 0) for j in range(4)]
    for g in range(SSM_GROUPS):
        units += [("x", TPG * g + j, 0) for j in range(TPG)] + [("z", TPG * g + j, 0) for j in range(TPG)]
    units += [("kc", j, 0) for j in range(2)] + [("vc", j, 0) for j in range(2)]
    units += [("za", j, 0) for j in range(6)]
    units += [("za", 6, 0), ("ag", 0, 0), ("za", 7, 0), ("ag", 0, 1)]
    units += [("w1k", 0, part) for part in range(4)] + [("w1v", 0, part) for part in range(4)]
    for n, kind in enumerate(("ks", "kw", "vs")):
        for j in range(2):
            units += [(kind, j, 0), ("ag", 0, 2 + 2 * n + j)]
    units += [("q", j, 0) for j in range(8)] + [("vw", j, 0) for j in range(2)]
    units += [("mg", j, 0) for j in range(16)]
    units += [("ssm", j, part) for j in range(8) for part in range(2)]
    units += [("nsa", j, 0) for j in range(8)] + [("out", j, 0) for j in range(8)]
    return units


UNITS = weight_units()
NATIVE = ("w1k", "w1v", "ag")
CONV = ("b", "c", "x")
LAST_PART = {"w1k": 3, "w1v": 3, "ssm": 1, "ag": 8}


def schedule():
    after = {}

    def put(u, *steps):
        after.setdefault(u, []).extend(steps)

    put(2, ("dtT", 0))
    put(4, ("dtA", 0), ("dtE", 0))
    put(6, ("dtB", 0), ("dtL", 0))
    put(8, ("bt", 0), ("dtC", 0))
    put(10, ("acs", 0))
    put(11, ("cb", 0))
    put(12, ("cb", 1))
    for g in range(SSM_GROUPS):
        b = 17 + 8 * g
        put(b, ("xt", (g, 0)))
        put(b + 1, ("xt", (g, 1)), ("seg", 2 * g))
        put(b + 2, ("ea", 2 * g))
        put(b + 3, ("st", g))
        put(b + 4, ("y", 2 * g), ("seg", 2 * g + 1))
        put(b + 5, ("ea", 2 * g + 1))
        put(b + 7, ("y", 2 * g + 1))
        put(b + 8, ("ysq", g))
        put(b + 9, ("ssq", g))
        for j in range(TPG + 2):
            for ahead, name in ((2, "ynlo"), (1, "ynhi"), (0, "yn")):
                if 0 <= j - ahead < TPG:
                    put(b + 11 + j, (name, TPG * g + j - ahead))
    put(47, ("blk", 1))
    put(48, ("blk", 0))
    at = UNITS.index
    put(at(("w1k", 0, 3)) + 2, ("hidT", 0))
    put(at(("w1v", 0, 3)) + 2, ("hidT", 1))
    put(at(("w1v", 0, 3)) + 1, ("kcp", 0))
    put(at(("w1v", 0, 3)) + 4, ("vcp", 0))
    put(at(("vs", 1, 0)) + 2, ("vt", 0))
    put(at(("w1v", 0, 3)) + 3, ("zero", 0))
    put(at(("ag", 0, 7)) + 1, ("agR", 0))
    put(at(("ag", 0, 7)) + 2, ("agT", 0))
    q0 = at(("q", 0, 0))
    put(q0 + 8, ("cs", 0), ("cs", 1))
    put(q0 + 9, ("cs2", 0))
    put(q0 + 10, ("vt", 1))
    put(q0 + 12, ("ct", 0), ("ct", 1))
    t0 = q0 + 5
    for h in range(ATT_HEADS):
        put(t0 + 2 * h, ("sc", h))
        put(t0 + 1 + 2 * h, ("ex", h))
        put(t0 + 2 + 2 * h, ("ps", h))
        put(t0 + 4 + 2 * h, ("pt", h))
    last_h = at(("mg", 15, 0))
    for p in range(ATT_HEADS // 2):
        put(t0 + 8 + 4 * p + (p == 0), ("pv", p))
        put(max(last_h + 3, t0 + 8 + 4 * p), ("osp", p))
    out0 = UNITS.index(("out", 0, 0))
    for m in range(7):
        put(out0 + 1 + m, ("osq", m))
    steps = []
    for u in range(len(UNITS)):
        steps.append(("gemm", u))
        steps += after.get(u, [])
    steps += [("flush", 0), ("osq", 7)]
    late = []
    for u in range(len(UNITS)):
        late += [("gemm", u)] + after.get(u - 1, [])
    late += [("flush", 0)] + after.get(len(UNITS) - 1, [])
    return steps, late


STEPS, LATE_STEPS = schedule()
SPLIT_IDX, NATIVE_IDX, TILE_IDX = {}, {}, {}
for _u, (_kind, _j, _part) in enumerate(UNITS):
    if _kind in NATIVE:
        NATIVE_IDX[_u] = len(NATIVE_IDX)
    else:
        SPLIT_IDX[_u] = len(SPLIT_IDX)
    if _part == 0 and _kind != "ag":
        TILE_IDX[(_kind, _j)] = len(TILE_IDX)
SPLIT_UNITS = sorted(SPLIT_IDX)
T_STEPS = ("dtT", "acs", "bt", "cb", "xt", "ea", "st", "ssq", "hidT", "kcp", "vcp", "vt", "cs", "ct", "pt", "agT")
T_IDX, S_IDX, Y_IDX, HAPPENS = {}, {}, {}, {}
_seen = {}
for _s in STEPS:
    HAPPENS[_s] = _seen.get(_s[0], 0)
    _seen[_s[0]] = HAPPENS[_s] + 1
    if _s[0] in T_STEPS:
        for _n in range(2 if _s[0] == "pt" else 1):
            T_IDX[_s + (_n,)] = len(T_IDX)
    if _s[0] in ("seg", "sc"):
        S_IDX[_s] = len(S_IDX)
    if _s[0] in ("y", "pv"):
        Y_IDX[_s] = len(Y_IDX)

TH_IDX, _pending = {}, None
for _kind, _j, _part in UNITS:
    if _part != LAST_PART.get(_kind, 0):
        continue
    if _kind in CONV or _pending:
        if _pending:
            TH_IDX[_pending] = len(TH_IDX)
            _pending = None
    if _kind in CONV:
        _pending = (_kind, _j)
    elif _kind in ("z", "za", "w1k", "w1v"):
        TH_IDX[(_kind, _j)] = len(TH_IDX)

PAR = {}


def _par(name, n):
    PAR[name] = (PAR["end"][1] if "end" in PAR else 0, (PAR["end"][1] if "end" in PAR else 0) + n)
    PAR["end"] = (0, PAR[name][1])


for _name, _n in (("c", KT), ("conv_w", 96), ("conv_b", 24), ("dt_bias", 1), ("g_pre", 8), ("g_post", 8), ("b_ada", 24),
                  ("g_ssm", 16), ("d_skip", 16), ("a_log", SSM_HEADS), ("pos_k", 32), ("pos_v", 32),
                  ("w2k", 256), ("w2v", 128)):
    _par(_name, _n)
CST = {}


def _cst(name, n):
    CST[name] = (CST["end"][1] if "end" in CST else 0, (CST["end"][1] if "end" in CST else 0) + n)
    CST["end"] = (0, CST[name][1])


for _name, _n in (("ident", P), ("ones", P), ("tri", P), ("tri_strict", P), ("mask_sl", P), ("mask_qk", P),
                  ("onehot", SSM_HEADS), ("bias_c", 2 * 16 * 16), ("valid_c", 2 * 16)):
    _cst(_name, _n)

G_BANKS = 3
RAW_SLOTS, HI_SLOTS, LO_SLOTS = 4, 4, 4
FINAL_DVE = 6
AHEAD = LO_SLOTS - 1


def lo_share(n):
    return 7 if UNITS[SPLIT_UNITS[n]][0] in ("x", "z") else 6


def build(nc, xT, par_in, cst_in, alibi_q, alibi_k, w_ada1, wpack, out):
    f32, f32r, bf16 = mybir.dt.float32, mybir.dt.float32r, mybir.dt.bfloat16
    ALU, ACT, AX = mybir.AluOpType, mybir.ActivationFunctionType, mybir.AxisListType

    cursor = [(nc.sbuf_base + 63) // 64 * 64]

    def place(name, shape, dt, at=None):
        size = (int(np.prod(shape[1:])) * (2 if dt == bf16 else 4) + 63) // 64 * 64
        off = cursor[0] if at is None else at
        if at is None:
            cursor[0] += size
        return nc.alloc_sbuf_tensor_at(name, shape, dt, offset=off)

    h_at = cursor[0]
    HH = place("h_hi", [P, KT, SEQ], f32r)
    HL = place("h_lo", [P, KT, SEQ], f32r)
    RAW = place("w_raw", [P, RAW_SLOTS, 1024], f32)
    WH = place("w_hi", [P, HI_SLOTS, 1024], f32r)
    WL = place("w_lo", [P, LO_SLOTS, 1024], f32r)
    PR = place("params", [P, PAR["end"][1]], f32)
    CS = place("consts", [P, CST["end"][1]], f32)
    IDB = place("ident_bf16", [P, P], bf16)
    MSL = place("mask_sl_bf16", [P, P], bf16)
    MQK = place("mask_qk_bf16", [P, P], bf16)
    CW = place("conv_half", [P, 120], f32)
    MOD = place("mod", [P, 16], f32)
    AB = place("ada_scale", [P, 16], f32)
    GG = place("gate_times_g", [P, 2, 8], f32)
    GATE = place("att_gate", [P, 2, ATT_HEADS, 3], f32)
    SM = place("softmax_small", [P, 2, 4, 4], f32)
    ys_at = cursor[0]
    F0 = place("dt_gate_T", [P, SEQ], f32)
    DTT = place("dt_gate_tok", [P, 2, P], f32)
    DT = place("dt", [P, 2, SSM_HEADS], f32)
    DTW = place("dt_work", [P, 6, 2, SSM_HEADS], f32)
    ADT4 = place("adt4", [P, 2, 4, SSM_HEADS], f32)
    HI4 = place("acs_hi", [P, 2, P], f32r)
    TP = place("acs_rows", [P, 2, P], f32)
    ST = place("acs_cols", [P, 2, P], f32r)
    ONZ = place("ones_then_zeros", [P, P], f32r)
    DS = place("decay_to_end", [P, SSM_HEADS], f32)
    AEX = place("exp_a_log", [P, SSM_HEADS], f32)
    HI4X = place("released", [1, 1], f32)
    assert cursor[0] - ys_at >= 8192, cursor[0] - ys_at
    YS = place("y_ssm_out", [P, 8, SEQ], f32, at=ys_at)
    z_at = cursor[0]
    Z = place("z_gate_then_y", [P, 16, SEQ], f32)
    YNH = place("ynorm_hi", [P, 16, SEQ], f32r, at=z_at)
    YNL = place("ynorm_lo", [P, 16, SEQ], f32r)
    ZA = place("z_att_then_o", [P, 8, SEQ], f32)
    q_at = cursor[0]
    QS = place("q_hi_lo", [P, ATT_HEADS, SEQ], f32r)
    KH = place("k_hi", [P, KV_GROUPS, 2, SEQ], f32r)
    KL = place("k_lo", [P, KV_GROUPS, 2, SEQ], f32r)
    V = place("v", [P, 2, 2, KV_GROUPS, HEAD_DIM], f32)
    over_at = cursor[0]
    kb = 1024
    assert over_at + 48 * kb <= 229344, over_at
    ADA = place("w_ada_shift_scale", [P, KT, 2048], f32, at=z_at)
    XT = place("x_T", [P, KT, SEQ], f32, at=over_at)
    SQX = place("x_sq", [P, KT, SEQ], f32, at=over_at + 8 * kb)
    RX = place("rstd_x", [P, 2, SEQ], f32, at=over_at + 16 * kb)
    ROWS = place("ada_rows", [P, 512], f32, at=over_at + 18 * kb)
    XG = place("x_conv_T", [P, 2, TPG, SEQ], f32, at=q_at)
    BTT = place("b_T", [P, 4, SEQ], f32, at=q_at + 8 * kb)
    CTT = place("c_T", [P, 4, SEQ], f32, at=q_at + 12 * kb)
    BTOK = place("b_tok", [P, 4, STATE], f32, at=q_at + 16 * kb)
    XDT = place("x_dt", [P, 2, HPC, HEAD_DIM], f32, at=q_at + 18 * kb)
    XDS = place("x_dt_decay", [P, HPC, HEAD_DIM], f32, at=q_at + 22 * kb)
    STA = place("state", [P, HPC * HEAD_DIM], f32, at=q_at + 24 * kb)
    CB = place("cb_T", [P, 4, 2, P], f32, at=q_at + 26 * kb)
    MV = place("seg_moving", [P, 2, 4, P], f32r, at=over_at)
    EX = place("decay", [P, 2, 4, P], f32, at=over_at + 4 * kb)
    MM = place("cb_decay", [P, 2, 4, P], f32, at=over_at + 8 * kb)
    EA = place("exp_acs", [P, 4, P], f32, at=over_at + 12 * kb)
    CE = place("c_exp_acs", [P, 4, P], f32, at=over_at + 14 * kb)
    SQ = place("y_sq", [P, 4, SEQ], f32, at=over_at + 16 * kb)
    YT = place("y_tmp", [P, 2, SEQ], f32, at=over_at + 20 * kb)
    RN = place("rstd_y", [P, 2, SEQ], f32, at=over_at + 22 * kb)
    BLK = place("cmp_blocks", [P, 2, 16, KV_GROUPS * N_CMP], f32, at=over_at + 24 * kb)
    KVC = place("kv_cmp_T", [P, 4, SEQ], f32, at=over_at + 32 * kb)
    HID = place("cmp_hidden", [P, 2, CMP_HIDDEN], f32, at=over_at + 36 * kb)
    HVR = place("hid_v_T", [P, 2, KV_GROUPS, 4, 32], f32, at=over_at + 38 * kb)
    ACC = place("conv_acc", [P, 2, SEQ], f32, at=over_at + 42 * kb)
    TH = place("tanh_tmp", [P, 2, SEQ], f32, at=over_at + 44 * kb)
    HIDK = place("hid_k_T", [P, 2, 60], f32, at=over_at + 46 * kb)
    KC = place("k_cmp_hi_lo", [P, KV_GROUPS, 32], f32r, at=over_at + 46 * kb + 512)
    MT = place("merge_tanh", [P, 16, SEQ], f32, at=over_at)
    CSW = place("cmp_scores", [P, 2, ATT_HEADS, 16], f32, at=ys_at + 4 * kb)
    CSM = place("cmp_small", [P, 3, 2, ATT_HEADS], f32, at=ys_at + 6 * kb)
    E = place("probs", [P, 2, 2, 384], f32, at=over_at + 16 * kb)
    PT = place("probs_T", [P, 2, 2, 384], f32, at=over_at + 22 * kb)
    PC = place("cmp_probs", [P, 2, ATT_HEADS, 32], f32, at=ys_at)
    PCT = place("cmp_probs_T", [P, KV_GROUPS, SEQ], f32, at=over_at + 28 * kb)
    VC = place("v_cmp", [P, KV_GROUPS, 2, P], f32, at=over_at + 32 * kb)
    ALQ = place("alibi_q", [P, ATT_HEADS * SEQ], bf16, at=over_at + 36 * kb)
    ALK = place("alibi_k", [P, 2, SEQ], bf16, at=over_at + 47 * kb)
    VT = place("v_T", [P, 2, SEQ], f32, at=over_at + 44 * kb)
    OH = place("o_hi", [P, 8, SEQ], f32r, at=h_at)
    OL = place("o_lo", [P, 8, SEQ], f32r, at=h_at + 8 * kb)
    MH = place("merged_hi", [P, 8, SEQ], f32r, at=z_at)
    ML = place("merged_lo", [P, 8, SEQ], f32r, at=z_at + 8 * kb)
    MTMP = place("merge_tmp", [P, 2, 2, SEQ], f32, at=over_at + 16 * kb)
    SQO = place("out_sq", [P, 2, SEQ], f32, at=over_at + 20 * kb)
    ROWS2 = place("ada_gate_rows", [P, 256], f32, at=ys_at + 6 * kb + 512)
    RF = place("rstd_out", [P, 2, SEQ], f32, at=over_at + 24 * kb)
    XR = place("x_residual", [P, 8, SEQ], f32, at=over_at + 28 * kb)
    OUT = place("out_T", [P, 8, SEQ], f32, at=q_at - 8 * kb)

    def par(name, lo=0, hi=None):
        a, b = PAR[name]
        return PR[:, a + lo:(b if hi is None else a + hi)]

    def cst(name, lo=0, hi=None):
        a, b = CST[name]
        return CS[:, a + lo:(b if hi is None else a + hi)]

    GB = [nc.alloc_psum_tensor(f"gemm{i}", [P, 512], f32) for i in range(G_BANKS)]
    SB = [nc.alloc_psum_tensor(f"score{i}", [P, 512], f32) for i in range(2)]
    TB = [nc.alloc_psum_tensor(f"small{i}", [P, 512], f32) for i in range(2)]
    YB = nc.alloc_psum_tensor("y_or_o", [P, 512], f32)
    sems = {}

    def sem(name):
        if name not in sems:
            sems[name] = nc.alloc_semaphore(name)
        return sems[name]

    ada_in = [sem(f"ada_in{k}") for k in range(KT)]
    w_in = [sem(f"w_in{r}") for r in range(RAW_SLOTS)]
    par_in_s, cst_in_s, cst2_in_s, x_in, al_in, al2_in, xr_in, out_done = map(
        sem, ("params_in", "consts_in", "consts2_in", "x_in", "alibi_in", "alibi2_in", "xr_in", "out_done"))
    hi_ready, lo_ready, lo_rest_ready, unit_mm, native_mm = map(
        sem, ("hi_ready", "lo_ready", "lo_rest_ready", "unit_mm", "native_mm"))
    t_full, t_free, s_full, s_free = ([sem(f"{n}{b}") for b in range(2)] for n in ("t_full", "t_free", "s_full", "s_free"))
    g_free = [sem(f"g_free{b}") for b in range(G_BANKS)]
    y_full, y_free = sem("y_full"), sem("y_free")
    consts_made, zeros = sem("consts_made"), sem("zeros")
    cw_ready, sqx_done, ssx_full, varx_done, rx_done, ada_full, rows_done, modT_full, h_f32, h_hi, h_ready = map(
        sem, ("cw_ready", "sqx", "ssx_full", "varx", "rx", "ada_full", "rows", "modT_full", "h_f32", "h_hi_done", "h_ready"))
    abs_done, dt_exp, dt_u, dt_ln, dt_inv, a_exp, gate_tanh, adt_done, hi4_done, cols_ready = map(
        sem, ("abs", "dt_exp", "dt_u", "dt_ln", "dt_inv", "a_exp", "gate_tanh", "adt", "hi4", "cols_ready"))
    conv_acc, th_full, gated = map(sem, ("conv_acc_s", "th_full", "gated"))
    xds_done, mv_done, ce_done, ypre_done, ysq_done, rn_done, ynf_done, ynh_done, yn_done = map(
        sem, ("xds", "mv", "ce", "ypre", "ysq", "rn", "ynf", "ynh", "yn"))
    mm_done = [sem("mm0"), sem("mm1")]
    blk_done = [sem("blk0"), sem("blk1")]
    kch_done, kh_done, qh_done, cs_sub, cs_exp, pc_done, max_done, p_done, oh_done, o_split = map(
        sem, ("kch", "kh", "qh", "cs_sub", "cs_exp", "pc", "max", "p", "oh", "o_split"))
    rows2_done, gg_done, mf_done, mh_done, ml_done, osq_full, varf_done, rf_done = map(
        sem, ("rows2", "gg", "mf", "mh", "ml", "osq_full", "varf", "rf"))
    fin_done = [sem("fin_vector"), sem("fin_gpsimd")]
    dve_seq, act_seq, pool_seq = sem("dve_seq"), sem("act_seq"), sem("pool_seq")

    def conv_index(kind, j):
        return {"b": j, "c": 4 + j, "x": 8 + j}[kind]

    def conv_src(kind, j):
        return {"x": j, "b": 16 + j, "c": 20 + j}[kind]

    def conv_dst(kind, j):
        return {"b": BTT, "c": CTT}[kind][:, j, :] if kind != "x" else XG[:, (j // TPG) % 2, j % TPG, :]

    zeroed = ["rows", "hid_v", "v_cmp", "k_cmp", "p_cmp", "rows2", "alibi"]

    def wait_zeros(eng, name):
        eng.wait_ge(zeros, zeroed.index(name) + 1)

    def wait_small_full(eng, key):
        eng.wait_ge(t_full[T_IDX[key] % 2], T_IDX[key] // 2 + 1)

    def wait_small_out(eng, key):
        eng.wait_ge(t_free[T_IDX[key] % 2], T_IDX[key] // 2 + 1)

    def wait_tile_full(eng, tile):
        u = UNITS.index(tile + (LAST_PART.get(tile[0], 0),))
        if u in SPLIT_IDX:
            eng.wait_ge(unit_mm, SPLIT_IDX[u] + 1)
        else:
            eng.wait_ge(native_mm, NATIVE_IDX[u] + 1)

    out_count = {}
    for tile in TILE_IDX:
        if tile[0] not in ("z", "za", "w1k", "w1v"):
            b = TILE_IDX[tile] % G_BANKS
            out_count[tile] = sum(1 for other in out_count if TILE_IDX[other] % G_BANKS == b) + 1

    def wait_tile_out(eng, tile):
        if tile in out_count:
            eng.wait_ge(g_free[TILE_IDX[tile] % G_BANKS], out_count[tile])
        else:
            eng.wait_ge(gated, TH_IDX[tile] + 1)

    def wait_y_full(eng, key):
        eng.wait_ge(y_full, Y_IDX[key] + 1)

    def wait_y_out(eng, key):
        eng.wait_ge(y_free, Y_IDX[key] + 1)

    def finished_tile(u):
        kind, j, part = UNITS[u]
        return (kind, j) if part == LAST_PART.get(kind, 0) else None

    def compress_blocks(eng, e, b):
        wait_tile_out(eng, ("vc" if b else "kc", 0))
        wait_tile_out(eng, ("vc" if b else "kc", 1))
        pos = PAR["pos_v" if b else "pos_k"][0]
        for g in range(KV_GROUPS):
            rows = slice(64 * (g % 2), 64 * (g % 2) + 64)
            kv = KVC[rows, 2 * b + g // 2, :].rearrange("p (j r n) -> p n r j", r=8, n=2)
            for n in range(2):
                for half in range(2):
                    r = PR[rows, pos + 16 * half + n:pos + 16 * half + 16:2].unsqueeze(2).to_broadcast([64, 8, N_CMP])
                    e.tensor_tensor(BLK[64 * n:64 * n + 64, b, 8 * half:8 * half + 8, N_CMP * g:N_CMP * (g + 1)],
                                    kv[:, n, :, half:half + N_CMP], r, ALU.add).then_inc(blk_done[b], 1)
                    if b:
                        eng.wait_ge(blk_done[b], 4 * g + 2 * n + half + 1)

    with nc.Block() as block:

        @block.sync
        def _(sp):
            early = 2 * P
            sp.dma_start(PR[:], par_in).then_inc(par_in_s, 16)
            sp.dma_start(CS[:, 0:early], cst_in[:, 0:early]).then_inc(cst_in_s, 16)
            for k in range(KT):
                sp.dma_start(ADA[:, k, :], w_ada1[:, k, :]).then_inc(ada_in[k], 16)
                if k == 1:
                    sp.dma_start(XT[:], xT).then_inc(x_in, 16)
                if k == KT - 2:
                    sp.dma_start(RAW[:, 0, :], wpack[0]).then_inc(w_in[0], 16)
            sp.dma_start(RAW[:, 1, :], wpack[1]).then_inc(w_in[1], 16)
            sp.dma_start(CS[:, early:CST["end"][1]], cst_in[:, early:CST["end"][1]]).then_inc(cst2_in_s, 16)
            for u in range(2, len(UNITS)):
                if u >= RAW_SLOTS:
                    v = u - RAW_SLOTS
                    if v in SPLIT_IDX:
                        sp.wait_ge(lo_ready, SPLIT_IDX[v] + 1)
                        sp.wait_ge(lo_rest_ready, SPLIT_IDX[v] + 1)
                    else:
                        sp.wait_ge(native_mm, NATIVE_IDX[v] + 1)
                sp.dma_start(RAW[:, u % RAW_SLOTS, :], wpack[u]).then_inc(w_in[u % RAW_SLOTS], 16)
                if u == UNITS.index(("q", 0, 0)):
                    wait_small_full(sp, ("vcp", 0, 0))
                    wait_zeros(sp, "alibi")
                    sp.dma_start(ALQ[0:6].bitcast(mybir.dt.uint16), alibi_q).then_inc(al_in, 16)
                    sp.dma_start(ALK[0:6].bitcast(mybir.dt.uint16), alibi_k).then_inc(al2_in, 16)
                if u == UNITS.index(("out", 0, 0)):
                    wait_y_out(sp, ("pv", 7))
                    sp.dma_start(XR[:], xT).then_inc(xr_in, 16)
            for m, (who, value) in ((6, (1, 1)), (0, (0, 1)), (2, (0, 2)), (4, (0, 3))):
                sp.wait_ge(fin_done[who], value)
                sp.dma_start(out[:, m:m + 2, :], OUT[:, m:m + 2, :]).then_inc(out_done, 16)
            sp.wait_ge(out_done, 4 * 16)

        @block.tensor
        def _(pe):
            ident = cst("ident")
            pe.wait_ge(cst_in_s, 16)
            pe.wait_ge(sqx_done, 1)
            for k in range(KT):
                last = nc.tensor.matmul(YB[:, 0:SEQ], cst("ones"), SQX[:, k, :], start=(k == 0), stop=(k == KT - 1))
            last.then_inc(ssx_full, 1)
            pe.wait_ge(par_in_s, 16)
            for k in range(KT):
                pe.wait_ge(ada_in[k], 16)
                for j in range(4):
                    last = nc.tensor.matmul(SB[0][32 * j:32 * j + 1, :], par("c", k, k + 1), ADA[:, k, 512 * j:512 * j + 512],
                                            start=(k == 0), stop=(k == KT - 1))
            last.then_inc(ada_full, 1)
            pe.wait_ge(rows_done, 4)
            wait_zeros(pe, "rows")
            for m in range(4):
                last = nc.tensor.transpose(SB[1][:, P * m:P * m + P], ROWS[:, P * m:P * m + P], ident)
            last.then_inc(modT_full, 1)

            def begin_small(key):
                n = T_IDX[key]
                if n >= 2:
                    pe.wait_ge(t_free[n % 2], n // 2)
                return TB[n % 2]

            def end_small(ins, key):
                ins.then_inc(t_full[T_IDX[key] % 2], 1)

            tiles = list(TILE_IDX)

            def weight_unit(u):
                kind, j, part = UNITS[u]
                if kind == "ag":
                    if part == 0:
                        wait_y_out(pe, ("y", 7))
                    pe.wait_ge(w_in[u % RAW_SLOTS], 16 * (u // RAW_SLOTS + 1))
                    for q in range(4):
                        last = nc.tensor.matmul(YB[32 * q:32 * q + 1, 0:256], par("c", part, part + 1),
                                                RAW[:, u % RAW_SLOTS, 256 * q:256 * q + 256], start=(part == 0), stop=(part == KT - 1))
                    last.then_inc(native_mm, 1)
                    return
                tile = TILE_IDX[(kind, j)]
                bank = GB[tile % G_BANKS]
                if part == 0 and tile >= G_BANKS:
                    wait_tile_out(pe, tiles[tile - G_BANKS])
                raw = RAW[:, u % RAW_SLOTS, :]
                if kind in NATIVE:
                    b = 0 if kind == "w1k" else 1
                    pe.wait_ge(w_in[u % RAW_SLOTS], 16 * (u // RAW_SLOTS + 1))
                    if part == 0:
                        pe.wait_ge(blk_done[b], 16)
                    for r in range(4):
                        last = nc.tensor.matmul(bank[0:60, 0:CMP_HIDDEN], BLK[:, b, 4 * part + r, :],
                                                raw[:, CMP_HIDDEN * r:CMP_HIDDEN * (r + 1)],
                                                start=(part == 0 and r == 0), stop=(part == 3 and r == 3))
                    last.then_inc(native_mm, 1)
                    return
                n = SPLIT_IDX[u]
                if kind == "ssm":
                    hi, lo, k0, parts = YNH, YNL, 8 * part, 2
                    if j == 0:
                        pe.wait_ge(yn_done, 8 * (part + 1))
                elif kind == "nsa":
                    hi, lo, k0, parts = OH, OL, 0, 1
                elif kind == "out":
                    hi, lo, k0, parts = MH, ML, 0, 1
                else:
                    hi, lo, k0, parts = HH, HL, 0, 1
                pe.wait_ge(hi_ready, n + 1)
                pe.wait_ge(lo_ready, n + 1)
                for k in range(KT):
                    if k == lo_share(n):
                        pe.wait_ge(lo_rest_ready, n + 1)
                    if u == 0:
                        pe.wait_ge(h_ready, k + 1)
                    if kind == "nsa" and j == 0:
                        pe.wait_ge(o_split, k + 1)
                    if kind == "out" and j == 0:
                        pe.wait_ge(ml_done, k + 1)
                    w_hi = WH[:, n % HI_SLOTS, P * k:P * k + P]
                    w_lo = WL[:, n % LO_SLOTS, P * k:P * k + P]
                    first, end = (k == 0 and part == 0), (k == KT - 1 and part == parts - 1)
                    nc.tensor.matmul(bank[:, 0:SEQ], w_hi, hi[:, k0 + k, :], start=first, stop=False)
                    nc.tensor.matmul(bank[:, 0:SEQ], w_hi, lo[:, k0 + k, :], start=False, stop=False)
                    last = nc.tensor.matmul(bank[:, 0:SEQ], w_lo, hi[:, k0 + k, :], start=False, stop=end)
                last.then_inc(unit_mm, 1)

            for step in STEPS:
                what, i = step
                if what == "gemm":
                    weight_unit(i)
                elif what == "dtT":
                    key = step + (0,)
                    bank = begin_small(key)
                    wait_tile_out(pe, ("dtg", 0))
                    for c in range(2):
                        last = nc.tensor.transpose(bank[:, P * c:P * c + P], F0[:, P * c:P * c + P], ident)
                    end_small(last, key)
                elif what == "acs":
                    key = step + (0,)
                    bank = begin_small(key)
                    pe.wait_ge(adt_done, 2)
                    pe.wait_ge(cst2_in_s, 16)
                    for c in range(2):
                        nc.tensor.matmul(bank[:, P * c:P * c + P], ADT4[:, c, :, :].rearrange("p r h -> p (r h)"),
                                         cst("tri"), start=True, stop=True)
                    last = nc.tensor.matmul(bank[:, 256:256 + SSM_HEADS], cst("tri_strict"), ADT4[:, 0, 0, :],
                                            start=True, stop=True)
                    end_small(last, key)
                elif what == "bt":
                    key = step + (0,)
                    bank = begin_small(key)
                    pe.wait_ge(gated, TH_IDX[("b", 3)] + 1)
                    for g in range(4):
                        last = nc.tensor.transpose(bank[:, P * g:P * g + P], BTT[:, g, 0:CHUNK], ident)
                    end_small(last, key)
                elif what == "cb":
                    key = step + (0,)
                    bank = begin_small(key)
                    pe.wait_ge(gated, TH_IDX[("c", 3)] + 1)
                    for gg in range(2):
                        for c in range(2):
                            o = P * (2 * gg + c)
                            last = nc.tensor.matmul(bank[:, o:o + P], BTT[:, 2 * i + gg, CHUNK * c:CHUNK * (c + 1)],
                                                    CTT[:, 2 * i + gg, CHUNK * c:CHUNK * (c + 1)], start=True, stop=True)
                    end_small(last, key)
                elif what == "xt":
                    g, c = i
                    key = step + (0,)
                    bank = begin_small(key)
                    pe.wait_ge(gated, TH_IDX[("x", TPG * g + 3)] + 1)
                    for t in range(TPG):
                        last = nc.tensor.transpose(bank[:, P * t:P * t + P], XG[:, g % 2, t, CHUNK * c:CHUNK * (c + 1)], ident)
                    end_small(last, key)
                elif what == "st":
                    key = step + (0,)
                    bank = begin_small(key)
                    pe.wait_ge(xds_done, i + 1)
                    wait_small_out(pe, ("bt", 0, 0))
                    last = nc.tensor.matmul(bank[:, :], BTOK[:, i, :], XDS[:, :, :].rearrange("p h d -> p (h d)"),
                                            start=True, stop=True)
                    end_small(last, key)
                elif what == "seg":
                    n = S_IDX[step]
                    for c in range(2):
                        if n >= 1:
                            pe.wait_ge(s_free[c], n)
                        if i == 0 and c == 0:
                            pe.wait_ge(cols_ready, 4)
                            pe.wait_ge(consts_made, 7)
                        pe.wait_ge(mv_done, 2 * i + c + 1)
                        mv = MV[:, c, :, :].rearrange("p j l -> p (j l)")
                        nc.tensor.matmul(SB[c][:, :], ST[:, c, :], mv, start=True, stop=False)
                        last = nc.tensor.matmul(SB[c][:, :], IDB[:], MSL[:].unsqueeze(1).to_broadcast([P, 4, P]),
                                                start=False, stop=True)
                        last.then_inc(s_full[c], 1)
                elif what == "ea":
                    key = step + (0,)
                    bank = begin_small(key)
                    last = nc.tensor.matmul(bank[:, :], ONZ[:], MV[:, 1, :, :].rearrange("p j l -> p (j l)"),
                                            start=True, stop=True)
                    end_small(last, key)
                elif what == "y":
                    n, g = Y_IDX[step], i // 2
                    if n >= 1:
                        pe.wait_ge(y_free, n)
                    pe.wait_ge(mm_done[0], i + 1)
                    pe.wait_ge(mm_done[1], i + 1)
                    pe.wait_ge(ce_done, i + 1)
                    wait_small_out(pe, ("st", g, 0))
                    wait_small_out(pe, ("xt", (g, 1), 0))
                    for t in range(2):
                        bank = YB[:, SEQ * t:SEQ * (t + 1)]
                        heads = [(k, 2 * t + k, 4 * (i % 2) + 2 * t + k) for k in range(2)]
                        for c in range(2):
                            for k, q4, h in heads:
                                nc.tensor.matmul(bank[64 * k:64 * k + 64, CHUNK * c:CHUNK * (c + 1)], XDT[:, c, h, :],
                                                 MM[:, c, q4, :], start=True, stop=(c == 0))
                        for k, q4, h in heads:
                            last = nc.tensor.matmul(bank[64 * k:64 * k + 64, CHUNK:SEQ], STA[:, HEAD_DIM * h:HEAD_DIM * (h + 1)],
                                                    CE[:, q4, :], start=False, stop=True)
                    last.then_inc(y_full, 1)
                elif what == "ssq":
                    key = step + (0,)
                    bank = begin_small(key)
                    pe.wait_ge(ysq_done, i + 1)
                    for t in range(TPG):
                        last = nc.tensor.matmul(bank[:, 0:SEQ], cst("ones"), SQ[:, t, :], start=(t == 0), stop=(t == TPG - 1))
                    end_small(last, key)
                elif what == "hidT":
                    key = step + (0,)
                    bank = begin_small(key)
                    pe.wait_ge(gated, TH_IDX[("w1v" if i else "w1k", 0)] + 1)
                    for k in range(2):
                        last = nc.tensor.transpose(bank[:, 60 * k:60 * k + 60], HID[0:60, i, P * k:P * k + P],
                                                   CS[0:60, CST["ident"][0]:CST["ident"][0] + 60])
                    end_small(last, key)
                elif what == "kcp":
                    key = step + (0,)
                    bank = begin_small(key)
                    wait_small_out(pe, ("hidT", 0, 0))
                    for k in range(2):
                        last = nc.tensor.matmul(bank[:, 0:60], par("w2k", P * k, P * k + P), HIDK[:, k, :],
                                                start=(k == 0), stop=(k == 1))
                    end_small(last, key)
                elif what == "vcp":
                    key = step + (0,)
                    bank = begin_small(key)
                    wait_small_out(pe, ("hidT", 1, 0))
                    for g in range(KV_GROUPS):
                        for k in range(2):
                            last = nc.tensor.matmul(bank[:, 64 * g:64 * g + 64], HVR[:, k, g, :, :].rearrange("p a b -> p (a b)"),
                                                    par("w2v", 64 * k, 64 * k + 64), start=(k == 0), stop=(k == 1))
                    end_small(last, key)
                elif what == "vt":
                    key = step + (0,)
                    bank = begin_small(key)
                    wait_tile_out(pe, ("vw" if i else "vs", 0))
                    wait_tile_out(pe, ("vw" if i else "vs", 1))
                    for kt in range(2):
                        for j in range(2):
                            o = P * (2 * kt + j)
                            last = nc.tensor.transpose(bank[:, o:o + P], VT[:, j, P * kt:P * kt + P], ident)
                    end_small(last, key)
                elif what == "cs":
                    key = step + (0,)
                    bank = begin_small(key)
                    for j in (6, 7):
                        wait_tile_out(pe, ("q", j))
                    wait_zeros(pe, "k_cmp")
                    wait_small_out(pe, ("kcp", 0, 0))
                    for h in range(ATT_HEADS):
                        last = nc.tensor.matmul(bank[:, 32 * h:32 * h + 32], QS[:, h, P * i:P * i + P], KC[:, h // HPG, :],
                                                start=True, stop=True)
                    end_small(last, key)
                elif what == "ct":
                    key = step + (0,)
                    bank = begin_small(key)
                    pe.wait_ge(pc_done, 1)
                    for gg in range(2):
                        for qt in range(2):
                            src = PC[:, qt, 4 * (2 * i + gg):4 * (2 * i + gg) + 4, :].rearrange("p h j -> p (h j)")
                            o = 256 * gg + P * qt
                            last = nc.tensor.transpose(bank[:, o:o + P], src, ident)
                    end_small(last, key)
                elif what == "sc":
                    n = S_IDX[step]
                    if i == 0:
                        for tile in (("ks", 0), ("ks", 1), ("kw", 0), ("kw", 1)):
                            wait_tile_out(pe, tile)
                        pe.wait_ge(al_in, 16)
                        pe.wait_ge(al2_in, 16)
                    for qt in range(2):
                        pe.wait_ge(s_free[qt], n)
                        nk = P * (qt + 1)
                        o = SB[qt][:, 0:2 * nk].rearrange("p (b k) -> p b k", b=2)
                        q = QS[:, i, P * qt:P * qt + P]
                        nc.tensor.matmul(o, q, KH[:, i // HPG, :, 0:nk], start=True, stop=False)
                        nc.tensor.matmul(o, q, KL[:, i // HPG, :, 0:nk], start=False, stop=False)
                        nc.tensor.matmul(o, ALQ[:, SEQ * i + P * qt:SEQ * i + P * qt + P], ALK[:, :, 0:nk], start=False, stop=False)
                        last = nc.tensor.matmul(o[:, :, P * qt:nk], IDB[:], MQK[:].unsqueeze(1).to_broadcast([P, 2, P]),
                                                start=False, stop=True)
                        last.then_inc(s_full[qt], 1)
                elif what == "pt":
                    pe.wait_ge(p_done, 4 * (i + 1))
                    e = E[:, i % 2, :, :]
                    key = step + (0,)
                    bank = begin_small(key)
                    for b in range(2):
                        nc.tensor.transpose(bank[:, 256 * b:256 * b + P], e[:, b, 0:P], ident)
                        last = nc.tensor.transpose(bank[:, 256 * b + P:256 * b + 256], e[:, b, P:2 * P], ident)
                    end_small(last, key)
                    key = step + (1,)
                    bank = begin_small(key)
                    for b in range(2):
                        last = nc.tensor.transpose(bank[:, P * b:P * b + P], e[:, b, 2 * P:3 * P], ident)
                    end_small(last, key)
                elif what == "pv":
                    n, bank = Y_IDX[step], YB
                    pe.wait_ge(y_free, n)
                    g = (2 * i) // HPG
                    if i == 0:
                        pe.wait_ge(rows2_done, 4)
                        wait_small_out(pe, ("ct", 0, 0))
                        wait_small_out(pe, ("ct", 1, 0))
                    for h in (2 * i, 2 * i + 1):
                        wait_small_out(pe, ("pt", h, 0))
                        wait_small_out(pe, ("pt", h, 1))
                    nc.tensor.matmul(bank[:, 0:SEQ], VC[:, g, i % 2, :], PCT[:, g, :], start=True, stop=False,
                                     skip_group_check=True)
                    for b in range(2):
                        for kt in range(2):
                            for k in range(2):
                                src = PT[:, k, b, 0:SEQ] if kt == 0 else PT[:, k, b, SEQ:SEQ + P]
                                last = nc.tensor.matmul(bank[64 * k:64 * k + 64, P * kt:SEQ], V[:, b, kt, g, :], src,
                                                        start=False, stop=(b == 1 and kt == 1), skip_group_check=True)
                    last.then_inc(y_full, 1)
                elif what == "agT":
                    key = step + (0,)
                    bank = begin_small(key)
                    pe.wait_ge(rows2_done, 4)
                    for m in range(2):
                        last = nc.tensor.transpose(bank[:, P * m:P * m + P], ROWS2[:, P * m:P * m + P], ident)
                    end_small(last, key)
                elif what == "osq":
                    if i == 0:
                        wait_y_out(pe, ("pv", 7))
                    wait_tile_out(pe, ("out", i))
                    last = nc.tensor.matmul(YB[:, 0:SEQ], cst("ones"), SQO[:, i % 2, :], start=(i == 0), stop=(i == 7))
                    last.then_inc(osq_full, 1)

        @block.scalar
        def _(act):
            def split_hi(n):
                u = SPLIT_UNITS[n]
                act.wait_ge(w_in[u % RAW_SLOTS], 16 * (u // RAW_SLOTS + 1))
                if n >= HI_SLOTS:
                    act.wait_ge(unit_mm, n - HI_SLOTS + 1)
                nc.scalar.copy(WH[:, n % HI_SLOTS, :], RAW[:, u % RAW_SLOTS, :]).then_inc(hi_ready, 1)

            def tanh_half(tile, src, rows=P):
                k = TH_IDX[tile]
                if k >= 2:
                    act.wait_ge(gated, k - 1)
                nc.scalar.activation(TH[0:rows, k % 2, :], src, ACT.Tanh, scale=0.5).then_inc(th_full, 1)

            pending = []

            def read_out(tile):
                if tile is None:
                    return
                kind, j = tile
                t = TILE_IDX[tile]
                bank = GB[t % G_BANKS][:, 0:SEQ]
                wait_tile_full(act, tile)
                if kind in CONV:
                    ci, col = conv_index(kind, j), conv_src(kind, j)
                    if ci >= 2:
                        act.wait_ge(gated, max(v for k, v in TH_IDX.items() if k[0] in CONV and conv_index(*k) == ci - 2) + 1)
                    nc.scalar.activation(ACC[:, ci % 2, :], bank, ACT.Identity, bias=CW[:, 96 + col:97 + col],
                                         scale=CW[:, 4 * col + 3:4 * col + 4]).then_inc(conv_acc, 1)
                if pending:
                    prev = pending.pop()
                    ci = conv_index(*prev)
                    wait_tile_out(act, prev)
                    k = TH_IDX[prev]
                    if k >= 2:
                        act.wait_ge(gated, k - 1)
                    nc.scalar.activation(TH[:, k % 2, :], ACC[:, ci % 2, :], ACT.Tanh).then_inc(th_full, 1)
                if kind in CONV:
                    pending.append(tile)
                elif kind == "dtg":
                    nc.scalar.activation(F0[:], bank, ACT.Identity, bias=par("dt_bias")).then_inc(g_free[t % G_BANKS], 1)
                elif kind in ("z", "za"):
                    tanh_half(tile, bank)
                elif kind in NATIVE:
                    tanh_half(tile, GB[t % G_BANKS][0:60, 0:CMP_HIDDEN], 60)
                elif kind in ("kc", "vc"):
                    nc.scalar.copy(KVC[:, j + 2 * (kind == "vc"), :], bank).then_inc(g_free[t % G_BANKS], 1)
                elif kind in ("vs", "vw"):
                    if kind == "vw":
                        wait_small_full(act, ("vt", 0, 0))
                    else:
                        wait_tile_out(act, ("w1v", 0))
                    nc.scalar.copy(VT[:, j, :], bank).then_inc(g_free[t % G_BANKS], 1)
                elif kind in ("ks", "kw"):
                    for half in range(2):
                        for dup in range(2):
                            nc.scalar.copy(KH[64 * dup:64 * dup + 64, 2 * j + half, int(kind == "kw"), :],
                                           GB[t % G_BANKS][64 * half:64 * half + 64, 0:SEQ]).then_inc(kh_done, 1)
                elif kind == "q":
                    for half in range(2):
                        nc.scalar.mul(QS[0:64, 2 * j + half, :], GB[t % G_BANKS][64 * half:64 * half + 64, 0:SEQ],
                                      HEAD_DIM ** -0.5).then_inc(qh_done, 1)
                elif kind == "mg":
                    nc.scalar.activation(MT[:, j, :], bank, ACT.Tanh, scale=0.5).then_inc(g_free[t % G_BANKS], 1)
                elif kind == "nsa":
                    act.wait_ge(mf_done, j + 1)
                    nc.scalar.copy(MH[:, j, :], MTMP[:, j % 2, 1, :]).then_inc(mh_done, 1)
                elif kind == "out":
                    act.wait_ge(gg_done, 1)
                    nc.scalar.mul(OUT[:, j, :], bank, GG[:, 1, j:j + 1])
                    if j >= 2:
                        act.wait_ge(osq_full, j - 1)
                    nc.scalar.activation(SQO[:, j % 2, :], bank, ACT.Square).then_inc(g_free[t % G_BANKS], 1)

            act.wait_ge(x_in, 16)
            nc.scalar.activation(SQX[:], XT[:], ACT.Square).then_inc(sqx_done, 1)
            act.wait_ge(par_in_s, 16)
            nc.scalar.activation(AEX[:], par("a_log"), ACT.Exp).then_inc(a_exp, 1)
            act.wait_ge(varx_done, 1)
            nc.scalar.activation(RX[:, 0, :], RX[:, 0, :], ACT.Sqrt).then_inc(rx_done, 1)
            split_hi(0)
            wait_zeros(act, "rows")
            act.wait_ge(ada_full, 1)
            for j in range(4):
                nc.scalar.copy(ROWS[32 * j:32 * j + 1, :], SB[0][32 * j:32 * j + 1, :]).then_inc(rows_done, 1)
            for k in range(KT):
                act.wait_ge(h_f32, k + 1)
                nc.scalar.copy(HH[:, k, :], XT[:, k, :]).then_inc(h_hi, 1)
            for n in range(1, AHEAD):
                split_hi(n)
            act.wait_ge(cw_ready, 1)

            done = None
            for step in LATE_STEPS:
                what, i = step
                key = step + (0,)
                bank = TB[T_IDX[key] % 2] if key in T_IDX else None
                release = t_free[T_IDX[key] % 2] if key in T_IDX else None
                if what == "gemm":
                    read_out(done)
                    done = finished_tile(i)
                    if i + AHEAD in SPLIT_IDX:
                        split_hi(SPLIT_IDX[i + AHEAD])
                elif what == "flush":
                    read_out(done)
                elif what == "dtT":
                    wait_small_full(act, key)
                    nc.scalar.copy(DTT[:], bank[:, 0:2 * P].rearrange("p (c f) -> p c f", c=2)).then_inc(release, 1)
                    wait_small_out(act, key)
                    nc.scalar.activation(GATE[:], DTT[:, :, GATE_ROW:GATE_ROW + 48].rearrange("p c (h n) -> p c h n", n=3),
                                         ACT.Tanh, scale=0.5).then_inc(gate_tanh, 1)
                elif what == "dtE":
                    act.wait_ge(abs_done, 1)
                    nc.scalar.activation(DTW[:, 2], DTW[:, 0], ACT.Exp, scale=-1.0).then_inc(dt_exp, 1)
                elif what == "dtL":
                    act.wait_ge(dt_u, 1)
                    nc.scalar.activation(DTW[:, 4], DTW[:, 3], ACT.Ln).then_inc(dt_ln, 1)
                    act.wait_ge(dt_ln, 1)
                    nc.scalar.activation(DTW[:, 5], DTW[:, 4], ACT.Exp, scale=-1.0).then_inc(dt_inv, 1)
                elif what == "acs":
                    wait_small_full(act, key)
                    nc.scalar.activation(DS[:], bank[:, 256:256 + SSM_HEADS], ACT.Exp)
                    nc.scalar.copy(HI4[:], bank[:, 0:2 * P].rearrange("p (c l) -> p c l", c=2)).then_inc(hi4_done, 1)
                elif what == "bt":
                    wait_small_full(act, key)
                    nc.scalar.copy(BTOK[:].rearrange("p g n -> p (g n)"), bank[:, :]).then_inc(release, 1)
                elif what == "cb":
                    wait_small_full(act, key)
                    nc.scalar.copy(CB[:, 2 * i:2 * i + 2, :, :].rearrange("p g c l -> p (g c l)"), bank[:, :]).then_inc(release, 1)
                elif what == "st":
                    wait_small_full(act, key)
                    if i >= 1:
                        wait_y_full(act, ("y", 2 * i - 1))
                    nc.scalar.copy(STA[:], bank[:, :]).then_inc(release, 1)
                elif what == "seg":
                    n = S_IDX[step]
                    for c in range(2):
                        act.wait_ge(s_full[c], n + 1)
                        if i >= 1:
                            act.wait_ge(mm_done[c], i)
                        nc.scalar.activation(EX[:, c, :, :].rearrange("p j l -> p (j l)"), SB[c][:, :],
                                             ACT.Exp).then_inc(s_free[c], 1)
                elif what == "ea":
                    wait_small_full(act, key)
                    if i >= 1:
                        act.wait_ge(ce_done, i)
                    nc.scalar.activation(EA[:].rearrange("p j l -> p (j l)"), bank[:, :], ACT.Exp).then_inc(release, 1)
                elif what == "ysq":
                    act.wait_ge(ypre_done, 2 * (i + 1))
                    if i >= 1:
                        wait_small_full(act, ("ssq", i - 1, 0))
                    nc.scalar.activation(SQ[:], Z[:, TPG * i:TPG * (i + 1), :], ACT.Square).then_inc(ysq_done, 1)
                elif what == "ssq":
                    wait_small_out(act, key)
                    nc.scalar.activation(RN[:, 0, :], RN[:, 0, :], ACT.Sqrt).then_inc(rn_done, 1)
                elif what == "ynhi":
                    act.wait_ge(ynf_done, i + 1)
                    nc.scalar.copy(YNH[:, i, :], YT[:, i % 2, :]).then_inc(ynh_done, 1)
                elif what == "hidT":
                    wait_small_full(act, key)
                    if i == 0:
                        nc.scalar.mul(HIDK[:].rearrange("p k n -> p (k n)"), bank[:, 0:120], 0.5).then_inc(release, 1)
                    else:
                        wait_zeros(act, "hid_v")
                        for k in range(2):
                            src = bank[:, 60 * k:60 * k + 60].rearrange("p (g j) -> p g j", g=KV_GROUPS).unsqueeze(2)
                            last = nc.scalar.mul(HVR[:, k, :, :, 0:N_CMP], src.to_broadcast([P, KV_GROUPS, 4, N_CMP]), 0.5)
                        last.then_inc(release, 1)
                elif what == "kcp":
                    wait_small_full(act, key)
                    wait_zeros(act, "k_cmp")
                    nc.scalar.copy(KC[:, :, 0:N_CMP], bank[:, 0:60].rearrange("p (g j) -> p g j", g=KV_GROUPS)).then_inc(kch_done, 1)
                elif what == "vcp":
                    wait_small_full(act, key)
                    wait_zeros(act, "v_cmp")
                    for hh in range(4):
                        rows = slice(32 * hh, 32 * hh + 32)
                        last = nc.scalar.copy(VC[rows, :, hh // 2, 64 * (hh % 2):64 * (hh % 2) + 64],
                                              bank[rows, 0:256].rearrange("p (g d) -> p g d", g=KV_GROUPS))
                    last.then_inc(release, 1)
                elif what == "vt":
                    wait_small_full(act, key)
                    nc.scalar.copy(V[:, i, :, :, :].rearrange("p k g d -> p (k g d)"), bank[:, :]).then_inc(release, 1)
                elif what == "cs" and i == 1:
                    act.wait_ge(cs_sub, 1)
                    nc.scalar.activation(CSW[:], CSW[:], ACT.Exp).then_inc(cs_exp, 1)
                elif what == "ct":
                    wait_small_full(act, key)
                    nc.scalar.copy(PCT[:, 2 * i:2 * i + 2, :].rearrange("p g q -> p (g q)"), bank[:, :]).then_inc(release, 1)
                elif what == "ex":
                    n, k = S_IDX[("sc", i)], i % 2
                    if i >= 2:
                        wait_small_full(act, ("pt", i - 2, 1))
                    for qt in range(2):
                        act.wait_ge(max_done, 2 * i + qt + 1)
                        nk = P * (qt + 1)
                        for b in range(2):
                            c = 2 * qt + b
                            last = nc.scalar.activation(E[:, k, b, P * qt:P * qt + nk], SB[qt][:, nk * b:nk * b + nk], ACT.Exp,
                                                        bias=SM[:, k, 0, c:c + 1], accum_out=SM[:, k, 1, c:c + 1])
                        last.then_inc(s_free[qt], 1)
                elif what == "pt":
                    wait_small_full(act, key)
                    if i >= 2:
                        wait_y_full(act, ("pv", i // 2 - 1))
                    nc.scalar.copy(PT[:, i % 2, :, 0:SEQ], bank[:, :].rearrange("p (b q) -> p b q", b=2)).then_inc(release, 1)
                elif what == "osp":
                    wait_y_out(act, ("pv", i))
                    nc.scalar.copy(OH[:, i, :], ZA[:, i, :]).then_inc(oh_done, 1)
                elif what == "agR":
                    wait_zeros(act, "rows2")
                    act.wait_ge(native_mm, NATIVE_IDX[UNITS.index(("ag", 0, KT - 1))] + 1)
                    for j in range(4):
                        nc.scalar.copy(ROWS2[32 * j:32 * j + 1, :], YB[32 * j:32 * j + 1, 0:256]).then_inc(rows2_done, 1)
            act.wait_ge(varf_done, 1)
            nc.scalar.activation(RF[:, 0, :], RF[:, 0, :], ACT.Sqrt).then_inc(rf_done, 1)

        @block.vector
        def _(dve):
            count = [0]

            def link(ins):
                count[0] += 1
                ins.then_inc(dve_seq, 1)
                dve.wait_ge(dve_seq, count[0])

            def split_lo(n):
                u = SPLIT_UNITS[n]
                dve.wait_ge(hi_ready, n + 1)
                if n >= LO_SLOTS:
                    dve.wait_ge(unit_mm, n - LO_SLOTS + 1)
                c = P * lo_share(n)
                nc.vector.tensor_tensor(WL[:, n % LO_SLOTS, 0:c], RAW[:, u % RAW_SLOTS, 0:c], WH[:, n % HI_SLOTS, 0:c],
                                        ALU.subtract).then_inc(lo_ready, 1)

            def gate(tile, out_ap, src, rows=P):
                k = TH_IDX[tile]
                dve.wait_ge(th_full, k + 1)
                if tile[0] in CONV:
                    wait_tile_out(dve, tile)
                nc.vector.scalar_tensor_tensor(out_ap, TH[0:rows, k % 2, :], 1.0, src, ALU.add, ALU.mult).then_inc(gated, 1)

            pending = []

            def read_out(tile):
                if tile is None:
                    return
                kind, j = tile
                t = TILE_IDX[tile]
                bank = GB[t % G_BANKS][:, 0:SEQ]
                if kind in CONV:
                    ci, col = conv_index(kind, j), conv_src(kind, j)
                    dve.wait_ge(conv_acc, ci + 1)
                    for tap in (2, 1, 0):
                        s = 3 - tap
                        ins = nc.vector.scalar_tensor_tensor(ACC[:, ci % 2, s:SEQ], GB[t % G_BANKS][:, 0:SEQ - s],
                                                             CW[:, 4 * col + tap:4 * col + tap + 1], ACC[:, ci % 2, s:SEQ],
                                                             ALU.mult, ALU.add)
                        if tap:
                            link(ins)
                        else:
                            ins.then_inc(g_free[t % G_BANKS], 1)
                if pending:
                    prev = pending.pop()
                    ci = conv_index(*prev)
                    if prev[0] == "x" and prev[1] >= 2 * TPG:
                        wait_small_full(dve, ("xt", (prev[1] // TPG - 2, 1), 0))
                        wait_y_out(dve, ("y", 2 * (prev[1] // TPG - 2) + 1))
                    gate(prev, conv_dst(*prev), ACC[:, ci % 2, :])
                if kind in CONV:
                    pending.append(tile)
                elif kind in ("z", "za"):
                    gate(tile, (Z if kind == "z" else ZA)[:, j, :], bank)
                elif kind in NATIVE:
                    gate(tile, HID[0:60, int(kind == "w1v"), :], GB[t % G_BANKS][0:60, 0:CMP_HIDDEN], 60)
                elif kind in ("ks", "kw"):
                    br = int(kind == "kw")
                    for half in range(2):
                        for dup in range(2):
                            dve.wait_ge(kh_done, 8 * br + 4 * j + 4)
                            rows = slice(64 * dup, 64 * dup + 64)
                            last = nc.vector.tensor_tensor(KL[rows, 2 * j + half, br, :], GB[t % G_BANKS][64 * half:64 * half + 64, 0:SEQ],
                                                           KH[rows, 2 * j + half, br, :], ALU.subtract)
                    last.then_inc(g_free[t % G_BANKS], 1)
                elif kind == "q":
                    for half in range(2):
                        dve.wait_ge(qh_done, 2 * j + 2)
                        last = nc.vector.scalar_tensor_tensor(QS[64:128, 2 * j + half, :], GB[t % G_BANKS][64 * half:64 * half + 64, 0:SEQ],
                                                              HEAD_DIM ** -0.5, QS[0:64, 2 * j + half, :], ALU.mult, ALU.subtract)
                    last.then_inc(g_free[t % G_BANKS], 1)
                elif kind == "ssm":
                    wait_tile_full(dve, tile)
                    if j == 0:
                        wait_small_full(dve, ("ct", 1, 0))
                    nc.vector.scalar_tensor_tensor(YS[:, j, :], MT[:, j, :], 1.0, bank, ALU.add, ALU.mult).then_inc(g_free[t % G_BANKS], 1)
                elif kind == "nsa":
                    wait_tile_full(dve, tile)
                    if j >= 2:
                        dve.wait_ge(ml_done, j - 1)
                    nc.vector.scalar_tensor_tensor(MTMP[:, j % 2, 0, :], MT[:, 8 + j, :], 1.0, bank, ALU.add,
                                                   ALU.mult).then_inc(g_free[t % G_BANKS], 1)
                    wait_tile_out(dve, tile)
                    nc.vector.tensor_tensor(MTMP[:, j % 2, 1, :], MTMP[:, j % 2, 0, :], YS[:, j, :], ALU.add).then_inc(mf_done, 1)
                    for m in ([j - 1] if j else []) + ([7] if j == 7 else []):
                        dve.wait_ge(mh_done, m + 1)
                        nc.vector.tensor_tensor(ML[:, m, :], MTMP[:, m % 2, 1, :], MH[:, m, :], ALU.subtract).then_inc(ml_done, 1)

            dve.wait_ge(par_in_s, 16)
            nc.vector.tensor_scalar(CW[:], PR[:, PAR["conv_w"][0]:PAR["conv_b"][1]], 0.5, None, ALU.mult).then_inc(cw_ready, 1)
            dve.wait_ge(ssx_full, 1)
            nc.vector.tensor_scalar(RX[:, 0, :], YB[:, 0:SEQ], 1.0 / D_MODEL, EPS, ALU.mult, ALU.add).then_inc(varx_done, 1)
            dve.wait_ge(rx_done, 1)
            link(nc.vector.reciprocal(RX[:, 1, :], RX[:, 0, :]))
            link(nc.vector.tensor_tensor(XT[:], XT[:], RX[:, 1, :].unsqueeze(1).to_broadcast([P, KT, SEQ]), ALU.mult))
            split_lo(0)
            dve.wait_ge(modT_full, 1)
            rows = SB[1][:, :].rearrange("p (m j r) -> p j m r", m=4, j=4)[:, :, :, 0]
            link(nc.vector.tensor_tensor(MOD[:].rearrange("p (j m) -> p j m", j=4), rows,
                                         par("b_ada", 0, 16).rearrange("p (j m) -> p j m", j=4), ALU.add))
            link(nc.vector.scalar_tensor_tensor(AB[:, 0:8], MOD[:, 8:16], 1.0, par("g_pre"), ALU.add, ALU.mult))
            for k in range(KT):
                nc.vector.tensor_scalar(XT[:, k, :], XT[:, k, :], AB[:, k:k + 1], MOD[:, k:k + 1], ALU.mult,
                                        ALU.add).then_inc(h_f32, 1)
                if k >= 1:
                    dve.wait_ge(h_hi, k)
                    nc.vector.tensor_tensor(HL[:, k - 1, :], XT[:, k - 1, :], HH[:, k - 1, :], ALU.subtract).then_inc(h_ready, 1)
            dve.wait_ge(h_hi, KT)
            nc.vector.tensor_tensor(HL[:, KT - 1, :], XT[:, KT - 1, :], HH[:, KT - 1, :], ALU.subtract).then_inc(h_ready, 1)
            for n in range(1, AHEAD):
                split_lo(n)

            done = None
            for step in LATE_STEPS:
                what, i = step
                key = step + (0,)
                bank = TB[T_IDX[key] % 2] if key in T_IDX else None
                release = t_free[T_IDX[key] % 2] if key in T_IDX else None
                if what == "gemm":
                    read_out(done)
                    done = finished_tile(i)
                    if i + AHEAD in SPLIT_IDX:
                        split_lo(SPLIT_IDX[i + AHEAD])
                elif what == "flush":
                    read_out(done)
                elif what == "acs":
                    dve.wait_ge(hi4_done, 1)
                    dve.wait_ge(adt_done, 2)
                    dve.wait_ge(consts_made, 7)
                    acs = bank[:, 0:2 * P].rearrange("p (c l) -> p c l", c=2)
                    nc.vector.tensor_copy(TP[0:32], HI4[0:32]).then_inc(cols_ready, 1)
                    nc.vector.tensor_tensor(TP[32:64], acs[32:64], HI4[32:64], ALU.subtract).then_inc(cols_ready, 1)
                    nc.vector.tensor_copy(ST[64:96], HI4[64:96]).then_inc(cols_ready, 1)
                    nc.vector.tensor_tensor(ST[96:128], acs[96:128], HI4[96:128], ALU.subtract).then_inc(cols_ready, 1)
                    nc.vector.tensor_copy(HI4X[:], bank[0:1, 0:1]).then_inc(release, 1)
                elif what == "xt":
                    g, c = i
                    wait_small_full(dve, key)
                    if g >= 1:
                        wait_y_full(dve, ("y", 2 * g - 1))
                    if c == 0 and g >= 1:
                        dve.wait_ge(xds_done, g)
                    dt = DT[:, c, HPC * g:HPC * (g + 1)].unsqueeze(2).to_broadcast([P, HPC, HEAD_DIM])
                    nc.vector.tensor_tensor(XDT[:, c, :, :], bank[:, :].rearrange("p (h d) -> p h d", h=HPC), dt,
                                            ALU.mult).then_inc(release, 1)
                elif what == "seg":
                    dve.wait_ge(s_free[0], S_IDX[step] + 1)
                    if i >= 1:
                        wait_y_full(dve, ("y", i - 1))
                    wait_small_out(dve, ("cb", i // 4, 0))
                    nc.vector.tensor_tensor(MM[:, 0, :, :], EX[:, 0, :, :], CB[:, i // 2, 0, :].unsqueeze(1).to_broadcast([P, 4, P]),
                                            ALU.mult).then_inc(mm_done[0], 1)
                elif what == "y":
                    wait_y_full(dve, step)
                    for t in (2 * i, 2 * i + 1):
                        x = XG[:, (t // TPG) % 2, t % TPG, :]
                        last = nc.vector.scalar_tensor_tensor(x, x, par("d_skip", t, t + 1), YB[:, SEQ * (t % 2):SEQ * (t % 2 + 1)],
                                                              ALU.mult, ALU.add)
                    last.then_inc(y_free, 1)
                    wait_y_out(dve, step)
                    x2 = XG[:, (i // 2) % 2, 2 * (i % 2):2 * (i % 2) + 2, :]
                    nc.vector.tensor_tensor(Z[:, 2 * i:2 * i + 2, :], x2, Z[:, 2 * i:2 * i + 2, :], ALU.mult).then_inc(ypre_done, 1)
                elif what == "ssq":
                    wait_small_full(dve, key)
                    gsz = D_INNER // SSM_GROUPS
                    nc.vector.tensor_scalar(RN[:, 0, :], bank[:, 0:SEQ], 1.0 / gsz, 4.0 * EPS, ALU.mult, ALU.add).then_inc(release, 1)
                elif what == "yn":
                    if i % TPG == 0:
                        dve.wait_ge(rn_done, i // TPG + 1)
                        link(nc.vector.reciprocal(RN[:, 1, :], RN[:, 0, :]))
                        dve.wait_ge(ysq_done, i // TPG + 1)
                    if i >= 2:
                        dve.wait_ge(yn_done, i - 1)
                    nc.vector.scalar_tensor_tensor(YT[:, i % 2, :], Z[:, i, :], par("g_ssm", i, i + 1), RN[:, 1, :], ALU.mult,
                                                   ALU.mult).then_inc(ynf_done, 1)
                elif what == "ynlo":
                    dve.wait_ge(ynh_done, i + 1)
                    nc.vector.tensor_tensor(YNL[:, i, :], YT[:, i % 2, :], YNH[:, i, :], ALU.subtract).then_inc(yn_done, 1)
                elif what == "blk" and i == 0:
                    compress_blocks(dve, nc.vector, 0)
                elif what == "kcp":
                    dve.wait_ge(kch_done, 1)
                    nc.vector.tensor_tensor(KC[:, :, 16:16 + N_CMP], bank[:, 0:60].rearrange("p (g j) -> p g j", g=KV_GROUPS),
                                            KC[:, :, 0:N_CMP], ALU.subtract).then_inc(release, 1)
                elif what == "cs":
                    wait_small_full(dve, key)
                    dve.wait_ge(cst2_in_s, 16)
                    sc = bank[:, :].rearrange("p (h n j) -> p h n j", h=ATT_HEADS, n=2)
                    bias = cst("bias_c").rearrange("p (t h j) -> p t h j", t=2, h=ATT_HEADS)[:, i]
                    link(nc.vector.tensor_tensor(CSW[:, i], sc[:, :, 1, :], bias, ALU.add))
                    nc.vector.tensor_tensor(CSW[:, i], sc[:, :, 0, :], CSW[:, i], ALU.add).then_inc(release, 1)
                    wait_small_out(dve, key)
                    if i == 0:
                        continue
                    link(nc.vector.tensor_reduce(CSM[:, 0], CSW[:], AX.X, ALU.max))
                    nc.vector.tensor_tensor(CSW[:], CSW[:], CSM[:, 0].unsqueeze(3).to_broadcast([P, 2, ATT_HEADS, 16]),
                                            ALU.subtract).then_inc(cs_sub, 1)
                elif what == "cs2":
                    dve.wait_ge(cs_exp, 1)
                    wait_zeros(dve, "p_cmp")
                    link(nc.vector.tensor_reduce(CSM[:, 1], CSW[:], AX.X, ALU.add))
                    link(nc.vector.reciprocal(CSM[:, 2], CSM[:, 1]))
                    nc.vector.tensor_tensor(CSM[:, 0], CSM[:, 2], GATE[:, :, :, 0], ALU.mult)
                    valid = cst("valid_c").rearrange("p (t j) -> p t j", t=2).unsqueeze(2).to_broadcast([P, 2, ATT_HEADS, 16])
                    link(nc.vector.tensor_tensor(CSW[:], CSW[:], valid, ALU.mult))
                    nc.vector.tensor_tensor(PC[:, :, :, 0:16], CSW[:], CSM[:, 0].unsqueeze(3).to_broadcast([P, 2, ATT_HEADS, 16]),
                                            ALU.mult).then_inc(pc_done, 1)
                elif what == "sc":
                    n, k = S_IDX[step], i % 2
                    for qt in range(2):
                        dve.wait_ge(s_full[qt], n + 1)
                        nk = P * (qt + 1)
                        nc.vector.tensor_reduce(SM[:, k, 0, 2 * qt:2 * qt + 2], SB[qt][:, 0:2 * nk].rearrange("p (b n) -> p b n", b=2),
                                                AX.X, ALU.max, negate=True).then_inc(max_done, 1)
                elif what == "ps":
                    n, k = S_IDX[("sc", i)], i % 2
                    dve.wait_ge(s_free[0], n + 1)
                    dve.wait_ge(s_free[1], n + 1)
                    link(nc.vector.reciprocal(SM[:, k, 2, :], SM[:, k, 1, :]))
                    link(nc.vector.tensor_tensor(SM[:, k, 3, :].rearrange("p (t b) -> p t b", t=2),
                                                 SM[:, k, 2, :].rearrange("p (t b) -> p t b", t=2), GATE[:, :, i, 1:3], ALU.mult))
                    for qt in range(2):
                        for b in range(2):
                            e = E[:, k, b, P * qt:P * qt + P * (qt + 1)]
                            nc.vector.tensor_scalar(e, e, SM[:, k, 3, 2 * qt + b:2 * qt + b + 1], None, ALU.mult).then_inc(p_done, 1)
                elif what == "pt":
                    key1 = step + (1,)
                    wait_small_full(dve, key1)
                    if i >= 2:
                        wait_y_full(dve, ("pv", i // 2 - 1))
                    nc.vector.tensor_copy(PT[:, i % 2, :, SEQ:SEQ + P],
                                          TB[T_IDX[key1] % 2][:, 0:SEQ].rearrange("p (b q) -> p b q", b=2)
                                          ).then_inc(t_free[T_IDX[key1] % 2], 1)
                elif what == "pv":
                    wait_y_full(dve, step)
                    dve.wait_ge(gated, TH_IDX[("za", i)] + 1)
                    nc.vector.tensor_tensor(ZA[:, i, :], ZA[:, i, :], YB[:, 0:SEQ], ALU.mult).then_inc(y_free, 1)
                elif what == "osp":
                    dve.wait_ge(oh_done, i + 1)
                    nc.vector.tensor_tensor(OL[:, i, :], ZA[:, i, :], OH[:, i, :], ALU.subtract).then_inc(o_split, 1)
                elif what == "agT":
                    wait_small_full(dve, key)
                    rows = bank[:, 0:2 * P].rearrange("p (m j r) -> p j m r", m=2, j=4)[:, :, :, 0]
                    nc.vector.tensor_tensor(GG[:, 0, :].rearrange("p (j m) -> p j m", j=4), rows,
                                            par("b_ada", 16, 24).rearrange("p (j m) -> p j m", j=4), ALU.add).then_inc(release, 1)
                    wait_small_out(dve, key)
                    nc.vector.tensor_tensor(GG[:, 1, :], GG[:, 0, :], par("g_post"), ALU.mult).then_inc(gg_done, 1)
            dve.wait_ge(osq_full, 8)
            nc.vector.tensor_scalar(RF[:, 0, :], YB[:, 0:SEQ], 1.0 / D_MODEL, 4.0 * EPS, ALU.mult, ALU.add).then_inc(varf_done, 1)
            dve.wait_ge(rf_done, 1)
            nc.vector.reciprocal(RF[:, 1, :], RF[:, 0, :]).then_inc(rf_done, 1)
            dve.wait_ge(rf_done, 2)
            dve.wait_ge(xr_in, 16)
            wait_tile_out(dve, ("out", 6))
            wait_tile_out(dve, ("out", 7))
            for m in range(0, FINAL_DVE, 2):
                r = RF[:, 1, :].unsqueeze(1).to_broadcast([P, 2, SEQ])
                link(nc.vector.tensor_tensor(OUT[:, m:m + 2, :], OUT[:, m:m + 2, :], r, ALU.mult))
                nc.vector.tensor_tensor(OUT[:, m:m + 2, :], OUT[:, m:m + 2, :], XR[:, m:m + 2, :], ALU.add).then_inc(fin_done[0], 1)

        @block.gpsimd
        def _(pool):
            made = [0]

            def link(ins):
                made[0] += 1
                ins.then_inc(pool_seq, 1)
                pool.wait_ge(pool_seq, made[0])

            nc.gpsimd.memset(ROWS[:], 0.0).then_inc(zeros, 1)
            wait_zeros(pool, "rows")
            for n, (ap, value) in enumerate(((ST[0:64].bitcast(f32), 1.0), (TP[64:128], -1.0), (ONZ[0:64].bitcast(f32), 1.0),
                                             (ONZ[64:128].bitcast(f32), 0.0))):
                nc.gpsimd.memset(ap, value).then_inc(consts_made, 1)
                pool.wait_ge(consts_made, n + 1)
            pool.wait_ge(cst_in_s, 16)
            pool.wait_ge(cst2_in_s, 16)
            nc.gpsimd.tensor_copy(IDB[:], cst("ident")).then_inc(consts_made, 1)
            nc.gpsimd.tensor_copy(MSL[:], cst("mask_sl")).then_inc(consts_made, 1)
            nc.gpsimd.tensor_copy(MQK[:], cst("mask_qk")).then_inc(consts_made, 1)

            def split_lo_rest(n):
                u, c = SPLIT_UNITS[n], P * lo_share(n)
                pool.wait_ge(hi_ready, n + 1)
                if n >= LO_SLOTS:
                    pool.wait_ge(unit_mm, n - LO_SLOTS + 1)
                nc.gpsimd.tensor_tensor(WL[:, n % LO_SLOTS, c:1024], RAW[:, u % RAW_SLOTS, c:1024], WH[:, n % HI_SLOTS, c:1024],
                                        ALU.subtract).then_inc(lo_rest_ready, 1)

            for n in range(AHEAD):
                split_lo_rest(n)

            def moving_rows(quad):
                for c in range(2):
                    oh = cst("onehot", 4 * quad, 4 * quad + 4).unsqueeze(2).to_broadcast([P, 4, P])
                    nc.gpsimd.tensor_tensor(MV[:, c, :, :], TP[:, c, :].unsqueeze(1).to_broadcast([P, 4, P]), oh,
                                            ALU.mult).then_inc(mv_done, 1)

            for step in STEPS:
                what, i = step
                key = step + (0,)
                if what == "gemm":
                    if i + AHEAD in SPLIT_IDX:
                        split_lo_rest(SPLIT_IDX[i + AHEAD])
                elif what == "dtA":
                    wait_small_out(pool, ("dtT", 0, 0))
                    x = DTT[:, :, 0:SSM_HEADS]
                    link(nc.gpsimd.tensor_scalar(DTW[:, 1], x, 0.0, None, ALU.max))
                    link(nc.gpsimd.tensor_scalar(DTW[:, 0], DTW[:, 1], 2.0, None, ALU.mult))
                    nc.gpsimd.tensor_tensor(DTW[:, 0], DTW[:, 0], x, ALU.subtract).then_inc(abs_done, 1)
                    pool.wait_ge(gate_tanh, 1)
                    nc.gpsimd.tensor_scalar(GATE[:], GATE[:], 0.25, 0.25, ALU.mult, ALU.add).then_inc(adt_done, 1)
                elif what == "dtB":
                    pool.wait_ge(dt_exp, 1)
                    nc.gpsimd.tensor_scalar(DTW[:, 3], DTW[:, 2], 1.0, None, ALU.add).then_inc(dt_u, 1)
                elif what == "dtC":
                    pool.wait_ge(dt_u, 1)
                    link(nc.gpsimd.tensor_scalar(DT[:], DTW[:, 3], 1.0, None, ALU.subtract))
                    link(nc.gpsimd.tensor_tensor(DT[:], DTW[:, 2], DT[:], ALU.subtract))
                    pool.wait_ge(dt_inv, 1)
                    link(nc.gpsimd.tensor_tensor(DT[:], DT[:], DTW[:, 5], ALU.mult))
                    link(nc.gpsimd.tensor_tensor(DT[:], DT[:], DTW[:, 1], ALU.add))
                    link(nc.gpsimd.tensor_tensor(DT[:], DT[:], DTW[:, 4], ALU.add))
                    pool.wait_ge(a_exp, 1)
                    link(nc.gpsimd.tensor_tensor(DTW[:, 0], DT[:], AEX[:].unsqueeze(1).to_broadcast([P, 2, SSM_HEADS]), ALU.mult))
                    nc.gpsimd.tensor_scalar(ADT4[:], DTW[:, 0].unsqueeze(2).to_broadcast([P, 2, 4, SSM_HEADS]), -1.0, None,
                                            ALU.mult).then_inc(adt_done, 1)
                elif what == "acs":
                    pool.wait_ge(cols_ready, 4)
                    moving_rows(0)
                elif what == "xt" and i[1] == 0:
                    g = i[0]
                    wait_small_out(pool, key)
                    if g >= 1:
                        wait_small_full(pool, ("st", g - 1, 0))
                    pool.wait_ge(hi4_done, 1)
                    nc.gpsimd.tensor_tensor(XDS[:], XDT[:, 0, :, :],
                                            DS[:, HPC * g:HPC * (g + 1)].unsqueeze(2).to_broadcast([P, HPC, HEAD_DIM]),
                                            ALU.mult).then_inc(xds_done, 1)
                elif what == "seg":
                    pool.wait_ge(s_free[1], S_IDX[step] + 1)
                    if i >= 1:
                        wait_y_full(pool, ("y", i - 1))
                    wait_small_out(pool, ("cb", i // 4, 0))
                    nc.gpsimd.tensor_tensor(MM[:, 1, :, :], EX[:, 1, :, :], CB[:, i // 2, 1, :].unsqueeze(1).to_broadcast([P, 4, P]),
                                            ALU.mult).then_inc(mm_done[1], 1)
                elif what == "ea":
                    wait_small_out(pool, key)
                    g = i // 2
                    nc.gpsimd.tensor_tensor(CE[:], EA[:], CTT[:, g, CHUNK:SEQ].unsqueeze(1).to_broadcast([P, 4, P]),
                                            ALU.mult).then_inc(ce_done, 1)
                    if i + 1 < QUADS:
                        moving_rows(i + 1)
                elif what == "blk" and i == 1:
                    nc.gpsimd.memset(HVR[:], 0.0).then_inc(zeros, 1)
                    compress_blocks(pool, nc.gpsimd, 1)
                    pool.wait_ge(blk_done[0], 16)
                    nc.gpsimd.memset(VC[:], 0.0).then_inc(zeros, 1)
                    nc.gpsimd.memset(KC[:].bitcast(f32), 0.0).then_inc(zeros, 1)
                elif what == "zero":
                    wait_y_full(pool, ("y", 7))
                    nc.gpsimd.memset(PC[:], 0.0).then_inc(zeros, 1)
                    nc.gpsimd.memset(ROWS2[:], 0.0).then_inc(zeros, 1)
                    wait_small_full(pool, ("vcp", 0, 0))
                    pool.wait_ge(gated, TH_IDX[("w1v", 0)] + 1)
                    nc.gpsimd.memset(ALK[:], 0.0)
                    nc.gpsimd.memset(ALQ[:], 0.0).then_inc(zeros, 1)
            pool.wait_ge(rf_done, 2)
            pool.wait_ge(xr_in, 16)
            wait_tile_out(pool, ("out", 6))
            wait_tile_out(pool, ("out", 7))
            r = RF[:, 1, :].unsqueeze(1).to_broadcast([P, KT - FINAL_DVE, SEQ])
            link(nc.gpsimd.tensor_tensor(OUT[:, FINAL_DVE:KT, :], OUT[:, FINAL_DVE:KT, :], r, ALU.mult))
            nc.gpsimd.tensor_tensor(OUT[:, FINAL_DVE:KT, :], OUT[:, FINAL_DVE:KT, :], XR[:, FINAL_DVE:KT, :],
                                    ALU.add).then_inc(fin_done[1], 1)


def host_constants():
    f = np.float32
    i = np.arange(P)
    onehot = (i[:, None] % SSM_HEADS == np.arange(SSM_HEADS)[None, :]).astype(f)
    slopes = (2.0 ** (-8.0 * np.arange(1, ATT_HEADS + 1) / ATT_HEADS)).astype(f)
    t = np.arange(SEQ).reshape(2, P).T
    end = np.arange(16) * CMP_STRIDE + CMP_BLOCK - 1
    dist = (t[:, :, None] - end[None, None, :]).astype(f)
    valid = (dist >= 0) & (np.arange(16) < N_CMP)[None, None, :]
    bias = np.where(valid[:, :, None, :], -slopes[None, None, :, None] * dist[:, :, None, :], f(NEG)).astype(f)
    parts = {"ident": np.eye(P), "tri": i[:, None] <= i[None, :], "tri_strict": i[:, None] > i[None, :],
             "ones": np.ones((P, P)), "mask_sl": np.where(i[None, :] < i[:, None], NEG, 0.0),
             "mask_qk": np.where(i[None, :] > i[:, None], NEG, 0.0), "onehot": onehot,
             "bias_c": bias.reshape(P, -1), "valid_c": valid.reshape(P, -1)}
    consts = np.concatenate([np.asarray(parts[n], f).reshape(P, -1) for n in CST if n != "end"], axis=1)

    def bf16_bits(v):
        out, rest = [], v.astype(f)
        for _ in range(3):
            bits = rest.view(np.uint32) & np.uint32(0xFFFF0000)
            out.append((bits >> 16).astype(np.uint16))
            rest = (rest - bits.view(f)).astype(f)
        return out

    alibi_q = np.zeros((P, ATT_HEADS, SEQ), np.uint16)
    alibi_k = np.zeros((P, 2, SEQ), np.uint16)
    pos = np.arange(SEQ, dtype=f)
    for n, bits in enumerate(bf16_bits(np.repeat(slopes[:, None], SEQ, 1).copy())):
        alibi_q[n] = bits
        alibi_k[n] = (pos.view(np.uint32) >> 16).astype(np.uint16)[None, :]
    for n, bits in enumerate(bf16_bits((-slopes[:, None] * pos[None, :]).astype(f))):
        alibi_q[3 + n] = bits
        alibi_k[3 + n] = np.uint16(0x3F80)
    return consts, alibi_q.reshape(P, -1)[0:6], alibi_k[0:6]


def lay_out(inputs):
    w = {k: np.asarray(v) for k, v in inputs.items()}
    f = np.float32

    def cols(v, n):
        return v.reshape(n, P).T

    def tile_of(m):
        k, n = m.shape
        return m.reshape(k // P, P, n // P, P).transpose(2, 1, 0, 3)

    w_in = w["w_in"][0]
    lens = {"z": (OFF_Z, D_INNER), "x": (OFF_X, D_INNER), "b": (OFF_B, 512), "c": (OFF_C, 512), "q": (OFF_Q, 1024),
            "kc": (OFF_KV, 256), "vc": (OFF_KV + 256, 256), "ks": (OFF_KV + 512, 256), "vs": (OFF_KV + 768, 256),
            "kw": (OFF_KV + 1024, 256), "vw": (OFF_KV + 1280, 256), "za": (OFF_ZA, 1024), "mg": (OFF_MG, 2048)}
    tiles = {k: tile_of(w_in[:, a:a + n]) for k, (a, n) in lens.items()}
    dtg = np.zeros((D_MODEL, P), f)
    dtg[:, 0:SSM_HEADS] = w_in[:, OFF_DT:OFF_DT + SSM_HEADS]
    dtg[:, GATE_ROW:GATE_ROW + 48] = w_in[:, OFF_GATE:OFF_GATE + 48]
    tiles["dtg"] = tile_of(dtg)
    ssm = tile_of(w["w_ssm_out"][0])
    tiles["nsa"], tiles["out"] = tile_of(w["w_nsa_out"][0]), tile_of(w["w_out"][0])
    w1 = {k: w[n][0].reshape(16, 2, 64, CMP_HIDDEN).transpose(1, 2, 0, 3).reshape(P, 4, 1024)
          for k, n in (("w1k", "cmp_w1_k"), ("w1v", "cmp_w1_v"))}
    ada = w["w_ada"][0].reshape(KT, P, 3 * D_MODEL).transpose(1, 0, 2)
    wpack = np.empty((len(UNITS), P, 1024), f)
    for u, (kind, j, part) in enumerate(UNITS):
        if kind in w1:
            wpack[u] = w1[kind][:, part]
        elif kind == "ag":
            wpack[u] = ada[:, part, 2048:3072]
        elif kind == "ssm":
            wpack[u] = ssm[j][:, 8 * part:8 * part + 8].reshape(P, 1024)
        else:
            wpack[u] = tiles[kind][j].reshape(P, 1024)
    dt_bias = np.zeros((P, 1), f)
    dt_bias[0:SSM_HEADS, 0] = w["dt_bias"][0]
    pos = {k: np.concatenate([w[k][0].T, w[k][0].T], 0) for k in ("cmp_pos_k", "cmp_pos_v")}
    w2 = {k: w[k][0].reshape(2, P, 64).transpose(1, 0, 2) for k in ("cmp_w2_k", "cmp_w2_v")}
    parts = {"c": cols(w["c"][0], KT), "conv_w": w["conv_w"][0].reshape(4, 24, P).transpose(2, 1, 0).reshape(P, 96),
             "conv_b": cols(w["conv_b"][0], 24), "dt_bias": dt_bias, "g_pre": cols(w["g_pre"][0], 8),
             "g_post": cols(w["g_post"][0], 8), "b_ada": cols(w["b_ada"][0], 24), "g_ssm": cols(w["g_ssm_norm"][0], 16),
             "d_skip": cols(np.repeat(w["d_skip"][0], HEAD_DIM), 16), "a_log": np.repeat(w["a_log"], P, 0),
             "pos_k": pos["cmp_pos_k"], "pos_v": pos["cmp_pos_v"],
             "w2k": np.concatenate([w2["cmp_w2_k"]] * 2, 2).reshape(P, 256), "w2v": w2["cmp_w2_v"].reshape(P, 128)}
    params = np.concatenate([parts[n] for n in PAR if n != "end"], axis=1)
    xT = w["x"][0].T.reshape(KT, P, SEQ).transpose(1, 0, 2)
    consts, alibi_q, alibi_k = host_constants()
    return {"xT": xT, "params": params, "consts": consts, "alibi_q": alibi_q, "alibi_k": alibi_k,
            "w_ada1": ada[:, :, 0:2048], "wpack": wpack}


def kernel(**inputs):
    import concourse.bacc as bacc
    from concourse.bass_utils import run_bass_kernel_spmd

    nc = bacc.Bacc("TRN2", target_bir_lowering=False, num_devices=1)
    arrays, args = {}, []
    for name, a in lay_out(inputs).items():
        a = np.ascontiguousarray(a)
        arrays[f"in_{name}"] = a
        args.append(nc.dram_tensor(f"in_{name}", a.shape, mybir.dt.from_np(a.dtype), kind="ExternalInput").ap())
    out = nc.dram_tensor("out_T_dram", (P, KT, SEQ), mybir.dt.float32, kind="ExternalOutput").ap()
    build(nc, *args, out)
    r = run_bass_kernel_spmd(nc, [arrays], core_ids=[0])
    got = r.results[0]["out_T_dram"]
    return got.transpose(2, 1, 0).reshape(1, SEQ, D_MODEL)
```

```python
import numpy as np

import concourse.bass as bass
from concourse import mybir

P = 128
SEQ, D_MODEL = 256, 1024
D_INNER, SSM_HEADS, HEAD_DIM, SSM_GROUPS, STATE, CHUNK = 2048, 32, 64, 4, 128, 128
ATT_HEADS, KV_GROUPS, HPG = 16, 4, 4
CMP_BLOCK, CMP_STRIDE, CMP_HIDDEN = 32, 16, 256
N_CMP = (SEQ - CMP_BLOCK) // CMP_STRIDE + 1
EPS = 1e-6
NEG = -1e30
KT = D_MODEL // P
NCHUNK = SEQ // CHUNK
HPC = SSM_HEADS // SSM_GROUPS
QUADS = SSM_HEADS // 4
TPG = 4

D_CONV = D_INNER + 2 * SSM_GROUPS * STATE
OFF_Z = 0
OFF_X = D_INNER
OFF_B = OFF_X + D_INNER
OFF_C = OFF_B + SSM_GROUPS * STATE
OFF_DT = OFF_X + D_CONV
OFF_Q = OFF_DT + SSM_HEADS
OFF_KV = OFF_Q + ATT_HEADS * HEAD_DIM
OFF_GATE = OFF_KV + 6 * KV_GROUPS * HEAD_DIM
OFF_ZA = OFF_GATE + 3 * ATT_HEADS
OFF_MG = OFF_ZA + ATT_HEADS * HEAD_DIM
GATE_ROW = 64


def weight_units():
    units = [("dtg", 0, 0)]
    units += [("b", j, 0) for j in range(4)] + [("c", j, 0) for j in range(4)]
    for g in range(SSM_GROUPS):
        units += [("x", TPG * g + j, 0) for j in range(TPG)] + [("z", TPG * g + j, 0) for j in range(TPG)]
    units += [("kc", j, 0) for j in range(2)] + [("vc", j, 0) for j in range(2)]
    units += [("za", j, 0) for j in range(6)]
    units += [("w1k", 0, part) for part in range(4)] + [("za", j, 0) for j in range(6, 8)]
    units += [("w1v", 0, part) for part in range(4)]
    units += [("ks", 0, 0), ("ks", 1, 0)]
    for n, kind in enumerate(("kw", "vs")):
        for j in range(2):
            units += [(kind, j, 0), ("ag", 0, 2 * n + j)]
    for j in range(4):
        units += [("q", j, 0), ("ag", 0, 4 + j)]
    units += [("q", j, 0) for j in range(4, 8)]
    units += [("vw", j, 0) for j in range(2)]
    units += [("mg", j, 0) for j in range(16)]
    units += [("ssm", j, part) for j in range(8) for part in range(2)]
    units += [("nsa", j, 0) for j in range(8)] + [("out", j, 0) for j in range(8)]
    return units


UNITS = weight_units()
NATIVE = ("w1k", "w1v", "ag")
CONV = ("b", "c", "x")
LAST_PART = {"w1k": 3, "w1v": 3, "ssm": 1, "ag": 8}


def schedule():
    after = {}

    def put(u, *steps):
        after.setdefault(u, []).extend(steps)

    put(2, ("dtT", 0))
    put(4, ("dtA", 0), ("dtE", 0))
    put(6, ("dtB", 0), ("dtL", 0))
    put(8, ("bt", 0), ("dtC", 0))
    put(10, ("acs", 0))
    put(11, ("cb", 0))
    put(12, ("cb", 1))
    ssq_after = 12
    for g in range(SSM_GROUPS):
        b = 17 + 8 * g
        put(b, ("xt", (g, 0)))
        put(b + 1, ("xt", (g, 1)), ("seg", 2 * g))
        put(b + 2, ("ea", 2 * g))
        put(b + 3, ("st", g))
        put(b + 4, ("y", 2 * g), ("seg", 2 * g + 1))
        put(b + 5, ("ea", 2 * g + 1))
        put(b + 7, ("y", 2 * g + 1))
        put(b + 8, ("ysq", g))
        put(b + 10, ("ysum", g))
        put(b + ssq_after, ("ssq", g))
        for j in range(TPG + 2):
            for ahead, name in ((2, "ynlo"), (1, "ynhi"), (0, "yn")):
                if 0 <= j - ahead < TPG:
                    put(b + ssq_after + 2 + j, (name, TPG * g + j - ahead))
    put(47, ("blk", 1))
    put(48, ("blk", 0))
    at = UNITS.index
    put(at(("w1k", 0, 3)) + 2, ("hidT", 0))
    put(at(("w1v", 0, 3)) + 2, ("hidT", 1))
    put(at(("w1v", 0, 3)) + 1, ("kcp", 0))
    put(at(("w1v", 0, 3)) + 4, ("vcp", 0))
    put(at(("vs", 1, 0)) + 2, ("vt", 0))
    put(at(("w1v", 0, 3)) + 3, ("zero", 0))
    put(at(("ag", 0, 7)) + 1, ("agR", 0))
    put(at(("ag", 0, 7)) + 3, ("agT", 0))
    q7 = at(("q", 7, 0))
    put(q7 + 1, ("cs", 0), ("cs", 1))
    put(q7 + 2, ("cs2", 0))
    put(q7 + 3, ("vt", 1))
    put(q7 + 5, ("ct", 0), ("ct", 1))
    t0 = q7 - 2
    put(t0 - 3, ("kpos", 0))
    for h in range(ATT_HEADS):
        put(t0 - 2 + 2 * h, ("q2", h))
    for h in range(ATT_HEADS):
        put(t0 + 2 * h, ("sc", h))
        put(t0 + 1 + 2 * h, ("ex", h))
        put(t0 + 2 + 2 * h, ("ps", h))
        put(t0 + 4 + 2 * h, ("pt", h))
    last_h = at(("mg", 15, 0))
    for p in range(ATT_HEADS // 2):
        put(t0 + 8 + 4 * p + (p == 0), ("pv", p))
        put(max(last_h + 3, t0 + 8 + 4 * p), ("osp", p))
    out0 = UNITS.index(("out", 0, 0))
    for m in range(1, 7):
        put(out0 + 1 + m, ("osum", m))
    steps = []
    for u in range(len(UNITS)):
        steps.append(("gemm", u))
        steps += after.get(u, [])
    steps += [("osq", 0), ("flush", 0), ("osq", 1)]
    late = []
    for u in range(len(UNITS)):
        late += [("gemm", u)] + after.get(u - 1, [])
    late += [("flush", 0)] + after.get(len(UNITS) - 1, [])
    return steps, late


STEPS, LATE_STEPS = schedule()
SPLIT_IDX, NATIVE_IDX, TILE_IDX = {}, {}, {}
for _u, (_kind, _j, _part) in enumerate(UNITS):
    if _kind in NATIVE:
        NATIVE_IDX[_u] = len(NATIVE_IDX)
    else:
        SPLIT_IDX[_u] = len(SPLIT_IDX)
    if _part == 0 and _kind != "ag":
        TILE_IDX[(_kind, _j)] = len(TILE_IDX)
SPLIT_UNITS = sorted(SPLIT_IDX)
T_STEPS = ("dtT", "acs", "bt", "cb", "xt", "ea", "st", "ssq", "hidT", "kcp", "vcp", "vt", "cs", "ct", "pt", "agT")
T_IDX, S_IDX, Y_IDX = {}, {}, {}
for _s in STEPS:
    if _s[0] in T_STEPS:
        for _n in range(2 if _s[0] == "pt" else 1):
            T_IDX[_s + (_n,)] = len(T_IDX)
    if _s[0] in ("seg", "sc"):
        S_IDX[_s] = len(S_IDX)
    if _s[0] in ("y", "pv"):
        Y_IDX[_s] = len(Y_IDX)

TH_IDX, _pending = {}, None
for _kind, _j, _part in UNITS:
    if _part != LAST_PART.get(_kind, 0):
        continue
    if _kind in CONV or _pending:
        if _pending:
            TH_IDX[_pending] = len(TH_IDX)
            _pending = None
    if _kind in CONV:
        _pending = (_kind, _j)
    elif _kind in ("z", "za", "w1k", "w1v"):
        TH_IDX[(_kind, _j)] = len(TH_IDX)

PAR = {}


def _par(name, n):
    PAR[name] = (PAR["end"][1] if "end" in PAR else 0, (PAR["end"][1] if "end" in PAR else 0) + n)
    PAR["end"] = (0, PAR[name][1])


for _name, _n in (("c", KT), ("conv_w", 96), ("conv_b", 24), ("dt_bias", 1), ("g_pre", 8), ("g_post", 8), ("b_ada", 24),
                  ("g_ssm", 16), ("d_skip", 16), ("a_log", SSM_HEADS), ("pos_k", 32), ("pos_v", 32)):
    _par(_name, _n)
CST = {}


def _cst(name, n):
    CST[name] = (CST["end"][1] if "end" in CST else 0, (CST["end"][1] if "end" in CST else 0) + n)
    CST["end"] = (0, CST[name][1])


for _name, _n in (("ident", P), ("ones", P), ("tri", P), ("tri_strict", P), ("mask_sl", P), ("mask_qk", P),
                  ("onehot", SSM_HEADS)):
    _cst(_name, _n)

G_BANKS = 3
RAW_SLOTS, HI_SLOTS, LO_SLOTS = 5, 4, 4
H_POOL = (2, 4, 6)
FINAL_DVE = 6
AHEAD = LO_SLOTS - 1


def lo_share(n):
    return 7 if UNITS[SPLIT_UNITS[n]][0] in ("x", "z") else 6


def build(nc, xT, par_in, cst_in, alibi_q, alibi_k, w_ada1, w2_dram, cbias_dram, wpack, out):
    f32, f32r, bf16 = mybir.dt.float32, mybir.dt.float32r, mybir.dt.bfloat16
    ALU, ACT, AX = mybir.AluOpType, mybir.ActivationFunctionType, mybir.AxisListType

    cursor = [(nc.sbuf_base + 63) // 64 * 64]

    def place(name, shape, dt, at=None):
        size = (int(np.prod(shape[1:])) * (2 if dt == bf16 else 4) + 63) // 64 * 64
        off = cursor[0] if at is None else at
        if at is None:
            cursor[0] += size
        return nc.alloc_sbuf_tensor_at(name, shape, dt, offset=off)

    h_at = cursor[0]
    HH = place("h_hi", [P, KT, SEQ], f32r)
    HL = place("h_lo", [P, KT, SEQ], f32r)
    RAW = place("w_raw", [P, RAW_SLOTS, 1024], f32)
    WH = place("w_hi", [P, HI_SLOTS, 1024], f32r)
    WL = place("w_lo", [P, LO_SLOTS, 1024], f32r)
    PR = place("params", [P, PAR["end"][1]], f32)
    CS = place("consts", [P, CST["end"][1]], f32)
    IDB = place("ident_bf16", [P, P], bf16)
    MSL = place("mask_sl_bf16", [P, P], bf16)
    MQK = place("mask_qk_bf16", [P, P], bf16)
    CW = place("conv_half", [P, 120], f32)
    MOD = place("mod", [P, 16], f32)
    EPSC = place("eps_columns", [P, 3], f32)
    AB = place("ada_scale", [P, 16], f32)
    GG = place("gate_times_g", [P, 2, 8], f32)
    GATE = place("att_gate", [P, 2, ATT_HEADS, 3], f32)
    SM = place("softmax_small", [P, 2, 4, 4], f32)
    ys_at = cursor[0]
    F0 = place("dt_gate_T", [P, SEQ], f32)
    DTT = place("dt_gate_tok", [P, 2, P], f32)
    DT = place("dt", [P, 2, SSM_HEADS], f32)
    DTW = place("dt_work", [P, 6, 2, SSM_HEADS], f32)
    ADT4 = place("adt4", [P, 2, 4, SSM_HEADS], f32)
    HI4 = place("acs_hi", [P, 2, P], f32r)
    TP = place("acs_rows", [P, 2, P], f32)
    ST = place("acs_cols", [P, 2, P], f32r)
    ONZ = place("ones_then_zeros", [P, P], f32r)
    DS = place("decay_to_end", [P, SSM_HEADS], f32)
    AEX = place("exp_a_log", [P, SSM_HEADS], f32)
    assert cursor[0] - ys_at >= 8192, cursor[0] - ys_at
    YS = place("y_ssm_out", [P, 8, SEQ], f32, at=ys_at)
    z_at = cursor[0]
    Z = place("z_gate_then_y", [P, 16, SEQ], f32)
    YNH = place("ynorm_hi", [P, 16, SEQ], f32r, at=z_at)
    YNL = place("ynorm_lo", [P, 16, SEQ], f32r)
    ZA = place("z_att_then_o", [P, 8, SEQ], f32)
    q_at = cursor[0]
    QS = place("q_hi_lo", [P, ATT_HEADS, SEQ], f32r)
    KH = place("k_hi", [P, KV_GROUPS, 2, SEQ], f32r)
    KL = place("k_lo", [P, KV_GROUPS, 2, SEQ], f32r)
    V = place("v", [P, 2, 2, KV_GROUPS, HEAD_DIM], f32)
    over_at = cursor[0]
    kb = 1024
    assert over_at + 49 * kb <= 229344, over_at
    ADA = place("w_ada_shift_scale", [P, KT, 2048], f32, at=z_at)
    XT = place("x_T", [P, KT, SEQ], f32, at=over_at)
    HF = place("h", [P, KT, SEQ], f32, at=over_at + 8 * kb)
    SQX = place("x_sq", [P, KT, SEQ], f32, at=over_at + 8 * kb)
    RX = place("rstd_x", [P, 2, SEQ], f32, at=over_at + 16 * kb)
    ROWS = place("ada_rows", [P, 512], f32, at=over_at + 18 * kb)
    XG = place("x_conv_T", [P, 2, TPG, SEQ], f32, at=q_at)
    BTT = place("b_T", [P, 4, SEQ], f32, at=q_at + 8 * kb)
    CTT = place("c_T", [P, 4, SEQ], f32, at=q_at + 12 * kb)
    BTOK = place("b_tok", [P, 4, STATE], f32, at=q_at + 16 * kb)
    XDT = place("x_dt", [P, 2, HPC, HEAD_DIM], f32, at=q_at + 18 * kb)
    XDS = place("x_dt_decay", [P, HPC, HEAD_DIM], f32, at=q_at + 22 * kb)
    STA = place("state", [P, HPC * HEAD_DIM], f32, at=q_at + 24 * kb)
    CB = place("cb_T", [P, 4, 2, P], f32, at=q_at + 26 * kb)
    MV = place("seg_moving", [P, 2, 4, P], f32r, at=over_at)
    EX = place("decay", [P, 2, 4, P], f32, at=over_at + 4 * kb)
    MM = place("cb_decay", [P, 2, 4, P], f32, at=over_at + 8 * kb)
    EA = place("exp_acs", [P, 4, P], f32, at=over_at + 12 * kb)
    CE = place("c_exp_acs", [P, 4, P], f32, at=over_at + 14 * kb)
    SQ = place("y_sq", [P, 4, SEQ], f32, at=over_at + 16 * kb)
    YT = place("y_tmp", [P, 2, SEQ], f32, at=over_at + 20 * kb)
    RN = place("rstd_y", [P, 2, SEQ], f32, at=over_at + 22 * kb)
    BLK = place("cmp_blocks", [P, 2, 16, KV_GROUPS * N_CMP], f32, at=over_at + 24 * kb)
    KVC = place("kv_cmp_T", [P, 4, SEQ], f32, at=over_at + 32 * kb)
    HID = place("cmp_hidden", [P, 2, CMP_HIDDEN], f32, at=over_at + 36 * kb)
    HVR = place("hid_v_T", [P, 2, KV_GROUPS, 4, 32], f32, at=over_at + 38 * kb)
    ACC = place("conv_acc", [P, 2, SEQ], f32, at=over_at + 42 * kb)
    TH = place("tanh_tmp", [P, 2, SEQ], f32, at=over_at + 44 * kb)
    HIDK = place("hid_k_T", [P, 2, 60], f32, at=over_at + 46 * kb)
    KC = place("k_cmp_hi_lo", [P, KV_GROUPS, 32], f32r, at=over_at + 46 * kb + 512)
    W2 = place("w_compress_2", [P, 384], f32, at=over_at)
    CBI = place("cmp_bias_and_valid", [P, 544], f32, at=over_at + 28 * kb)
    MT = place("merge_tanh", [P, 16, SEQ], f32, at=over_at)
    CSW = place("cmp_scores", [P, 2, ATT_HEADS, 16], f32, at=ys_at + 4 * kb)
    CSM = place("cmp_small", [P, 3, 2, ATT_HEADS], f32, at=ys_at + 6 * kb)
    E = place("probs", [P, 2, 2, 384], f32, at=over_at + 16 * kb)
    PT = place("probs_T", [P, 2, 2, 384], f32, at=over_at + 22 * kb)
    PC = place("cmp_probs", [P, 2, ATT_HEADS, 32], f32, at=ys_at)
    PCT = place("cmp_probs_T", [P, KV_GROUPS, SEQ], f32, at=over_at + 28 * kb)
    VC = place("v_cmp", [P, KV_GROUPS, 2, P], f32, at=over_at + 32 * kb)
    ALQ = place("alibi_q", [P, ATT_HEADS * SEQ], bf16, at=over_at + 36 * kb)
    ALK = place("alibi_k", [P, 2, SEQ], bf16, at=over_at + 16 * kb)
    Q2 = place("q_hi_and_alibi", [P, 2, SEQ], f32r, at=over_at + 47 * kb)
    VT = place("v_T", [P, 2, SEQ], f32, at=over_at + 44 * kb)
    OH = place("o_hi", [P, 8, SEQ], f32r, at=h_at)
    OL = place("o_lo", [P, 8, SEQ], f32r, at=h_at + 8 * kb)
    MH = place("merged_hi", [P, 8, SEQ], f32r, at=z_at)
    ML = place("merged_lo", [P, 8, SEQ], f32r, at=z_at + 8 * kb)
    MTMP = place("merge_tmp", [P, 2, 2, SEQ], f32, at=over_at + 16 * kb)
    SQO = place("out_sq", [P, 2, SEQ], f32, at=over_at + 20 * kb)
    ROWS2 = place("ada_gate_rows", [P, 256], f32, at=ys_at + 6 * kb + 512)
    SQA = place("out_sq_sum", [P, SEQ], f32, at=over_at + 22 * kb)
    RF = place("rstd_out", [P, 2, SEQ], f32, at=over_at + 24 * kb)
    XR = place("x_residual", [P, 8, SEQ], f32, at=over_at + 28 * kb)
    OUT = place("out_T", [P, 8, SEQ], f32, at=q_at - 8 * kb)

    def par(name, lo=0, hi=None):
        a, b = PAR[name]
        return PR[:, a + lo:(b if hi is None else a + hi)]

    def cst(name, lo=0, hi=None):
        a, b = CST[name]
        return CS[:, a + lo:(b if hi is None else a + hi)]

    GB = [nc.alloc_psum_tensor(f"gemm{i}", [P, 512], f32) for i in range(G_BANKS)]
    SB = [nc.alloc_psum_tensor(f"score{i}", [P, 512], f32) for i in range(2)]
    TB = [nc.alloc_psum_tensor(f"small{i}", [P, 512], f32) for i in range(2)]
    YB = nc.alloc_psum_tensor("y_or_o", [P, 512], f32)
    sems = {}

    def sem(name):
        if name not in sems:
            sems[name] = nc.alloc_semaphore(name)
        return sems[name]

    ada_in = [sem(f"ada_in{k}") for k in range(KT)]
    w_in = [sem(f"w_in{r}") for r in range(RAW_SLOTS)]
    par_in_s, cst_in_s, cst2_in_s, x_in, al_in, al2_in, xr_in, out_done = map(
        sem, ("params_in", "consts_in", "consts2_in", "x_in", "alibi_in", "alibi2_in", "xr_in", "out_done"))
    w2_in, cbias_in = sem("w2_in"), sem("cmp_bias_in")
    hi_ready, lo_ready, lo_rest_ready, unit_mm, native_mm = map(
        sem, ("hi_ready", "lo_ready", "lo_rest_ready", "unit_mm", "native_mm"))
    t_full, t_free, s_full, s_free = ([sem(f"{n}{b}") for b in range(2)] for n in ("t_full", "t_free", "s_full", "s_free"))
    g_free = [sem(f"g_free{b}") for b in range(G_BANKS)]
    y_full, y_free = sem("y_full"), sem("y_free")
    consts_made, zeros, bank_zeroed = sem("consts_made"), sem("zeros"), sem("bank_zeroed")
    cw_ready, sqx_done, ssx_full, rx_done, ada_full, rows_done, modT_full, ab_done, h_f32, h_f32_pool, h_hi, h_ready = map(
        sem, ("cw_ready", "sqx", "ssx_full", "rx", "ada_full", "rows", "modT_full", "ab", "h_f32", "h_f32_pool", "h_hi_done", "h_ready"))
    abs_done, dt_exp, dt_u, dt_ln, dt_inv, a_exp, gate_tanh, adt_done, hi4_done, cols_ready = map(
        sem, ("abs", "dt_exp", "dt_u", "dt_ln", "dt_inv", "a_exp", "gate_tanh", "adt", "hi4", "cols_ready"))
    conv_acc, th_full, gated = map(sem, ("conv_acc_s", "th_full", "gated"))
    xds_done, mv_done, ce_done, ypre_done, ysq_done, ysum_done, recip_done, ynf_done, ynh_done, yn_done = map(
        sem, ("xds", "mv", "ce", "ypre", "ysq", "ysum", "recip", "ynf", "ynh", "yn"))
    mm_done = [sem("mm0"), sem("mm1")]
    blk_done = [sem("blk0"), sem("blk1")]
    kl_alibi, q2_done, kch_done, kh_done, qh_done, cs_sub, cs_exp, pc_done, max_done, p_done, oh_done, o_split = map(
        sem, ("kl_alibi", "q2", "kch", "kh", "qh", "cs_sub", "cs_exp", "pc", "max", "p", "oh", "o_split"))
    rows2_done, gg_done, mf_done, mh_done, ml_done, osq_full, rf_done, sqo_done, sqa_done, eps_made = map(
        sem, ("rows2", "gg", "mf", "mh", "ml", "osq_full", "rf", "sqo", "sqa", "eps_made"))
    fin_done = [sem("fin_vector"), sem("fin_gpsimd")]
    dve_seq, act_seq, pool_seq = sem("dve_seq"), sem("act_seq"), sem("pool_seq")

    def conv_index(kind, j):
        return {"b": j, "c": 4 + j, "x": 8 + j}[kind]

    def conv_src(kind, j):
        return {"x": j, "b": 16 + j, "c": 20 + j}[kind]

    def conv_dst(kind, j):
        return {"b": BTT, "c": CTT}[kind][:, j, :] if kind != "x" else XG[:, (j // TPG) % 2, j % TPG, :]

    zeroed = ["hid_v", "v_cmp", "k_cmp", "p_cmp", "rows2", "q2", "k_lo"]

    def wait_zeros(eng, name):
        eng.wait_ge(zeros, zeroed.index(name) + 1)

    def wait_small_full(eng, key):
        eng.wait_ge(t_full[T_IDX[key] % 2], T_IDX[key] // 2 + 1)

    def wait_small_out(eng, key):
        eng.wait_ge(t_free[T_IDX[key] % 2], T_IDX[key] // 2 + 1)

    def wait_tile_full(eng, tile):
        u = UNITS.index(tile + (LAST_PART.get(tile[0], 0),))
        if u in SPLIT_IDX:
            eng.wait_ge(unit_mm, SPLIT_IDX[u] + 1)
        else:
            eng.wait_ge(native_mm, NATIVE_IDX[u] + 1)

    out_count = {}
    for tile in TILE_IDX:
        if tile[0] not in ("z", "za"):
            b = TILE_IDX[tile] % G_BANKS
            out_count[tile] = sum(1 for other in out_count if TILE_IDX[other] % G_BANKS == b) + 1

    def wait_tile_out(eng, tile):
        if tile in out_count:
            eng.wait_ge(g_free[TILE_IDX[tile] % G_BANKS], out_count[tile])
        else:
            eng.wait_ge(gated, TH_IDX[tile] + 1)

    def wait_y_full(eng, key):
        eng.wait_ge(y_full, Y_IDX[key] + 1)

    def wait_y_out(eng, key):
        eng.wait_ge(y_free, Y_IDX[key] + 1)

    def finished_tile(u):
        kind, j, part = UNITS[u]
        return (kind, j) if part == LAST_PART.get(kind, 0) else None

    def compress_blocks(eng, e, b):
        wait_tile_out(eng, ("vc" if b else "kc", 0))
        wait_tile_out(eng, ("vc" if b else "kc", 1))
        pos = PAR["pos_v" if b else "pos_k"][0]
        for g in range(KV_GROUPS):
            rows = slice(64 * (g % 2), 64 * (g % 2) + 64)
            kv = KVC[rows, 2 * b + g // 2, :].rearrange("p (j r n) -> p n r j", r=8, n=2)
            for n in range(2):
                for half in range(2):
                    r = PR[rows, pos + 16 * half + n:pos + 16 * half + 16:2].unsqueeze(2).to_broadcast([64, 8, N_CMP])
                    e.tensor_tensor(BLK[64 * n:64 * n + 64, b, 8 * half:8 * half + 8, N_CMP * g:N_CMP * (g + 1)],
                                    kv[:, n, :, half:half + N_CMP], r, ALU.add).then_inc(blk_done[b], 1)
                    if b:
                        eng.wait_ge(blk_done[b], 4 * g + 2 * n + half + 1)

    with nc.Block() as block:

        @block.sync
        def _(sp):
            early = 2 * P
            sp.dma_start(PR[:], par_in).then_inc(par_in_s, 16)
            sp.dma_start(CS[:, 0:early], cst_in[:, 0:early]).then_inc(cst_in_s, 16)
            for k in range(KT):
                sp.dma_start(ADA[:, k, :], w_ada1[:, k, :]).then_inc(ada_in[k], 16)
                if k == 1:
                    sp.dma_start(XT[:], xT).then_inc(x_in, 16)
            for u in range(2):
                sp.dma_start(RAW[:, u, :], wpack[u]).then_inc(w_in[u], 16)
            sp.dma_start(CS[:, early:CST["end"][1]], cst_in[:, early:CST["end"][1]]).then_inc(cst2_in_s, 16)
            for u in range(2, len(UNITS)):
                if u >= RAW_SLOTS:
                    v = u - RAW_SLOTS
                    if v in SPLIT_IDX:
                        sp.wait_ge(lo_ready, SPLIT_IDX[v] + 1)
                        sp.wait_ge(lo_rest_ready, SPLIT_IDX[v] + 1)
                    else:
                        sp.wait_ge(native_mm, NATIVE_IDX[v] + 1)
                sp.dma_start(RAW[:, u % RAW_SLOTS, :], wpack[u]).then_inc(w_in[u % RAW_SLOTS], 16)
                if u == UNITS.index(("w1v", 0, 0)) + 4:
                    wait_y_full(sp, ("y", 7))
                    sp.dma_start(W2[:], w2_dram).then_inc(w2_in, 16)
                if u == UNITS.index(("kw",1,0)):
                    sp.wait_ge(native_mm, NATIVE_IDX[UNITS.index(("w1v", 0, 3))] + 1)
                    sp.dma_start(CBI[:], cbias_dram).then_inc(cbias_in, 16)
                if u == UNITS.index(("q",0,0)):
                    wait_small_full(sp, ("vcp", 0, 0))
                    sp.wait_ge(gated, TH_IDX[("w1v", 0)] + 1)
                    wait_small_full(sp, ("ssq", 3, 0))
                    sp.wait_ge(yn_done, 16)
                    sp.dma_start(ALK[0:6].bitcast(mybir.dt.uint16), alibi_k).then_inc(al2_in, 16)
                if u == UNITS.index(("q",0,0)):
                    sp.dma_start(ALQ[0:6].bitcast(mybir.dt.uint16), alibi_q).then_inc(al_in, 16)
                if u == UNITS.index(("out", 0, 0)):
                    wait_y_out(sp, ("pv", 7))
                    sp.dma_start(XR[:], xT).then_inc(xr_in, 16)
            for m, (who, value) in ((0, (0, 1)), (6, (1, 1)), (2, (0, 2)), (4, (0, 3))):
                sp.wait_ge(fin_done[who], value)
                sp.dma_start(out[:, m:m + 2, :], OUT[:, m:m + 2, :]).then_inc(out_done, 16)
            sp.wait_ge(out_done, 4 * 16)

        @block.tensor
        def _(pe):
            ident = cst("ident")
            pe.wait_ge(cst_in_s, 16)
            pe.wait_ge(sqx_done, 1)
            for k in range(KT):
                last = nc.tensor.matmul(YB[:, 0:SEQ], cst("ones"), SQX[:, k, :], start=(k == 0), stop=(k == KT - 1))
            last.then_inc(ssx_full, 1)
            pe.wait_ge(par_in_s, 16)
            pe.wait_ge(bank_zeroed, 1)
            for k in range(KT):
                pe.wait_ge(ada_in[k], 16)
                for j in range(4):
                    last = nc.tensor.matmul(SB[0][32 * j:32 * j + 1, :], par("c", k, k + 1), ADA[:, k, 512 * j:512 * j + 512],
                                            start=(k == 0), stop=(k == KT - 1))
            last.then_inc(ada_full, 1)
            pe.wait_ge(rows_done, 1)
            for m in range(4):
                last = nc.tensor.transpose(SB[1][:, P * m:P * m + P], ROWS[:, P * m:P * m + P], ident)
            last.then_inc(modT_full, 1)

            def begin_small(key):
                n = T_IDX[key]
                if n >= 2:
                    pe.wait_ge(t_free[n % 2], n // 2)
                return TB[n % 2]

            def end_small(ins, key):
                ins.then_inc(t_full[T_IDX[key] % 2], 1)

            tiles = list(TILE_IDX)

            def weight_unit(u):
                kind, j, part = UNITS[u]
                if kind == "ag":
                    if part == 0:
                        wait_y_out(pe, ("y", 7))
                    pe.wait_ge(w_in[u % RAW_SLOTS], 16 * (u // RAW_SLOTS + 1))
                    for q in range(4):
                        last = nc.tensor.matmul(YB[32 * q:32 * q + 1, 0:256], par("c", part, part + 1),
                                                RAW[:, u % RAW_SLOTS, 256 * q:256 * q + 256], start=(part == 0), stop=(part == KT - 1))
                    last.then_inc(native_mm, 1)
                    return
                tile = TILE_IDX[(kind, j)]
                bank = GB[tile % G_BANKS]
                if part == 0 and tile >= G_BANKS:
                    wait_tile_out(pe, tiles[tile - G_BANKS])
                raw = RAW[:, u % RAW_SLOTS, :]
                if kind in NATIVE:
                    b = 0 if kind == "w1k" else 1
                    pe.wait_ge(w_in[u % RAW_SLOTS], 16 * (u // RAW_SLOTS + 1))
                    if part == 0:
                        pe.wait_ge(blk_done[b], 16)
                    for r in range(4):
                        rows = slice(64 * (r % 2), 64 * (r % 2) + 60)
                        last = nc.tensor.matmul(bank[rows, 0:CMP_HIDDEN], BLK[:, b, 4 * part + r, :],
                                                raw[:, CMP_HIDDEN * r:CMP_HIDDEN * (r + 1)],
                                                start=(part == 0 and r < 2), stop=(part == 3 and r >= 2))
                    last.then_inc(native_mm, 1)
                    return
                n = SPLIT_IDX[u]
                if kind == "ssm":
                    hi, lo, k0, parts = YNH, YNL, 8 * part, 2
                    if j == 0:
                        pe.wait_ge(yn_done, 8 * (part + 1))
                elif kind == "nsa":
                    hi, lo, k0, parts = OH, OL, 0, 1
                elif kind == "out":
                    hi, lo, k0, parts = MH, ML, 0, 1
                else:
                    hi, lo, k0, parts = HH, HL, 0, 1
                pe.wait_ge(hi_ready, n + 1)
                pe.wait_ge(lo_ready, n + 1)
                for k in range(KT):
                    if k == lo_share(n):
                        pe.wait_ge(lo_rest_ready, n + 1)
                    if u == 0:
                        pe.wait_ge(h_ready, k + 1)
                    if kind == "nsa" and j == 0:
                        pe.wait_ge(o_split, k + 1)
                    if kind == "out" and j == 0:
                        pe.wait_ge(ml_done, k + 1)
                    w_hi = WH[:, n % HI_SLOTS, P * k:P * k + P]
                    w_lo = WL[:, n % LO_SLOTS, P * k:P * k + P]
                    first, end = (k == 0 and part == 0), (k == KT - 1 and part == parts - 1)
                    nc.tensor.matmul(bank[:, 0:SEQ], w_hi, hi[:, k0 + k, :], start=first, stop=False)
                    nc.tensor.matmul(bank[:, 0:SEQ], w_hi, lo[:, k0 + k, :], start=False, stop=False)
                    last = nc.tensor.matmul(bank[:, 0:SEQ], w_lo, hi[:, k0 + k, :], start=False, stop=end)
                last.then_inc(unit_mm, 1)

            for step in STEPS:
                what, i = step
                if what == "gemm":
                    weight_unit(i)
                elif what == "dtT":
                    key = step + (0,)
                    bank = begin_small(key)
                    wait_tile_out(pe, ("dtg", 0))
                    for c in range(2):
                        last = nc.tensor.transpose(bank[:, P * c:P * c + P], F0[:, P * c:P * c + P], ident)
                    end_small(last, key)
                elif what == "acs":
                    key = step + (0,)
                    bank = begin_small(key)
                    pe.wait_ge(adt_done, 2)
                    pe.wait_ge(cst2_in_s, 16)
                    for c in range(2):
                        nc.tensor.matmul(bank[:, P * c:P * c + P], ADT4[:, c, :, :].rearrange("p r h -> p (r h)"),
                                         cst("tri"), start=True, stop=True)
                    last = nc.tensor.matmul(bank[:, 256:256 + SSM_HEADS], cst("tri_strict"), ADT4[:, 0, 0, :],
                                            start=True, stop=True)
                    end_small(last, key)
                elif what == "bt":
                    key = step + (0,)
                    bank = begin_small(key)
                    pe.wait_ge(gated, TH_IDX[("b", 3)] + 1)
                    for g in range(4):
                        last = nc.tensor.transpose(bank[:, P * g:P * g + P], BTT[:, g, 0:CHUNK], ident)
                    end_small(last, key)
                elif what == "cb":
                    key = step + (0,)
                    bank = begin_small(key)
                    pe.wait_ge(gated, TH_IDX[("c", 3)] + 1)
                    for gg in range(2):
                        for c in range(2):
                            o = P * (2 * gg + c)
                            last = nc.tensor.matmul(bank[:, o:o + P], BTT[:, 2 * i + gg, CHUNK * c:CHUNK * (c + 1)],
                                                    CTT[:, 2 * i + gg, CHUNK * c:CHUNK * (c + 1)], start=True, stop=True)
                    end_small(last, key)
                elif what == "xt":
                    g, c = i
                    key = step + (0,)
                    bank = begin_small(key)
                    pe.wait_ge(gated, TH_IDX[("x", TPG * g + 3)] + 1)
                    for t in range(TPG):
                        last = nc.tensor.transpose(bank[:, P * t:P * t + P], XG[:, g % 2, t, CHUNK * c:CHUNK * (c + 1)], ident)
                    end_small(last, key)
                elif what == "st":
                    key = step + (0,)
                    bank = begin_small(key)
                    pe.wait_ge(xds_done, i + 1)
                    wait_small_out(pe, ("bt", 0, 0))
                    last = nc.tensor.matmul(bank[:, :], BTOK[:, i, :], XDS[:, :, :].rearrange("p h d -> p (h d)"),
                                            start=True, stop=True)
                    end_small(last, key)
                elif what == "seg":
                    n = S_IDX[step]
                    for c in range(2):
                        if n >= 1:
                            pe.wait_ge(s_free[c], n)
                        if i == 0 and c == 0:
                            pe.wait_ge(cols_ready, 4)
                            pe.wait_ge(consts_made, 7)
                        pe.wait_ge(mv_done, 2 * i + c + 1)
                        mv = MV[:, c, :, :].rearrange("p j l -> p (j l)")
                        nc.tensor.matmul(SB[c][:, :], ST[:, c, :], mv, start=True, stop=False)
                        last = nc.tensor.matmul(SB[c][:, :], IDB[:], MSL[:].unsqueeze(1).to_broadcast([P, 4, P]),
                                                start=False, stop=True)
                        last.then_inc(s_full[c], 1)
                elif what == "ea":
                    key = step + (0,)
                    bank = begin_small(key)
                    last = nc.tensor.matmul(bank[:, :], ONZ[:], MV[:, 1, :, :].rearrange("p j l -> p (j l)"),
                                            start=True, stop=True)
                    end_small(last, key)
                elif what == "y":
                    n, g = Y_IDX[step], i // 2
                    if n >= 1:
                        pe.wait_ge(y_free, n)
                    pe.wait_ge(mm_done[0], i + 1)
                    pe.wait_ge(mm_done[1], i + 1)
                    pe.wait_ge(ce_done, i + 1)
                    wait_small_out(pe, ("st", g, 0))
                    wait_small_out(pe, ("xt", (g, 1), 0))
                    for t in range(2):
                        bank = YB[:, SEQ * t:SEQ * (t + 1)]
                        heads = [(k, 2 * t + k, 4 * (i % 2) + 2 * t + k) for k in range(2)]
                        for c in range(2):
                            for k, q4, h in heads:
                                nc.tensor.matmul(bank[64 * k:64 * k + 64, CHUNK * c:CHUNK * (c + 1)], XDT[:, c, h, :],
                                                 MM[:, c, q4, :], start=True, stop=(c == 0))
                        for k, q4, h in heads:
                            last = nc.tensor.matmul(bank[64 * k:64 * k + 64, CHUNK:SEQ], STA[:, HEAD_DIM * h:HEAD_DIM * (h + 1)],
                                                    CE[:, q4, :], start=False, stop=True)
                    last.then_inc(y_full, 1)
                elif what == "ssq":
                    key = step + (0,)
                    bank = begin_small(key)
                    pe.wait_ge(ysum_done, i + 1)
                    last = nc.tensor.matmul(bank[:, 0:SEQ], cst("ones"), SQ[:, 0, :], start=True, stop=True)
                    end_small(last, key)
                elif what == "hidT":
                    key = step + (0,)
                    bank = begin_small(key)
                    pe.wait_ge(gated, TH_IDX[("w1v" if i else "w1k", 0)] + 1)
                    for k in range(2):
                        last = nc.tensor.transpose(bank[:, 60 * k:60 * k + 60], HID[0:60, i, P * k:P * k + P],
                                                   CS[0:60, CST["ident"][0]:CST["ident"][0] + 60])
                    end_small(last, key)
                elif what == "kcp":
                    key = step + (0,)
                    bank = begin_small(key)
                    wait_small_out(pe, ("hidT", 0, 0))
                    pe.wait_ge(w2_in, 16)
                    for k in range(2):
                        last = nc.tensor.matmul(bank[:, 0:60], W2[:, P * k:P * k + P], HIDK[:, k, :],
                                                start=(k == 0), stop=(k == 1))
                    end_small(last, key)
                elif what == "vcp":
                    key = step + (0,)
                    bank = begin_small(key)
                    wait_small_out(pe, ("hidT", 1, 0))
                    for g in range(KV_GROUPS):
                        for k in range(2):
                            last = nc.tensor.matmul(bank[:, 64 * g:64 * g + 64], HVR[:, k, g, :, :].rearrange("p a b -> p (a b)"),
                                                    W2[:, 256 + 64 * k:256 + 64 * k + 64], start=(k == 0), stop=(k == 1))
                    end_small(last, key)
                elif what == "vt":
                    key = step + (0,)
                    bank = begin_small(key)
                    wait_tile_out(pe, ("vw" if i else "vs", 0))
                    wait_tile_out(pe, ("vw" if i else "vs", 1))
                    for kt in range(2):
                        for j in range(2):
                            o = P * (2 * kt + j)
                            last = nc.tensor.transpose(bank[:, o:o + P], VT[:, j, P * kt:P * kt + P], ident)
                    end_small(last, key)
                elif what == "cs":
                    key = step + (0,)
                    bank = begin_small(key)
                    for j in (6, 7):
                        wait_tile_out(pe, ("q", j))
                    wait_zeros(pe, "k_cmp")
                    wait_small_out(pe, ("kcp", 0, 0))
                    for h in range(ATT_HEADS):
                        last = nc.tensor.matmul(bank[:, 32 * h:32 * h + 32], QS[:, h, P * i:P * i + P], KC[:, h // HPG, :],
                                                start=True, stop=True)
                    end_small(last, key)
                elif what == "ct":
                    key = step + (0,)
                    bank = begin_small(key)
                    pe.wait_ge(pc_done, 1)
                    for gg in range(2):
                        for qt in range(2):
                            src = PC[:, qt, 4 * (2 * i + gg):4 * (2 * i + gg) + 4, :].rearrange("p h j -> p (h j)")
                            o = 256 * gg + P * qt
                            last = nc.tensor.transpose(bank[:, o:o + P], src, ident)
                    end_small(last, key)
                elif what == "sc":
                    n = S_IDX[step]
                    if i == 0:
                        for tile in (("ks", 0), ("ks", 1), ("kw", 0), ("kw", 1)):
                            wait_tile_out(pe, tile)
                        pe.wait_ge(kl_alibi, 1)
                    pe.wait_ge(q2_done, i + 1)
                    for qt in range(2):
                        pe.wait_ge(s_free[qt], n)
                        nk = P * (qt + 1)
                        o = SB[qt][:, 0:2 * nk].rearrange("p (b k) -> p b k", b=2)
                        q = QS[:, i, P * qt:P * qt + P]
                        nc.tensor.matmul(o, q, KH[:, i // HPG, :, 0:nk], start=True, stop=False)
                        nc.tensor.matmul(o, Q2[:, i % 2, P * qt:P * qt + P], KL[:, i // HPG, :, 0:nk], start=False, stop=False)
                        last = nc.tensor.matmul(o[:, :, P * qt:nk], IDB[:], MQK[:].unsqueeze(1).to_broadcast([P, 2, P]),
                                                start=False, stop=True)
                        last.then_inc(s_full[qt], 1)
                elif what == "pt":
                    pe.wait_ge(p_done, 4 * (i + 1))
                    e = E[:, i % 2, :, :]
                    key = step + (0,)
                    bank = begin_small(key)
                    for b in range(2):
                        nc.tensor.transpose(bank[:, 256 * b:256 * b + P], e[:, b, 0:P], ident)
                        last = nc.tensor.transpose(bank[:, 256 * b + P:256 * b + 256], e[:, b, P:2 * P], ident)
                    end_small(last, key)
                    key = step + (1,)
                    bank = begin_small(key)
                    for b in range(2):
                        last = nc.tensor.transpose(bank[:, P * b:P * b + P], e[:, b, 2 * P:3 * P], ident)
                    end_small(last, key)
                elif what == "pv":
                    n, bank = Y_IDX[step], YB
                    pe.wait_ge(y_free, n)
                    g = (2 * i) // HPG
                    if i == 0:
                        pe.wait_ge(rows2_done, 4)
                        wait_small_out(pe, ("ct", 0, 0))
                        wait_small_out(pe, ("ct", 1, 0))
                    for h in (2 * i, 2 * i + 1):
                        wait_small_out(pe, ("pt", h, 0))
                        wait_small_out(pe, ("pt", h, 1))
                    nc.tensor.matmul(bank[:, 0:SEQ], VC[:, g, i % 2, :], PCT[:, g, :], start=True, stop=False,
                                     skip_group_check=True)
                    for b in range(2):
                        for kt in range(2):
                            for k in range(2):
                                src = PT[:, k, b, 0:SEQ] if kt == 0 else PT[:, k, b, SEQ:SEQ + P]
                                last = nc.tensor.matmul(bank[64 * k:64 * k + 64, P * kt:SEQ], V[:, b, kt, g, :], src,
                                                        start=False, stop=(b == 1 and kt == 1), skip_group_check=True)
                    last.then_inc(y_full, 1)
                elif what == "agT":
                    key = step + (0,)
                    bank = begin_small(key)
                    pe.wait_ge(rows2_done, 4)
                    for m in range(2):
                        last = nc.tensor.transpose(bank[:, P * m:P * m + P], ROWS2[:, P * m:P * m + P], ident)
                    end_small(last, key)
                elif what == "osq" and i == 0:
                    wait_y_out(pe, ("pv", 7))
                    pe.wait_ge(sqa_done, 6)
                    nc.tensor.matmul(YB[:, 0:SEQ], cst("ones"), SQA[:], start=True, stop=False)
                elif what == "osq":
                    pe.wait_ge(sqo_done, 8)
                    nc.tensor.matmul(YB[:, 0:SEQ], cst("ones"), SQO[:, 1, :], start=False, stop=True).then_inc(osq_full, 1)

        @block.scalar
        def _(act):
            def split_hi(n):
                u = SPLIT_UNITS[n]
                act.wait_ge(w_in[u % RAW_SLOTS], 16 * (u // RAW_SLOTS + 1))
                if n >= HI_SLOTS:
                    act.wait_ge(unit_mm, n - HI_SLOTS + 1)
                nc.scalar.copy(WH[:, n % HI_SLOTS, :], RAW[:, u % RAW_SLOTS, :]).then_inc(hi_ready, 1)

            def tanh_half(tile, src, rows=P):
                k = TH_IDX[tile]
                if k >= 2:
                    act.wait_ge(gated, k - 1)
                nc.scalar.activation(TH[0:rows, k % 2, :], src, ACT.Tanh, scale=0.5).then_inc(th_full, 1)

            pending = []

            def read_out(tile):
                if tile is None:
                    return
                kind, j = tile
                t = TILE_IDX[tile]
                bank = GB[t % G_BANKS][:, 0:SEQ]
                wait_tile_full(act, tile)
                if kind in CONV:
                    ci, col = conv_index(kind, j), conv_src(kind, j)
                    if ci >= 2:
                        act.wait_ge(gated, max(v for k, v in TH_IDX.items() if k[0] in CONV and conv_index(*k) == ci - 2) + 1)
                    nc.scalar.activation(ACC[:, ci % 2, :], bank, ACT.Identity, bias=CW[:, 96 + col:97 + col],
                                         scale=CW[:, 4 * col + 3:4 * col + 4]).then_inc(conv_acc, 1)
                if pending:
                    prev = pending.pop()
                    ci = conv_index(*prev)
                    wait_tile_out(act, prev)
                    k = TH_IDX[prev]
                    if k >= 2:
                        act.wait_ge(gated, k - 1)
                    nc.scalar.activation(TH[:, k % 2, :], ACC[:, ci % 2, :], ACT.Tanh).then_inc(th_full, 1)
                if kind in CONV:
                    pending.append(tile)
                elif kind == "dtg":
                    nc.scalar.activation(F0[:], bank, ACT.Identity, bias=par("dt_bias")).then_inc(g_free[t % G_BANKS], 1)
                elif kind in ("z", "za"):
                    tanh_half(tile, bank)
                elif kind in NATIVE:
                    b = int(kind == "w1v")
                    wait_tile_out(act, tile)
                    tanh_half(tile, HID[0:60, b, :], 60)
                elif kind in ("kc", "vc"):
                    nc.scalar.copy(KVC[:, j + 2 * (kind == "vc"), :], bank).then_inc(g_free[t % G_BANKS], 1)
                elif kind in ("vs", "vw"):
                    if kind == "vw":
                        wait_small_full(act, ("vt", 0, 0))
                    else:
                        act.wait_ge(gated, TH_IDX[("w1v", 0)] + 1)
                    nc.scalar.copy(VT[:, j, :], bank).then_inc(g_free[t % G_BANKS], 1)
                elif kind in ("ks", "kw"):
                    for half in range(2):
                        for dup in range(2):
                            nc.scalar.copy(KH[64 * dup:64 * dup + 64, 2 * j + half, int(kind == "kw"), :],
                                           GB[t % G_BANKS][64 * half:64 * half + 64, 0:SEQ]).then_inc(kh_done, 1)
                elif kind == "q":
                    for half in range(2):
                        nc.scalar.mul(QS[0:64, 2 * j + half, :], GB[t % G_BANKS][64 * half:64 * half + 64, 0:SEQ],
                                      HEAD_DIM ** -0.5).then_inc(qh_done, 1)
                elif kind == "mg":
                    nc.scalar.activation(MT[:, j, :], bank, ACT.Tanh, scale=0.5).then_inc(g_free[t % G_BANKS], 1)
                elif kind == "nsa":
                    act.wait_ge(mf_done, j + 1)
                    nc.scalar.copy(MH[:, j, :], MTMP[:, j % 2, 1, :]).then_inc(mh_done, 1)
                elif kind == "out":
                    if j >= 2:
                        act.wait_ge(sqa_done, max(1, j - 2))
                    nc.scalar.activation(SQO[:, j % 2, :], bank, ACT.Square).then_inc(sqo_done, 1)
                    act.wait_ge(gg_done, 1)
                    nc.scalar.mul(OUT[:, j, :], bank, GG[:, 1, j:j + 1]).then_inc(g_free[t % G_BANKS], 1)

            act.wait_ge(x_in, 16)
            nc.scalar.activation(SQX[:], XT[:], ACT.Square).then_inc(sqx_done, 1)
            act.wait_ge(par_in_s, 16)
            nc.scalar.activation(AEX[:], par("a_log"), ACT.Exp).then_inc(a_exp, 1)
            act.wait_ge(eps_made, 2)
            act.wait_ge(ssx_full, 1)
            nc.scalar.activation(RX[:, 0, :], YB[:, 0:SEQ], ACT.Sqrt, bias=EPSC[:, 0:1], scale=1.0 / D_MODEL).then_inc(rx_done, 1)
            split_hi(0)
            act.wait_ge(ada_full, 1)
            nc.scalar.copy(ROWS[:], SB[0][:]).then_inc(rows_done, 1)
            split_hi(1)
            act.wait_ge(ab_done, 1)
            for k in range(KT):
                nc.scalar.activation(HH[:, k, :], XT[:, k, :], ACT.Identity, bias=MOD[:, k:k + 1],
                                     scale=AB[:, k:k + 1]).then_inc(h_hi, 1)
            for n in range(2, AHEAD):
                split_hi(n)
            act.wait_ge(cw_ready, 1)

            done = None
            for step in LATE_STEPS:
                what, i = step
                key = step + (0,)
                bank = TB[T_IDX[key] % 2] if key in T_IDX else None
                release = t_free[T_IDX[key] % 2] if key in T_IDX else None
                if what == "gemm":
                    late_split = done is None or done[0] != "nsa"
                    if late_split:
                        read_out(done)
                    if i + AHEAD in SPLIT_IDX:
                        split_hi(SPLIT_IDX[i + AHEAD])
                    if not late_split:
                        read_out(done)
                    done = finished_tile(i)
                elif what == "flush":
                    read_out(done)
                elif what == "dtT":
                    wait_small_full(act, key)
                    nc.scalar.copy(DTT[:], bank[:, 0:2 * P].rearrange("p (c f) -> p c f", c=2)).then_inc(release, 1)
                    wait_small_out(act, key)
                    nc.scalar.activation(GATE[:], DTT[:, :, GATE_ROW:GATE_ROW + 48].rearrange("p c (h n) -> p c h n", n=3),
                                         ACT.Tanh, scale=0.5).then_inc(gate_tanh, 1)
                elif what == "dtE":
                    act.wait_ge(abs_done, 1)
                    nc.scalar.activation(DTW[:, 2], DTW[:, 0], ACT.Exp, scale=-1.0).then_inc(dt_exp, 1)
                elif what == "dtL":
                    act.wait_ge(dt_u, 1)
                    nc.scalar.activation(DTW[:, 4], DTW[:, 3], ACT.Ln).then_inc(dt_ln, 1)
                    act.wait_ge(dt_ln, 1)
                    nc.scalar.activation(DTW[:, 5], DTW[:, 4], ACT.Exp, scale=-1.0).then_inc(dt_inv, 1)
                elif what == "acs":
                    wait_small_full(act, key)
                    nc.scalar.activation(DS[:], bank[:, 256:256 + SSM_HEADS], ACT.Exp)
                    nc.scalar.copy(HI4[:], bank[:, 0:2 * P].rearrange("p (c l) -> p c l", c=2)).then_inc(hi4_done, 1)
                elif what == "bt":
                    wait_small_full(act, key)
                    nc.scalar.copy(BTOK[:].rearrange("p g n -> p (g n)"), bank[:, :]).then_inc(release, 1)
                elif what == "cb":
                    wait_small_full(act, key)
                    nc.scalar.copy(CB[:, 2 * i:2 * i + 2, :, :].rearrange("p g c l -> p (g c l)"), bank[:, :]).then_inc(release, 1)
                elif what == "st":
                    wait_small_full(act, key)
                    if i >= 1:
                        wait_y_full(act, ("y", 2 * i - 1))
                    nc.scalar.copy(STA[:], bank[:, :]).then_inc(release, 1)
                elif what == "seg":
                    n = S_IDX[step]
                    for c in range(2):
                        act.wait_ge(s_full[c], n + 1)
                        if i >= 1:
                            act.wait_ge(mm_done[c], i)
                        nc.scalar.activation(EX[:, c, :, :].rearrange("p j l -> p (j l)"), SB[c][:, :],
                                             ACT.Exp).then_inc(s_free[c], 1)
                elif what == "ea":
                    wait_small_full(act, key)
                    if i >= 1:
                        act.wait_ge(ce_done, i)
                    nc.scalar.activation(EA[:].rearrange("p j l -> p (j l)"), bank[:, :], ACT.Exp).then_inc(release, 1)
                elif what == "ysq":
                    act.wait_ge(ypre_done, 2 * (i + 1))
                    if i >= 1:
                        wait_small_full(act, ("ssq", i - 1, 0))
                    nc.scalar.activation(SQ[:], Z[:, TPG * i:TPG * (i + 1), :], ACT.Square).then_inc(ysq_done, 1)
                elif what == "ssq":
                    wait_small_full(act, key)
                    if i >= 1:
                        act.wait_ge(recip_done, i)
                    nc.scalar.activation(RN[:, 0, :], bank[:, 0:SEQ], ACT.Sqrt, bias=EPSC[:, 1:2],
                                         scale=SSM_GROUPS / D_INNER).then_inc(release, 1)
                elif what == "ynhi":
                    act.wait_ge(ynf_done, i + 1)
                    nc.scalar.copy(YNH[:, i, :], YT[:, i % 2, :]).then_inc(ynh_done, 1)
                elif what == "hidT":
                    wait_small_full(act, key)
                    if i == 0:
                        nc.scalar.mul(HIDK[:].rearrange("p k n -> p (k n)"), bank[:, 0:120], 0.5).then_inc(release, 1)
                    else:
                        wait_zeros(act, "hid_v")
                        for k in range(2):
                            src = bank[:, 60 * k:60 * k + 60].rearrange("p (g j) -> p g j", g=KV_GROUPS).unsqueeze(2)
                            last = nc.scalar.mul(HVR[:, k, :, :, 0:N_CMP], src.to_broadcast([P, KV_GROUPS, 4, N_CMP]), 0.5)
                        last.then_inc(release, 1)
                elif what == "kcp":
                    wait_small_full(act, key)
                    wait_zeros(act, "k_cmp")
                    nc.scalar.copy(KC[:, :, 0:N_CMP], bank[:, 0:60].rearrange("p (g j) -> p g j", g=KV_GROUPS)).then_inc(kch_done, 1)
                elif what == "vcp":
                    wait_small_full(act, key)
                    wait_zeros(act, "v_cmp")
                    for hh in range(4):
                        rows = slice(32 * hh, 32 * hh + 32)
                        last = nc.scalar.copy(VC[rows, :, hh // 2, 64 * (hh % 2):64 * (hh % 2) + 64],
                                              bank[rows, 0:256].rearrange("p (g d) -> p g d", g=KV_GROUPS))
                    last.then_inc(release, 1)
                elif what == "vt":
                    wait_small_full(act, key)
                    nc.scalar.copy(V[:, i, :, :, :].rearrange("p k g d -> p (k g d)"), bank[:, :]).then_inc(release, 1)
                elif what == "cs" and i == 1:
                    act.wait_ge(cs_sub, 1)
                    nc.scalar.activation(CSW[:], CSW[:], ACT.Exp).then_inc(cs_exp, 1)
                elif what == "ct":
                    wait_small_full(act, key)
                    nc.scalar.copy(PCT[:, 2 * i:2 * i + 2, :].rearrange("p g q -> p (g q)"), bank[:, :]).then_inc(release, 1)
                elif what == "ex":
                    k = i % 2
                    if i >= 2:
                        wait_small_full(act, ("pt", i - 2, 1))
                    for qt in range(2):
                        act.wait_ge(max_done, 2 * i + qt + 1)
                        nk = P * (qt + 1)
                        for b in range(2):
                            c = 2 * qt + b
                            last = nc.scalar.activation(E[:, k, b, P * qt:P * qt + nk], SB[qt][:, nk * b:nk * b + nk], ACT.Exp,
                                                        bias=SM[:, k, 0, c:c + 1], accum_out=SM[:, k, 1, c:c + 1])
                        last.then_inc(s_free[qt], 1)
                elif what == "pt":
                    wait_small_full(act, key)
                    if i >= 2:
                        wait_y_full(act, ("pv", i // 2 - 1))
                    nc.scalar.copy(PT[:, i % 2, :, 0:SEQ], bank[:, :].rearrange("p (b q) -> p b q", b=2)).then_inc(release, 1)
                elif what == "osp":
                    wait_y_out(act, ("pv", i))
                    nc.scalar.copy(OH[:, i, :], ZA[:, i, :]).then_inc(oh_done, 1)
                elif what == "kpos":
                    act.wait_ge(al2_in, 16)
                    wait_zeros(act, "k_lo")
                    keys = ALK[0:6].unsqueeze(1).to_broadcast([6, KV_GROUPS, 2, SEQ])
                    nc.scalar.copy(KL[64:70], keys).then_inc(kl_alibi, 1)
                elif what == "agR":
                    wait_zeros(act, "rows2")
                    act.wait_ge(native_mm, NATIVE_IDX[UNITS.index(("ag", 0, KT - 1))] + 1)
                    for j in range(4):
                        nc.scalar.copy(ROWS2[32 * j:32 * j + 1, :], YB[32 * j:32 * j + 1, 0:256]).then_inc(rows2_done, 1)
            act.wait_ge(osq_full, 1)
            nc.scalar.activation(RF[:, 0, :], YB[:, 0:SEQ], ACT.Sqrt, bias=EPSC[:, 1:2], scale=1.0 / D_MODEL).then_inc(rf_done, 1)

        @block.vector
        def _(dve):
            count = [0]

            def link(ins):
                count[0] += 1
                ins.then_inc(dve_seq, 1)
                dve.wait_ge(dve_seq, count[0])

            def split_lo(n):
                u = SPLIT_UNITS[n]
                dve.wait_ge(hi_ready, n + 1)
                if n >= LO_SLOTS:
                    dve.wait_ge(unit_mm, n - LO_SLOTS + 1)
                c = P * lo_share(n)
                nc.vector.tensor_tensor(WL[:, n % LO_SLOTS, 0:c], RAW[:, u % RAW_SLOTS, 0:c], WH[:, n % HI_SLOTS, 0:c],
                                        ALU.subtract).then_inc(lo_ready, 1)

            def gate(tile, out_ap, src, rows=P):
                k = TH_IDX[tile]
                dve.wait_ge(th_full, k + 1)
                if tile[0] in CONV:
                    wait_tile_out(dve, tile)
                nc.vector.scalar_tensor_tensor(out_ap, TH[0:rows, k % 2, :], 1.0, src, ALU.add, ALU.mult).then_inc(gated, 1)

            pending = []

            def read_out(tile):
                if tile is None:
                    return
                kind, j = tile
                t = TILE_IDX[tile]
                bank = GB[t % G_BANKS][:, 0:SEQ]
                if kind in CONV:
                    ci, col = conv_index(kind, j), conv_src(kind, j)
                    dve.wait_ge(conv_acc, ci + 1)
                    for tap in (2, 1, 0):
                        s = 3 - tap
                        ins = nc.vector.scalar_tensor_tensor(ACC[:, ci % 2, s:SEQ], GB[t % G_BANKS][:, 0:SEQ - s],
                                                             CW[:, 4 * col + tap:4 * col + tap + 1], ACC[:, ci % 2, s:SEQ],
                                                             ALU.mult, ALU.add)
                        if tap:
                            link(ins)
                        else:
                            ins.then_inc(g_free[t % G_BANKS], 1)
                if pending:
                    prev = pending.pop()
                    ci = conv_index(*prev)
                    if prev[0] == "x" and prev[1] >= 2 * TPG:
                        wait_small_full(dve, ("xt", (prev[1] // TPG - 2, 1), 0))
                        wait_y_out(dve, ("y", 2 * (prev[1] // TPG - 2) + 1))
                    gate(prev, conv_dst(*prev), ACC[:, ci % 2, :])
                if kind in CONV:
                    pending.append(tile)
                elif kind in ("z", "za"):
                    gate(tile, (Z if kind == "z" else ZA)[:, j, :], bank)
                elif kind in NATIVE:
                    hid = HID[0:60, int(kind == "w1v"), :]
                    wait_tile_full(dve, tile)
                    link(nc.vector.tensor_copy(hid, GB[t % G_BANKS][64:124, 0:CMP_HIDDEN]))
                    nc.vector.tensor_tensor(hid, GB[t % G_BANKS][0:60, 0:CMP_HIDDEN], hid,
                                            ALU.add).then_inc(g_free[t % G_BANKS], 1)
                    gate(tile, hid, hid, 60)
                elif kind in ("ks", "kw"):
                    br = int(kind == "kw")
                    for half in range(2):
                        dve.wait_ge(kh_done, 8 * br + 4 * j + 4)
                        last = nc.vector.tensor_tensor(KL[0:64, 2 * j + half, br, :], GB[t % G_BANKS][64 * half:64 * half + 64, 0:SEQ],
                                                       KH[0:64, 2 * j + half, br, :], ALU.subtract)
                    last.then_inc(g_free[t % G_BANKS], 1)
                elif kind == "q":
                    for half in range(2):
                        dve.wait_ge(qh_done, 2 * j + 2)
                        last = nc.vector.scalar_tensor_tensor(QS[64:128, 2 * j + half, :], GB[t % G_BANKS][64 * half:64 * half + 64, 0:SEQ],
                                                              HEAD_DIM ** -0.5, QS[0:64, 2 * j + half, :], ALU.mult, ALU.subtract)
                    last.then_inc(g_free[t % G_BANKS], 1)
                elif kind == "ssm":
                    wait_tile_full(dve, tile)
                    if j == 0:
                        wait_small_full(dve, ("ct", 1, 0))
                    nc.vector.scalar_tensor_tensor(YS[:, j, :], MT[:, j, :], 1.0, bank, ALU.add, ALU.mult).then_inc(g_free[t % G_BANKS], 1)
                elif kind == "nsa":
                    wait_tile_full(dve, tile)
                    if j >= 2:
                        dve.wait_ge(ml_done, j - 1)
                    nc.vector.scalar_tensor_tensor(MTMP[:, j % 2, 0, :], MT[:, 8 + j, :], 1.0, bank, ALU.add,
                                                   ALU.mult).then_inc(g_free[t % G_BANKS], 1)
                    wait_tile_out(dve, tile)
                    nc.vector.tensor_tensor(MTMP[:, j % 2, 1, :], MTMP[:, j % 2, 0, :], YS[:, j, :], ALU.add).then_inc(mf_done, 1)
                    for m in ([j - 1] if j else []) + ([7] if j == 7 else []):
                        dve.wait_ge(mh_done, m + 1)
                        nc.vector.tensor_tensor(ML[:, m, :], MTMP[:, m % 2, 1, :], MH[:, m, :], ALU.subtract).then_inc(ml_done, 1)

            nc.vector.memset(SB[0][:], 0.0).then_inc(bank_zeroed, 1)
            dve.wait_ge(par_in_s, 16)
            nc.vector.tensor_scalar(CW[:], PR[:, PAR["conv_w"][0]:PAR["conv_b"][1]], 0.5, None, ALU.mult).then_inc(cw_ready, 1)
            dve.wait_ge(rx_done, 1)
            link(nc.vector.reciprocal(RX[:, 1, :], RX[:, 0, :]))
            link(nc.vector.tensor_tensor(XT[:], XT[:], RX[:, 1, :].unsqueeze(1).to_broadcast([P, KT, SEQ]), ALU.mult))
            split_lo(0)
            dve.wait_ge(modT_full, 1)
            rows = SB[1][:, :].rearrange("p (m j r) -> p j m r", m=4, j=4)[:, :, :, 0]
            link(nc.vector.tensor_tensor(MOD[:].rearrange("p (j m) -> p j m", j=4), rows,
                                         par("b_ada", 0, 16).rearrange("p (j m) -> p j m", j=4), ALU.add))
            nc.vector.scalar_tensor_tensor(AB[:, 0:8], MOD[:, 8:16], 1.0, par("g_pre"), ALU.add, ALU.mult).then_inc(ab_done, 1)
            dve.wait_ge(ab_done, 1)
            for k in range(KT):
                if k not in H_POOL:
                    nc.vector.tensor_scalar(HF[:, k, :], XT[:, k, :], AB[:, k:k + 1], MOD[:, k:k + 1], ALU.mult,
                                            ALU.add).then_inc(h_f32, 1)
                if k >= 1:
                    dve.wait_ge(h_hi, k)
                    if k - 1 in H_POOL:
                        dve.wait_ge(h_f32_pool, H_POOL.index(k - 1) + 1)
                    else:
                        dve.wait_ge(h_f32, k - sum(m < k - 1 for m in H_POOL))
                    nc.vector.tensor_tensor(HL[:, k - 1, :], HF[:, k - 1, :], HH[:, k - 1, :], ALU.subtract).then_inc(h_ready, 1)
            dve.wait_ge(h_hi, KT)
            dve.wait_ge(h_f32, KT - len(H_POOL))
            nc.vector.tensor_tensor(HL[:, KT - 1, :], HF[:, KT - 1, :], HH[:, KT - 1, :], ALU.subtract).then_inc(h_ready, 1)
            for n in range(1, AHEAD):
                split_lo(n)

            done = None
            for step in LATE_STEPS:
                what, i = step
                key = step + (0,)
                bank = TB[T_IDX[key] % 2] if key in T_IDX else None
                release = t_free[T_IDX[key] % 2] if key in T_IDX else None
                if what == "gemm":
                    read_out(done)
                    done = finished_tile(i)
                    if i + AHEAD in SPLIT_IDX:
                        split_lo(SPLIT_IDX[i + AHEAD])
                elif what == "flush":
                    read_out(done)
                elif what == "acs":
                    dve.wait_ge(hi4_done, 1)
                    dve.wait_ge(adt_done, 2)
                    dve.wait_ge(consts_made, 7)
                    acs = bank[:, 0:2 * P].rearrange("p (c l) -> p c l", c=2)
                    nc.vector.tensor_copy(TP[0:32], HI4[0:32]).then_inc(cols_ready, 1)
                    nc.vector.tensor_tensor(TP[32:64], acs[32:64], HI4[32:64], ALU.subtract).then_inc(cols_ready, 1)
                    nc.vector.tensor_copy(ST[64:96], HI4[64:96]).then_inc(cols_ready, 1)
                    nc.vector.tensor_tensor(ST[96:128], acs[96:128], HI4[96:128], ALU.subtract).then_inc(cols_ready, 1)
                    nc.vector.tensor_copy(EPSC[0:1, 2:3], bank[0:1, 0:1]).then_inc(release, 1)
                elif what == "xt":
                    g, c = i
                    wait_small_full(dve, key)
                    if g >= 1:
                        wait_y_full(dve, ("y", 2 * g - 1))
                    if c == 0 and g >= 1:
                        dve.wait_ge(xds_done, g)
                    dt = DT[:, c, HPC * g:HPC * (g + 1)].unsqueeze(2).to_broadcast([P, HPC, HEAD_DIM])
                    nc.vector.tensor_tensor(XDT[:, c, :, :], bank[:, :].rearrange("p (h d) -> p h d", h=HPC), dt,
                                            ALU.mult).then_inc(release, 1)
                elif what == "seg":
                    dve.wait_ge(s_free[0], S_IDX[step] + 1)
                    if i >= 1:
                        wait_y_full(dve, ("y", i - 1))
                    wait_small_out(dve, ("cb", i // 4, 0))
                    nc.vector.tensor_tensor(MM[:, 0, :, :], EX[:, 0, :, :], CB[:, i // 2, 0, :].unsqueeze(1).to_broadcast([P, 4, P]),
                                            ALU.mult).then_inc(mm_done[0], 1)
                elif what == "y":
                    wait_y_full(dve, step)
                    for t in (2 * i, 2 * i + 1):
                        x = XG[:, (t // TPG) % 2, t % TPG, :]
                        last = nc.vector.scalar_tensor_tensor(x, x, par("d_skip", t, t + 1), YB[:, SEQ * (t % 2):SEQ * (t % 2 + 1)],
                                                              ALU.mult, ALU.add)
                    last.then_inc(y_free, 1)
                    wait_y_out(dve, step)
                    x2 = XG[:, (i // 2) % 2, 2 * (i % 2):2 * (i % 2) + 2, :]
                    nc.vector.tensor_tensor(Z[:, 2 * i:2 * i + 2, :], x2, Z[:, 2 * i:2 * i + 2, :], ALU.mult).then_inc(ypre_done, 1)
                elif what == "yn":
                    if i % TPG == 0:
                        wait_small_out(dve, ("ssq", i // TPG, 0))
                        nc.vector.reciprocal(RN[:, 1, :], RN[:, 0, :]).then_inc(recip_done, 1)
                        dve.wait_ge(recip_done, i // TPG + 1)
                        dve.wait_ge(ysq_done, i // TPG + 1)
                    if i >= 2:
                        dve.wait_ge(yn_done, i - 1)
                    nc.vector.scalar_tensor_tensor(YT[:, i % 2, :], Z[:, i, :], par("g_ssm", i, i + 1), RN[:, 1, :], ALU.mult,
                                                   ALU.mult).then_inc(ynf_done, 1)
                elif what == "ynlo":
                    dve.wait_ge(ynh_done, i + 1)
                    nc.vector.tensor_tensor(YNL[:, i, :], YT[:, i % 2, :], YNH[:, i, :], ALU.subtract).then_inc(yn_done, 1)
                elif what == "blk" and i == 0:
                    compress_blocks(dve, nc.vector, 0)
                elif what == "kcp":
                    dve.wait_ge(kch_done, 1)
                    nc.vector.tensor_tensor(KC[:, :, 16:16 + N_CMP], bank[:, 0:60].rearrange("p (g j) -> p g j", g=KV_GROUPS),
                                            KC[:, :, 0:N_CMP], ALU.subtract).then_inc(release, 1)
                elif what == "cs":
                    wait_small_full(dve, key)
                    dve.wait_ge(cbias_in, 16)
                    sc = bank[:, :].rearrange("p (h n j) -> p h n j", h=ATT_HEADS, n=2)
                    bias = CBI[:, 0:512].rearrange("p (t h j) -> p t h j", t=2, h=ATT_HEADS)[:, i]
                    link(nc.vector.tensor_tensor(CSW[:, i], sc[:, :, 1, :], bias, ALU.add))
                    nc.vector.tensor_tensor(CSW[:, i], sc[:, :, 0, :], CSW[:, i], ALU.add).then_inc(release, 1)
                    wait_small_out(dve, key)
                    if i == 0:
                        continue
                    link(nc.vector.tensor_reduce(CSM[:, 0], CSW[:], AX.X, ALU.max))
                    nc.vector.tensor_tensor(CSW[:], CSW[:], CSM[:, 0].unsqueeze(3).to_broadcast([P, 2, ATT_HEADS, 16]),
                                            ALU.subtract).then_inc(cs_sub, 1)
                elif what == "cs2":
                    dve.wait_ge(cs_exp, 1)
                    wait_zeros(dve, "p_cmp")
                    link(nc.vector.tensor_reduce(CSM[:, 1], CSW[:], AX.X, ALU.add))
                    link(nc.vector.reciprocal(CSM[:, 2], CSM[:, 1]))
                    nc.vector.tensor_tensor(CSM[:, 0], CSM[:, 2], GATE[:, :, :, 0], ALU.mult)
                    valid = CBI[:, 512:544].rearrange("p (t j) -> p t j", t=2).unsqueeze(2).to_broadcast([P, 2, ATT_HEADS, 16])
                    link(nc.vector.tensor_tensor(CSW[:], CSW[:], valid, ALU.mult))
                    nc.vector.tensor_tensor(PC[:, :, :, 0:16], CSW[:], CSM[:, 0].unsqueeze(3).to_broadcast([P, 2, ATT_HEADS, 16]),
                                            ALU.mult).then_inc(pc_done, 1)
                elif what == "sc":
                    n, k = S_IDX[step], i % 2
                    for qt in range(2):
                        dve.wait_ge(s_full[qt], n + 1)
                        nk = P * (qt + 1)
                        nc.vector.tensor_reduce(SM[:, k, 0, 2 * qt:2 * qt + 2], SB[qt][:, 0:2 * nk].rearrange("p (b n) -> p b n", b=2),
                                                AX.X, ALU.max, negate=True).then_inc(max_done, 1)
                elif what == "ps":
                    n, k = S_IDX[("sc", i)], i % 2
                    dve.wait_ge(s_free[0], n + 1)
                    dve.wait_ge(s_free[1], n + 1)
                    link(nc.vector.reciprocal(SM[:, k, 2, :], SM[:, k, 1, :]))
                    link(nc.vector.tensor_tensor(SM[:, k, 3, :].rearrange("p (t b) -> p t b", t=2),
                                                 SM[:, k, 2, :].rearrange("p (t b) -> p t b", t=2), GATE[:, :, i, 1:3], ALU.mult))
                    for qt in range(2):
                        for b in range(2):
                            e = E[:, k, b, P * qt:P * qt + P * (qt + 1)]
                            nc.vector.tensor_scalar(e, e, SM[:, k, 3, 2 * qt + b:2 * qt + b + 1], None, ALU.mult).then_inc(p_done, 1)
                elif what == "pt":
                    key1 = step + (1,)
                    wait_small_full(dve, key1)
                    if i >= 2:
                        wait_y_full(dve, ("pv", i // 2 - 1))
                    nc.vector.tensor_copy(PT[:, i % 2, :, SEQ:SEQ + P],
                                          TB[T_IDX[key1] % 2][:, 0:SEQ].rearrange("p (b q) -> p b q", b=2)
                                          ).then_inc(t_free[T_IDX[key1] % 2], 1)
                elif what == "pv":
                    wait_y_full(dve, step)
                    dve.wait_ge(gated, TH_IDX[("za", i)] + 1)
                    nc.vector.tensor_tensor(ZA[:, i, :], ZA[:, i, :], YB[:, 0:SEQ], ALU.mult).then_inc(y_free, 1)
                elif what == "osp":
                    dve.wait_ge(oh_done, i + 1)
                    nc.vector.tensor_tensor(OL[:, i, :], ZA[:, i, :], OH[:, i, :], ALU.subtract).then_inc(o_split, 1)
                elif what == "agT":
                    wait_small_full(dve, key)
                    rows = bank[:, 0:2 * P].rearrange("p (m j r) -> p j m r", m=2, j=4)[:, :, :, 0]
                    nc.vector.tensor_tensor(GG[:, 0, :].rearrange("p (j m) -> p j m", j=4), rows,
                                            par("b_ada", 16, 24).rearrange("p (j m) -> p j m", j=4), ALU.add).then_inc(release, 1)
                    wait_small_out(dve, key)
                    nc.vector.tensor_tensor(GG[:, 1, :], GG[:, 0, :], par("g_post"), ALU.mult).then_inc(gg_done, 1)
            dve.wait_ge(rf_done, 1)
            nc.vector.reciprocal(RF[:, 1, :], RF[:, 0, :]).then_inc(rf_done, 1)
            dve.wait_ge(rf_done, 2)
            dve.wait_ge(xr_in, 16)
            wait_tile_out(dve, ("out", 6))
            wait_tile_out(dve, ("out", 7))
            for m in range(0, FINAL_DVE, 2):
                r = RF[:, 1, :].unsqueeze(1).to_broadcast([P, 2, SEQ])
                link(nc.vector.tensor_tensor(OUT[:, m:m + 2, :], OUT[:, m:m + 2, :], r, ALU.mult))
                nc.vector.tensor_tensor(OUT[:, m:m + 2, :], OUT[:, m:m + 2, :], XR[:, m:m + 2, :], ALU.add).then_inc(fin_done[0], 1)

        @block.gpsimd
        def _(pool):
            made, made_rest = [0], [0]

            def link(ins):
                made[0] += 1
                ins.then_inc(pool_seq, 1)
                pool.wait_ge(pool_seq, made[0])

            nc.gpsimd.memset(EPSC[:, 0:1], EPS).then_inc(eps_made, 1)
            nc.gpsimd.memset(EPSC[:, 1:2], 4.0 * EPS).then_inc(eps_made, 1)
            for n, (ap, value) in enumerate(((ST[0:64].bitcast(f32), 1.0), (TP[64:128], -1.0), (ONZ[0:64].bitcast(f32), 1.0),
                                             (ONZ[64:128].bitcast(f32), 0.0))):
                nc.gpsimd.memset(ap, value).then_inc(consts_made, 1)
                pool.wait_ge(consts_made, n + 1)
            pool.wait_ge(cst_in_s, 16)
            pool.wait_ge(cst2_in_s, 16)
            nc.gpsimd.tensor_copy(IDB[:], cst("ident")).then_inc(consts_made, 1)
            nc.gpsimd.tensor_copy(MSL[:], cst("mask_sl")).then_inc(consts_made, 1)
            nc.gpsimd.tensor_copy(MQK[:], cst("mask_qk")).then_inc(consts_made, 1)

            pool.wait_ge(ab_done, 1)
            for k in H_POOL:
                nc.gpsimd.tensor_scalar(HF[:, k, :], XT[:, k, :], AB[:, k:k + 1], MOD[:, k:k + 1], ALU.mult,
                                        ALU.add).then_inc(h_f32_pool, 1)

            def split_lo_rest(n):
                u, c = SPLIT_UNITS[n], P * lo_share(n)
                made_rest[0] = n + 1
                pool.wait_ge(hi_ready, n + 1)
                if n >= LO_SLOTS:
                    pool.wait_ge(unit_mm, n - LO_SLOTS + 1)
                nc.gpsimd.tensor_tensor(WL[:, n % LO_SLOTS, c:1024], RAW[:, u % RAW_SLOTS, c:1024], WH[:, n % HI_SLOTS, c:1024],
                                        ALU.subtract).then_inc(lo_rest_ready, 1)

            for n in range(AHEAD):
                split_lo_rest(n)

            def moving_rows(quad):
                for c in range(2):
                    oh = cst("onehot", 4 * quad, 4 * quad + 4).unsqueeze(2).to_broadcast([P, 4, P])
                    nc.gpsimd.tensor_tensor(MV[:, c, :, :], TP[:, c, :].unsqueeze(1).to_broadcast([P, 4, P]), oh,
                                            ALU.mult).then_inc(mv_done, 1)

            for step in STEPS:
                what, i = step
                key = step + (0,)
                if what == "gemm":
                    if i + AHEAD in SPLIT_IDX:
                        split_lo_rest(SPLIT_IDX[i + AHEAD])
                elif what == "dtA":
                    wait_small_out(pool, ("dtT", 0, 0))
                    x = DTT[:, :, 0:SSM_HEADS]
                    link(nc.gpsimd.tensor_scalar(DTW[:, 1], x, 0.0, None, ALU.max))
                    link(nc.gpsimd.tensor_scalar(DTW[:, 0], DTW[:, 1], 2.0, None, ALU.mult))
                    nc.gpsimd.tensor_tensor(DTW[:, 0], DTW[:, 0], x, ALU.subtract).then_inc(abs_done, 1)
                    pool.wait_ge(gate_tanh, 1)
                    nc.gpsimd.tensor_scalar(GATE[:], GATE[:], 0.25, 0.25, ALU.mult, ALU.add).then_inc(adt_done, 1)
                elif what == "dtB":
                    pool.wait_ge(dt_exp, 1)
                    nc.gpsimd.tensor_scalar(DTW[:, 3], DTW[:, 2], 1.0, None, ALU.add).then_inc(dt_u, 1)
                elif what == "dtC":
                    pool.wait_ge(dt_u, 1)
                    link(nc.gpsimd.tensor_scalar(DT[:], DTW[:, 3], 1.0, None, ALU.subtract))
                    link(nc.gpsimd.tensor_tensor(DT[:], DTW[:, 2], DT[:], ALU.subtract))
                    pool.wait_ge(dt_inv, 1)
                    link(nc.gpsimd.tensor_tensor(DT[:], DT[:], DTW[:, 5], ALU.mult))
                    link(nc.gpsimd.tensor_tensor(DT[:], DT[:], DTW[:, 1], ALU.add))
                    link(nc.gpsimd.tensor_tensor(DT[:], DT[:], DTW[:, 4], ALU.add))
                    pool.wait_ge(a_exp, 1)
                    link(nc.gpsimd.tensor_tensor(DTW[:, 0], DT[:], AEX[:].unsqueeze(1).to_broadcast([P, 2, SSM_HEADS]), ALU.mult))
                    nc.gpsimd.tensor_scalar(ADT4[:], DTW[:, 0].unsqueeze(2).to_broadcast([P, 2, 4, SSM_HEADS]), -1.0, None,
                                            ALU.mult).then_inc(adt_done, 1)
                elif what == "acs":
                    pool.wait_ge(cols_ready, 4)
                    moving_rows(0)
                elif what == "xt" and i[1] == 0:
                    g = i[0]
                    wait_small_out(pool, key)
                    if g >= 1:
                        wait_small_full(pool, ("st", g - 1, 0))
                    pool.wait_ge(hi4_done, 1)
                    nc.gpsimd.tensor_tensor(XDS[:], XDT[:, 0, :, :],
                                            DS[:, HPC * g:HPC * (g + 1)].unsqueeze(2).to_broadcast([P, HPC, HEAD_DIM]),
                                            ALU.mult).then_inc(xds_done, 1)
                elif what == "seg":
                    pool.wait_ge(s_free[1], S_IDX[step] + 1)
                    if i >= 1:
                        wait_y_full(pool, ("y", i - 1))
                    wait_small_out(pool, ("cb", i // 4, 0))
                    nc.gpsimd.tensor_tensor(MM[:, 1, :, :], EX[:, 1, :, :], CB[:, i // 2, 1, :].unsqueeze(1).to_broadcast([P, 4, P]),
                                            ALU.mult).then_inc(mm_done[1], 1)
                elif what == "osum":
                    pool.wait_ge(sqo_done, i + 1)
                    if i >= 2:
                        pool.wait_ge(sqa_done, i - 1)
                    first = SQO[:, 0, :] if i == 1 else SQA[:]
                    nc.gpsimd.tensor_tensor(SQA[:], first, SQO[:, i % 2, :], ALU.add).then_inc(sqa_done, 1)
                elif what == "ysum":
                    pool.wait_ge(ysq_done, i + 1)
                    link(nc.gpsimd.tensor_tensor(SQ[:, 0:2, :], SQ[:, 0:2, :], SQ[:, 2:4, :], ALU.add))
                    nc.gpsimd.tensor_tensor(SQ[:, 0, :], SQ[:, 0, :], SQ[:, 1, :], ALU.add).then_inc(ysum_done, 1)
                elif what == "ea":
                    wait_small_out(pool, key)
                    g = i // 2
                    nc.gpsimd.tensor_tensor(CE[:], EA[:], CTT[:, g, CHUNK:SEQ].unsqueeze(1).to_broadcast([P, 4, P]),
                                            ALU.mult).then_inc(ce_done, 1)
                    if i + 1 < QUADS:
                        moving_rows(i + 1)
                elif what == "blk" and i == 1:
                    nc.gpsimd.memset(HVR[:], 0.0).then_inc(zeros, 1)
                    compress_blocks(pool, nc.gpsimd, 1)
                    pool.wait_ge(blk_done[0], 16)
                    nc.gpsimd.memset(VC[:], 0.0).then_inc(zeros, 1)
                    nc.gpsimd.memset(KC[:].bitcast(f32), 0.0).then_inc(zeros, 1)
                elif what == "zero":
                    wait_y_full(pool, ("y", 7))
                    nc.gpsimd.memset(PC[:], 0.0).then_inc(zeros, 1)
                    nc.gpsimd.memset(ROWS2[:], 0.0).then_inc(zeros, 1)
                    wait_zeros(pool, "rows2")
                    nc.gpsimd.memset(Q2[64:128].bitcast(f32), 0.0).then_inc(zeros, 1)
                    wait_zeros(pool, "q2")
                    nc.gpsimd.memset(KL[64:128].bitcast(f32), 0.0).then_inc(zeros, 1)
                    wait_zeros(pool, "k_lo")
                elif what == "q2":
                    pool.wait_ge(qh_done, 2 * (i // 2) + 2)
                    if i >= 2:
                        pool.wait_ge(s_full[1], S_IDX[("sc", i - 2)] + 1)
                    if i == 0:
                        pool.wait_ge(al_in, 16)
                    pool.wait_ge(lo_rest_ready, made_rest[0])
                    link(nc.gpsimd.tensor_copy(Q2[64:70, i % 2, :], ALQ[0:6, SEQ * i:SEQ * i + SEQ]))
                    nc.gpsimd.tensor_copy(Q2[0:64, i % 2, :], QS[0:64, i, :]).then_inc(q2_done, 1)
                    pool.wait_ge(q2_done, i + 1)
            pool.wait_ge(rf_done, 2)
            pool.wait_ge(xr_in, 16)
            wait_tile_out(pool, ("out", 6))
            wait_tile_out(pool, ("out", 7))
            r = RF[:, 1, :].unsqueeze(1).to_broadcast([P, KT - FINAL_DVE, SEQ])
            link(nc.gpsimd.tensor_tensor(OUT[:, FINAL_DVE:KT, :], OUT[:, FINAL_DVE:KT, :], r, ALU.mult))
            nc.gpsimd.tensor_tensor(OUT[:, FINAL_DVE:KT, :], OUT[:, FINAL_DVE:KT, :], XR[:, FINAL_DVE:KT, :],
                                    ALU.add).then_inc(fin_done[1], 1)


def host_constants():
    f = np.float32
    i = np.arange(P)
    onehot = (i[:, None] % SSM_HEADS == np.arange(SSM_HEADS)[None, :]).astype(f)
    slopes = (2.0 ** (-8.0 * np.arange(1, ATT_HEADS + 1) / ATT_HEADS)).astype(f)
    t = np.arange(SEQ).reshape(2, P).T
    end = np.arange(16) * CMP_STRIDE + CMP_BLOCK - 1
    dist = (t[:, :, None] - end[None, None, :]).astype(f)
    valid = (dist >= 0) & (np.arange(16) < N_CMP)[None, None, :]
    bias = np.where(valid[:, :, None, :], -slopes[None, None, :, None] * dist[:, :, None, :], f(NEG)).astype(f)
    parts = {"ident": np.eye(P), "tri": i[:, None] <= i[None, :], "tri_strict": i[:, None] > i[None, :],
             "ones": np.ones((P, P)), "mask_sl": np.where(i[None, :] < i[:, None], NEG, 0.0),
             "mask_qk": np.where(i[None, :] > i[:, None], NEG, 0.0), "onehot": onehot}
    consts = np.concatenate([np.asarray(parts[n], f).reshape(P, -1) for n in CST if n != "end"], axis=1)
    cmp_bias = np.concatenate([bias.reshape(P, -1), valid.reshape(P, -1).astype(f)], axis=1)

    def bf16_bits(v):
        out, rest = [], v.astype(f)
        for _ in range(3):
            bits = rest.view(np.uint32) & np.uint32(0xFFFF0000)
            out.append((bits >> 16).astype(np.uint16))
            rest = (rest - bits.view(f)).astype(f)
        return out

    alibi_q = np.zeros((P, ATT_HEADS, SEQ), np.uint16)
    alibi_k = np.zeros((P, 2, SEQ), np.uint16)
    pos = np.arange(SEQ, dtype=f)
    for n, bits in enumerate(bf16_bits(np.repeat(slopes[:, None], SEQ, 1).copy())):
        alibi_q[n] = bits
        alibi_k[n] = (pos.view(np.uint32) >> 16).astype(np.uint16)[None, :]
    for n, bits in enumerate(bf16_bits((-slopes[:, None] * pos[None, :]).astype(f))):
        alibi_q[3 + n] = bits
        alibi_k[3 + n] = np.uint16(0x3F80)
    return consts, cmp_bias, alibi_q.reshape(P, -1)[0:6], alibi_k[0:6]


def lay_out(inputs):
    w = {k: np.asarray(v) for k, v in inputs.items()}
    f = np.float32

    def cols(v, n):
        return v.reshape(n, P).T

    def tile_of(m):
        k, n = m.shape
        return m.reshape(k // P, P, n // P, P).transpose(2, 1, 0, 3)

    w_in = w["w_in"][0]
    lens = {"z": (OFF_Z, D_INNER), "x": (OFF_X, D_INNER), "b": (OFF_B, 512), "c": (OFF_C, 512), "q": (OFF_Q, 1024),
            "kc": (OFF_KV, 256), "vc": (OFF_KV + 256, 256), "ks": (OFF_KV + 512, 256), "vs": (OFF_KV + 768, 256),
            "kw": (OFF_KV + 1024, 256), "vw": (OFF_KV + 1280, 256), "za": (OFF_ZA, 1024), "mg": (OFF_MG, 2048)}
    tiles = {k: tile_of(w_in[:, a:a + n]) for k, (a, n) in lens.items()}
    dtg = np.zeros((D_MODEL, P), f)
    dtg[:, 0:SSM_HEADS] = w_in[:, OFF_DT:OFF_DT + SSM_HEADS]
    dtg[:, GATE_ROW:GATE_ROW + 48] = w_in[:, OFF_GATE:OFF_GATE + 48]
    tiles["dtg"] = tile_of(dtg)
    ssm = tile_of(w["w_ssm_out"][0])
    tiles["nsa"], tiles["out"] = tile_of(w["w_nsa_out"][0]), tile_of(w["w_out"][0])
    w1 = {k: w[n][0].reshape(16, 2, 64, CMP_HIDDEN).transpose(1, 2, 0, 3).reshape(P, 4, 1024)
          for k, n in (("w1k", "cmp_w1_k"), ("w1v", "cmp_w1_v"))}
    ada = w["w_ada"][0].reshape(KT, P, 3 * D_MODEL).transpose(1, 0, 2)
    wpack = np.empty((len(UNITS), P, 1024), f)
    for u, (kind, j, part) in enumerate(UNITS):
        if kind in w1:
            wpack[u] = w1[kind][:, part]
        elif kind == "ag":
            wpack[u] = ada[:, part, 2048:3072]
        elif kind == "ssm":
            wpack[u] = ssm[j][:, 8 * part:8 * part + 8].reshape(P, 1024)
        else:
            wpack[u] = tiles[kind][j].reshape(P, 1024)
    dt_bias = np.zeros((P, 1), f)
    dt_bias[0:SSM_HEADS, 0] = w["dt_bias"][0]
    pos = {k: np.concatenate([w[k][0].T, w[k][0].T], 0) for k in ("cmp_pos_k", "cmp_pos_v")}
    w2 = {k: w[k][0].reshape(2, P, 64).transpose(1, 0, 2) for k in ("cmp_w2_k", "cmp_w2_v")}
    parts = {"c": cols(w["c"][0], KT), "conv_w": w["conv_w"][0].reshape(4, 24, P).transpose(2, 1, 0).reshape(P, 96),
             "conv_b": cols(w["conv_b"][0], 24), "dt_bias": dt_bias, "g_pre": cols(w["g_pre"][0], 8),
             "g_post": cols(w["g_post"][0], 8), "b_ada": cols(w["b_ada"][0], 24), "g_ssm": cols(w["g_ssm_norm"][0], 16),
             "d_skip": cols(np.repeat(w["d_skip"][0], HEAD_DIM), 16), "a_log": np.repeat(w["a_log"], P, 0),
             "pos_k": pos["cmp_pos_k"], "pos_v": pos["cmp_pos_v"]}
    w2_both = np.concatenate([np.concatenate([w2["cmp_w2_k"]] * 2, 2).reshape(P, 256), w2["cmp_w2_v"].reshape(P, 128)], 1)
    params = np.concatenate([parts[n] for n in PAR if n != "end"], axis=1)
    xT = w["x"][0].T.reshape(KT, P, SEQ).transpose(1, 0, 2)
    consts, cmp_bias, alibi_q, alibi_k = host_constants()
    return {"xT": xT, "params": params, "consts": consts, "alibi_q": alibi_q, "alibi_k": alibi_k,
            "w_ada1": ada[:, :, 0:2048], "w_compress_2": w2_both, "cmp_bias": cmp_bias, "wpack": wpack}


def kernel(**inputs):
    import concourse.bacc as bacc
    from concourse.bass_utils import run_bass_kernel_spmd

    nc = bacc.Bacc("TRN2", target_bir_lowering=False, num_devices=1)
    arrays, args = {}, []
    for name, a in lay_out(inputs).items():
        a = np.ascontiguousarray(a)
        arrays[f"in_{name}"] = a
        args.append(nc.dram_tensor(f"in_{name}", a.shape, mybir.dt.from_np(a.dtype), kind="ExternalInput").ap())
    out = nc.dram_tensor("out_T_dram", (P, KT, SEQ), mybir.dt.float32, kind="ExternalOutput").ap()
    build(nc, *args, out)
    r = run_bass_kernel_spmd(nc, [arrays], core_ids=[0])
    got = r.results[0]["out_T_dram"]
    return got.transpose(2, 1, 0).reshape(1, SEQ, D_MODEL)
```
